# Optimizing a Trainium2 kernel written in Bass

```python
import jax, jax.numpy as jnp
from jax import lax
import numpy as np

D_MODEL = 1024
BATCH = 1
SEQ = 512
DEPTH = 2

CHUNK = 64
N_MEM = 256
HEAD_DIM = 64
N_HEADS = D_MODEL // HEAD_DIM
DECAY_LORA = 64
AAA_LORA = 64
GATE_LORA = 128
GN_EPS = 64e-5
N_MIX = 6
SB_BLOCK = 128
X_HEADS = 4
X_HEAD_DIM = D_MODEL // X_HEADS
N_GROUPS = 4
EXPERTS_PER_GROUP = 8
TOP_K = 2
D_EXPERT = 256
NORM_EPS = 1e-6
N_RWKV = (DEPTH + 1) // 2
N_SB = DEPTH // 2

kernel_name = "rwkv7_stickbreak_memx_hmoe_trunk"

def _rms_norm(x, g):
    xf = x.astype(jnp.float32)
    y = xf * lax.rsqrt(jnp.mean(xf * xf, axis=-1, keepdims=True) + NORM_EPS)
    return (y * g.astype(jnp.float32)).astype(x.dtype)

def _rwkv7_time_mix(h, mix, wr, wk, wv, w0, w1, w2, a0, a1, a2, g1, g2,
                    k_k, k_a, r_k, lnx_w, lnx_b, wo):
    B, S, C = h.shape
    H, N = N_HEADS, HEAD_DIM
    f32 = jnp.float32
    dt = h.dtype
    h_prev = jnp.pad(h, ((0, 0), (1, 0), (0, 0)))[:, :-1]
    dx = h_prev - h
    xr, xw, xk, xv, xa, xg = [h + dx * mix[i] for i in range(N_MIX)]

    r = (xr @ wr).astype(f32)
    k = (xk @ wk).astype(f32)
    v = (xv @ wv).astype(f32)
    w_log = -jax.nn.softplus(-(w0 + jnp.tanh(xw @ w1) @ w2).astype(f32)) - 0.5
    decay = jnp.exp(-jnp.exp(w_log))
    a = jax.nn.sigmoid((a0 + (xa @ a1) @ a2).astype(f32))
    g = jax.nn.sigmoid(xg @ g1) @ g2

    kk = (k * k_k).reshape(B, S, H, N)
    kk = kk / jnp.maximum(jnp.linalg.norm(kk, axis=-1, keepdims=True), 1e-12)
    k = k * (1.0 + (a - 1.0) * k_a)

    rh = r.reshape(B, S, H, N)
    kh = k.reshape(B, S, H, N)
    vh = v.reshape(B, S, H, N)
    bh = kk * a.reshape(B, S, H, N)
    dh = decay.reshape(B, S, H, N)

    def to_chunks(t):
        return jnp.moveaxis(t, 1, 0).reshape(S // CHUNK, CHUNK, B, H, N)

    def frame_step(state, inp):
        r_t, d_t, k_t, v_t, kk_t, b_t = inp
        sa = jnp.einsum('bhvk,bhk->bhv', state, -kk_t)
        state = (state * d_t[:, :, None, :]
                 + sa[..., None] * b_t[:, :, None, :]
                 + v_t[..., None] * k_t[:, :, None, :])
        y_t = jnp.einsum('bhvk,bhk->bhv', state, r_t)
        return state, y_t

    def chunk_step(state, inp_chunk):
        return lax.scan(frame_step, state, inp_chunk)

    state0 = jnp.zeros((B, H, N, N), f32)
    _, y = lax.scan(chunk_step, state0,
                    (to_chunks(rh), to_chunks(dh), to_chunks(kh), to_chunks(vh),
                     to_chunks(kk), to_chunks(bh)))
    y = jnp.moveaxis(y.reshape(S, B, H, N), 0, 1)

    mu = jnp.mean(y, axis=-1, keepdims=True)
    var = jnp.mean(jnp.square(y - mu), axis=-1, keepdims=True)
    y = ((y - mu) * lax.rsqrt(var + GN_EPS)).reshape(B, S, C) * lnx_w + lnx_b
    bonus = jnp.sum(rh * kh * r_k, axis=-1, keepdims=True) * vh
    y = y + bonus.reshape(B, S, C)
    return (y * g).astype(dt) @ wo

def _stick_breaking_attention(h, wqkv, wo):
    B, S, C = h.shape
    H, N = N_HEADS, HEAD_DIM
    f32 = jnp.float32
    qkv = (h @ wqkv).reshape(B, S, 3, H, N).astype(f32)
    q = qkv[:, :, 0] * (N ** -0.5)
    k = qkv[:, :, 1]
    v = qkv[:, :, 2]
    outs = []
    for blk in range(S // SB_BLOCK):
        q0 = blk * SB_BLOCK
        end = q0 + SB_BLOCK
        z = jnp.einsum('bthd,bshd->bhts', q[:, q0:end], k[:, :end])
        t_idx = q0 + jnp.arange(SB_BLOCK)[:, None]
        s_idx = jnp.arange(end)[None, :]
        before = s_idx < t_idx
        log_fail = jnp.where(before, jax.nn.log_sigmoid(-z), 0.0)
        later = lax.cumsum(log_fail, axis=3, reverse=True) - log_fail
        att = jnp.where(before, jnp.exp(jax.nn.log_sigmoid(z) + later), 0.0)
        outs.append(jnp.einsum('bhts,bshd->bthd', att, v[:, :end]))
    o = jnp.concatenate(outs, axis=1).reshape(B, S, C)
    return o.astype(h.dtype) @ wo

def _memory_cross_attention(h, mem_k, mem_v, wq, wo):
    B, S, C = h.shape
    q = (h @ wq).reshape(B, S, X_HEADS, X_HEAD_DIM)
    scores = jnp.einsum('bthd,bmhd->bhtm', q, mem_k).astype(jnp.float32) * (X_HEAD_DIM ** -0.5)
    p = jax.nn.softmax(scores, axis=-1).astype(h.dtype)
    o = jnp.einsum('bhtm,bmhd->bthd', p, mem_v).reshape(B, S, C)
    return o @ wo

def _hierarchical_moe(h, wg, bg, we, be, w1, w3, w2):
    B, S, C = h.shape
    G, E = N_GROUPS, EXPERTS_PER_GROUP
    f32 = jnp.float32
    t = h.reshape(B * S, C)
    g_logits = (t @ wg).astype(f32) + bg
    g_prob = jax.nn.softmax(g_logits, axis=-1)
    group = jnp.argmax(g_logits, axis=-1)
    p_group = jnp.take_along_axis(g_prob, group[:, None], axis=-1)
    e_logits = ((t @ we).astype(f32) + be).reshape(-1, G, E)
    e_sel = jnp.take_along_axis(e_logits, group[:, None, None], axis=1)[:, 0]
    top_val, top_idx = lax.top_k(e_sel, TOP_K)
    top_w = jax.nn.softmax(top_val, axis=-1) * p_group
    gate_e = jnp.sum(jax.nn.one_hot(top_idx, E, dtype=f32) * top_w[..., None], axis=1)
    gate = jax.nn.one_hot(group, G, dtype=f32)[:, :, None] * gate_e[:, None, :]
    y = jnp.zeros((B * S, C), f32)
    for gi in range(G):
        hid = jax.nn.silu(jnp.einsum('td,edf->tef', t, w1[gi])) * jnp.einsum('td,edf->tef', t, w3[gi])
        hid = hid * gate[:, gi, :, None].astype(hid.dtype)
        y = y + jnp.einsum('tef,efd->td', hid, w2[gi]).astype(f32)
    return y.astype(h.dtype).reshape(B, S, C)

def setup_inputs(seed: int = 0) -> dict:
    key = jax.random.key(seed)
    ks = iter(jax.random.split(key, 48))
    f32 = jnp.float32
    C, H, N = D_MODEL, N_HEADS, HEAD_DIM
    G, E, F = N_GROUPS, EXPERTS_PER_GROUP, D_EXPERT

    def nrm(shape, scale):
        return jax.random.normal(next(ks), shape, f32) * scale

    def gain(shape):
        return 1.0 + nrm(shape, 0.02)

    return {
        "x": nrm((BATCH, SEQ, C), 1.0),
        "mem": nrm((BATCH, N_MEM, C), 1.0),
        "norm_mix": gain((DEPTH, C)),
        "norm_cross": gain((DEPTH, C)),
        "norm_ffn": gain((DEPTH, C)),
        "norm_mem": gain((C,)),
        "norm_final": gain((C,)),
        "rw_mix": jax.random.uniform(next(ks), (N_RWKV, N_MIX, C), f32),
        "rw_wr": nrm((N_RWKV, C, C), C ** -0.5),
        "rw_wk": nrm((N_RWKV, C, C), C ** -0.5),
        "rw_wv": nrm((N_RWKV, C, C), C ** -0.5),
        "rw_w0": jax.random.uniform(next(ks), (N_RWKV, C), f32, -2.5, 1.0),
        "rw_w1": nrm((N_RWKV, C, DECAY_LORA), C ** -0.5),
        "rw_w2": nrm((N_RWKV, DECAY_LORA, C), 0.5 * DECAY_LORA ** -0.5),
        "rw_a0": nrm((N_RWKV, C), 0.5),
        "rw_a1": nrm((N_RWKV, C, AAA_LORA), C ** -0.5),
        "rw_a2": nrm((N_RWKV, AAA_LORA, C), 0.5 * AAA_LORA ** -0.5),
        "rw_g1": nrm((N_RWKV, C, GATE_LORA), C ** -0.5),
        "rw_g2": nrm((N_RWKV, GATE_LORA, C), GATE_LORA ** -0.5),
        "rw_kk": 1.0 + nrm((N_RWKV, C), 0.1),
        "rw_ka": 1.0 + nrm((N_RWKV, C), 0.1),
        "rw_rk": nrm((N_RWKV, H, N), 0.1),
        "rw_lnx_w": gain((N_RWKV, C)),
        "rw_lnx_b": nrm((N_RWKV, C), 0.02),
        "rw_wo": nrm((N_RWKV, C, C), C ** -0.5),
        "sb_wqkv": nrm((N_SB, C, 3 * C), C ** -0.5),
        "sb_wo": nrm((N_SB, C, C), C ** -0.5),
        "xa_wq": nrm((DEPTH, C, C), C ** -0.5),
        "xa_wkv": nrm((C, 2 * C), C ** -0.5),
        "xa_wo": nrm((DEPTH, C, C), C ** -0.5),
        "moe_wg": nrm((DEPTH, C, G), C ** -0.5),
        "moe_bg": nrm((DEPTH, G), 0.01),
        "moe_we": nrm((DEPTH, C, G * E), C ** -0.5),
        "moe_be": nrm((DEPTH, G * E), 0.01),
        "moe_w1": nrm((DEPTH, G, E, C, F), C ** -0.5),
        "moe_w3": nrm((DEPTH, G, E, C, F), C ** -0.5),
        "moe_w2": nrm((DEPTH, G, E, F, C), F ** -0.5),
    }

def reference(x, mem, norm_mix, norm_cross, norm_ffn, norm_mem, norm_final,
              rw_mix, rw_wr, rw_wk, rw_wv, rw_w0, rw_w1, rw_w2, rw_a0, rw_a1, rw_a2,
              rw_g1, rw_g2, rw_kk, rw_ka, rw_rk, rw_lnx_w, rw_lnx_b, rw_wo,
              sb_wqkv, sb_wo, xa_wq, xa_wkv, xa_wo,
              moe_wg, moe_bg, moe_we, moe_be, moe_w1, moe_w3, moe_w2):
    B = mem.shape[0]
    mem_kv = (_rms_norm(mem, norm_mem) @ xa_wkv).reshape(B, N_MEM, 2, X_HEADS, X_HEAD_DIM)
    mem_k = mem_kv[:, :, 0]
    mem_v = mem_kv[:, :, 1]
    h = x
    for i in range(DEPTH):
        hn = _rms_norm(h, norm_mix[i])
        j = i // 2
        if i % 2 == 0:
            h = h + _rwkv7_time_mix(hn, rw_mix[j], rw_wr[j], rw_wk[j], rw_wv[j],
                                    rw_w0[j], rw_w1[j], rw_w2[j], rw_a0[j], rw_a1[j], rw_a2[j],
                                    rw_g1[j], rw_g2[j], rw_kk[j], rw_ka[j], rw_rk[j],
                                    rw_lnx_w[j], rw_lnx_b[j], rw_wo[j])
        else:
            h = h + _stick_breaking_attention(hn, sb_wqkv[j], sb_wo[j])
        h = h + _memory_cross_attention(_rms_norm(h, norm_cross[i]), mem_k, mem_v,
                                        xa_wq[i], xa_wo[i])
        h = h + _hierarchical_moe(_rms_norm(h, norm_ffn[i]), moe_wg[i], moe_bg[i],
                                  moe_we[i], moe_be[i], moe_w1[i], moe_w3[i], moe_w2[i])
    return _rms_norm(h, norm_final)


_drawn_inputs = setup_inputs


def setup_inputs(seed=0):
    import zlib

    import numpy as np

    out = dict(_drawn_inputs(seed))
    spreads = {}
    factors = {'norm_cross': 5.488, 'norm_final': 7.486, 'moe_bg': 3.335, 'moe_be': 4.36}
    for name, (base, spread) in spreads.items():
        noise = np.random.default_rng([zlib.crc32(name.encode()), seed]).standard_normal(out[name].shape)
        drawn = base * np.exp(spread * noise) if base else spread * noise
        out[name] = __import__('jax').numpy.asarray(drawn.astype(out[name].dtype))
    for name, factor in factors.items():
        out[name] = (out[name] * factor).astype(out[name].dtype)
    return out
```

```python
from contextlib import ExitStack

import concourse.bass as bass
from concourse import mybir

F32 = mybir.dt.float32
I32 = mybir.dt.int32
ALU = mybir.AluOpType
ACT = mybir.ActivationFunctionType
AX = mybir.AxisListType

P = 128
C = 1024
T = 512
NT = T // P
KC = C // P
NPAIR = KC
HD = 64
CH = 64
NCH = T // CH
M = 256
XH = 4
XD = C // XH
G, E = 4, 8
NE = G * E
F = 256
BLK = 64
NOVER = (2 * T - NE) // BLK
NBLK = NE + NOVER
EPS = 1e-6
GN_EPS = 64e-5
DECAY_C = float(2.718281828459045 ** -0.5)
XSCALE = float(XD) ** -0.5
BIG = 1e30

RING = 3

PLAN = [
    ("w1", 1, "A"), ("a1", 1, "A"), ("g1", 1, "A"),
    ("wr", 8, "A"), ("wk", 8, "A"), ("wv", 8, "A"),
    ("memk", 8, "A"), ("memv", 4, "A"),
    ("gate", 8, "V"), ("rwo", 8, "V"),
    ("xq0", 8, "A"), ("xv0", 8, "A"), ("xo0", 8, "V"),
    ("sq", 8, "A"), ("sk", 8, "A"), ("sv", 8, "A"), ("so", 8, "V"),
    ("xq1", 8, "A"), ("xv1", 8, "A"), ("xo1", 8, "V"),
]
FIRST, OWNER = {}, []
for _name, _n, _eng in PLAN:
    FIRST[_name] = len(OWNER)
    OWNER += [_eng[_g % len(_eng)] for _g in range(_n)]
NBANK = 4


def groups_done(g):
    return OWNER[:g + 1].count(OWNER[g])


UNITS = ["wr", "wr", "wk", "wk", "wv", "wv",
         "memkv", "memkv", "memkv", "memkv", "rwo", "rwo", "xq0", "xq0", "xo0", "xo0",
         "sqkv", "sqkv", "sqkv", "sqkv", "sqkv", "sqkv", "so", "so",
         "xq1", "xq1", "xo1", "xo1"]

FILLS = [("TA", 0, "A"), ("TB", 1, "A"), ("TK", 0, "A"), ("BN", 1, "A")]
for _s, _e in [("A0", "V"), ("A1", "V"), ("CC", "V"), ("B0", "V"), ("B1", "V"),
               ("Q2", "A"), ("Q2T", "A"), ("WV", "A"),
               ("Q4", "A"), ("Q4T", "A"), ("Z2", "V"),
               ("Q8", "A"), ("Z3", "V"), ("Z4", "V"),
               ("X", "A"), ("XT", "V"), ("R1", "V"),
               ("X2T", "A"), ("R2", "V"), ("R3", "V")]:
    FILLS += [(_s, 0, _e), (_s, 1, _e)]
FILLS += [("G", 0, "V"), ("G", 1, "V"), ("H", 0, "A"), ("H", 1, "A"), ("RP", 0, "V")]
for _c in range(1, NCH - 1):
    FILLS += [(f"S{_c}", 0, "V"), (f"S{_c}", 1, "V")]
FILLS += [("Y", 0, "A"), ("Y", 1, "A")]
FILL_NO = {(s, h): n for n, (s, h, e) in enumerate(FILLS)}
NFILL = len(FILLS)


def bank_of(n):
    h = FILLS[n][1]
    return 4 * h + sum(1 for s in FILLS[:n] if s[1] == h) % 4


def bank_before(n):
    h = FILLS[n][1]
    mine = [m for m in range(n) if FILLS[m][1] == h]
    return mine[-4] if len(mine) >= 4 else None


def evacs(n):
    return sum(1 for s in FILLS[:n + 1] if s[2] == FILLS[n][2])


NEV = {e: sum(1 for s in FILLS if s[2] == e) for e in "AV"}

NEEDS = {
    "Q2": lambda h: [("CC", h)], "Q2T": lambda h: [("CC", h)], "WV": lambda h: [("B1", h)],
    "Q4": lambda h: [("Q2T", h)], "Q4T": lambda h: [("Q2T", h)], "Z2": lambda h: [("Q2", h)],
    "Q8": lambda h: [("Q4T", h)], "Z3": lambda h: [("Z2", h), ("Q4", h)], "Z4": lambda h: [("Q8", h), ("Z3", h)],
    "X": lambda h: [("Z4", h)], "XT": lambda h: [("Z4", h)], "R1": lambda h: [("Z4", h), ("WV", h)],
    "X2T": lambda h: [("X", h), ("XT", h)], "R2": lambda h: [("X2T", h), ("R1", h)],
    "R3": lambda h: [("R2", h)], "G": lambda h: [("R3", 1), ("TB", 1)], "H": lambda h: [("R3", 1), ("TK", 0)],
    "RP": lambda h: [("R3", 1)],
    "S1": lambda h: [("G", 1), ("H", 1)], "Y": lambda h: [(f"S{NCH - 2}", h), ("RP", 0)],
}
for _c in range(2, NCH - 1):
    NEEDS[f"S{_c}"] = lambda h, c=_c: [(f"S{c - 1}", h)]


def trunk(nc, A, out, scratch):
    ctx = ExitStack()
    with ctx:
        def sb(name, shape, dt=F32):
            return ctx.enter_context(nc.sbuf_tensor(name, shape, dt))

        sems = {}

        def S(name):
            if name not in sems:
                sems[name] = ctx.enter_context(nc.semaphore(name))
            return sems[name]

        def gate(eng):
            eng.nop().then_inc(S("gates"), 1)

        PS = ctx.enter_context(nc.psum_tensor("PS", [P, 8, 512], F32))

        def bank(b, *shape):
            v = PS[:, b, :]
            if len(shape) == 2:
                v = v.rearrange("p (a b) -> p a b", a=shape[0])
            if len(shape) == 3:
                v = v.rearrange("p (a b c) -> p a b c", a=shape[0], b=shape[1])
            return v

        h = sb("h", [P, NT, C])
        ring = sb("ring", [P, RING, KC, 512])
        ident = sb("ident", [P, P])
        ones = sb("ones", [P, P])
        gainT = sb("gainT", [P, 7, KC])
        sumsq = sb("sumsq", [P, NT])
        rms = sb("rms", [P, NT])
        rstd = sb("rstd", [P, NT])
        ARENA = 34 * 1024
        arena = sb("arena", [P, ARENA])

        def at(k1024, shape):
            n = 1
            for s in shape:
                n *= s
            o = int(k1024 * 1024)
            assert o + n <= ARENA, (o, n)
            return split(arena[:, o:o + n], shape)

        def split(v, shape):
            if len(shape) == 1:
                return v
            names = "abcd"[:len(shape)]
            return v.rearrange(f"p ({' '.join(names)}) -> p {' '.join(names)}",
                               **{names[j]: shape[j] for j in range(len(shape))})

        K_ = at(0, [KC, T])
        R_ = at(4, [KC, T])
        V_ = at(8, [NT, C])
        xT = at(12, [KC, T])
        dx = at(16, [KC, T])
        xm = [at(20, [KC, T]), at(24, [KC, T])]
        tn0 = at(24, [NT, C])
        KK = at(12, [KC, T])
        SG = at(16, [KC, T])
        AS = at(20, [KC, T])
        l1 = at(28, [KC, 256])
        w2s = at(30, [C])
        a2s = at(31, [C])
        g2s = at(32, [C])
        sg1 = at(33, [T])
        tw = at(33.5, [T])
        mixT = sb("mixT", [P, 6, KC])
        prow = sb("prow", [40, P])
        prm = sb("prm", [P, 5, KC])
        one_ka = sb("one_ka", [P, KC])
        hones = sb("hones", [P, P])
        masks = sb("masks", [P, 5, P])
        U16s, U64s, U64i, L16s, Loff = [masks[:, n, :] for n in range(5)]
        ident2 = sb("ident2", [P, HD])
        PC = sb("PC", [P, NCH])
        BN = sb("BN", [P, NT, 2 * NPAIR])

        hW = h[:, :, :].rearrange("p t c -> p (t c)")
        S_ = hW[:, 0:512]
        Pe = hW[:, 512:1024]
        Pp = hW[:, 1024:1536]
        Pi = hW[:, 1536:2048]
        Pf = hW[:, 2048:2560]
        bb = hW[:, 2560:3072]
        notfirst = hW[:, 3072:3584]
        ta = hW[:, 3584:4096]
        k2 = at(24, [T])
        AR = at(24.5, [2, T])
        BT = at(25.5, [T])
        KT = at(26, [T])
        B2 = at(26.5, [T])
        K2 = at(27, [T])
        RK = at(27.5, [T])
        Bt = at(28, [NT, P])
        Kt = at(28.5, [NT, P])
        Vp = at(29, [NT, P])
        Rpp = at(29.5, [T])
        GT = at(30, [NCH, HD])
        Hs = at(30.5, [NCH, HD])
        dPC = at(31, [NCH, HD])
        ringW = ring[:, :, :, :].rearrange("p r k n -> p (r k n)")

        def mat(slot, hh):
            o = (2 * slot + hh) * 512
            return split(ringW[:, o:o + 512], [NT, P])

        MdT, Md, Nf, RBT, RKT, WT, Q2, Q2T, Z, XT, RHS = [[mat(s, hh) for hh in range(2)] for s in range(11)]
        Q4, Q4T, Xm, X2T, Q8 = MdT, Md, WT, Q2, Q2T

        Yv = at(0, [NPAIR, NT, P])
        YT = at(4, [KC, T])
        lnw = at(12, [C])
        lnb = at(13, [C])
        Ysq = at(16, [NPAIR, NT, P])
        Vb = at(20, [NPAIR, NT, P])
        mem_rows = at(26, [M // P, C])
        mem_tn = at(14, [M // P, C])
        mem_xT = at(24, [KC, M])
        memK = at(28, [KC, M])
        memV = at(30, [M // P, C])
        mu, var = sb("mu", [P, 64]), sb("var", [P, 64])

        def src8(w):
            return w.rearrange("(p k) n -> p k n", k=KC)

        def srcn(w):
            return w.rearrange("(k p) n -> p k n", p=P)

        def unit_source(u):
            name = UNITS[u]
            i = u - UNITS.index(name)
            if name in ("wr", "wk", "wv"):
                w = src8(A["rw_" + name][0])
            elif name == "rwo":
                w = srcn(A["rw_wo"][0])
            elif name == "memkv":
                w = src8(A["xa_wkv"])
            elif name == "sqkv":
                w = src8(A["sb_wqkv"][0])
            elif name == "so":
                w = srcn(A["sb_wo"][0])
            elif name[:2] == "xq":
                w = src8(A["xa_wq"][int(name[2])])
            else:
                w = srcn(A["xa_wo"][int(name[2])])
            return w[:, :, 512 * i:512 * i + 512]

        def unit_last_group(u):
            name = UNITS[u]
            i = u - UNITS.index(name)
            if name == "memkv":
                return FIRST["memk"] + 4 * i + 3 if i < 2 else FIRST["memv"] + 2 * (i - 2) + 1
            if name == "sqkv":
                return FIRST["sq"] + 4 * i + 3
            return FIRST[name] + 4 * i + 3

        def load_units(sp, u0, u1):
            for u in range(u0, u1):
                if u >= RING:
                    sp.wait_ge(S("proj_filled"), unit_last_group(u - RING) + 1)
                sp.dma_start(ring[:, u % RING, :, :], unit_source(u)).then_inc(S(f"unit_in{u % RING}"), 16)

        def unit_arrived(eng, u):
            eng.wait_ge(S(f"unit_in{u % RING}"), 16 * (u // RING + 1))

        def ldnat(a):
            return a.rearrange("(j p) -> j p", p=P)

        def loads_first(sp):
            for t in range(NT):
                sp.dma_start(h[:, t, :], A["x"][0, P * t:P * t + P, :]).then_inc(S(f"x_in{t}"), 16)
            for n, g in enumerate([A["norm_mix"][0], A["norm_cross"][0], A["norm_ffn"][0], A["norm_mix"][1],
                                   A["norm_cross"][1], A["norm_ffn"][1], A["norm_mem"]]):
                sp.dma_start(gainT[:, n, :], g.rearrange("(p k) -> p k", k=KC)).then_inc(S("small_in"), 16)
            sp.dma_start(mixT[:, :, :], A["rw_mix"][0].rearrange("i (p k) -> p i k", k=KC)).then_inc(S("small_in"), 16)
            for n, g in enumerate([A["rw_w0"][0], A["rw_a0"][0], A["rw_kk"][0], A["rw_ka"][0]]):
                sp.dma_start(prow[8 * n:8 * n + 8, :], ldnat(g)).then_inc(S("small_in"), 16)
            sp.dma_start(prow[32:40, :], A["rw_rk"][0].rearrange("(j a) n -> j (a n)", a=2)).then_inc(S("small_in"), 16)
            sp.dma_start(l1[:, :, 0:64], src8(A["rw_w1"][0])).then_inc(S("small_in"), 16)
            sp.dma_start(l1[:, :, 64:128], src8(A["rw_a1"][0])).then_inc(S("small_in"), 16)
            sp.dma_start(l1[:, :, 128:256], src8(A["rw_g1"][0])).then_inc(S("small_in"), 16)
            sp.dma_start(w2s[0:HD, :], A["rw_w2"][0]).then_inc(S("small_in"), 16)
            sp.dma_start(a2s[0:HD, :], A["rw_a2"][0]).then_inc(S("small_in"), 16)
            sp.dma_start(g2s[:, :], A["rw_g2"][0]).then_inc(S("small_in"), 16)
        SMALL = 16 * (7 + 1 + 5 + 6)

        def loads_after_pairs(sp):
            sp.wait_ge(S("pair_over"), NPAIR + 1)
            for t in range(NT):
                sp.dma_start(h[:, t, :], A["x"][0, P * t:P * t + P, :]).then_inc(S("x_again"), 16)
            sp.dma_start(lnw, bcast(A["rw_lnx_w"][0])).then_inc(S("ln_in"), 16)
            sp.dma_start(lnb, bcast(A["rw_lnx_b"][0])).then_inc(S("ln_in"), 16)
            for m in range(M // P):
                sp.dma_start(mem_rows[:, m, :], A["mem"][0, P * m:P * m + P, :]).then_inc(S("mem_in"), 16)

        def bcast(v):
            return bass.AP(tensor=v.tensor, offset=v.offset, ap=[[0, P]] + [list(x) for x in v.ap])

        def constants(pool):
            n = [0]

            def sel(m, op, fill, base, pattern, cm, view=None):
                pool.wait_ge(S("const_step"), n[0])
                v = m if view is None else view
                pool.affine_select(out=v, in_=v, compare_op=op, fill=fill, base=base, pattern=pattern,
                                   channel_multiplier=cm).then_inc(S("const_step"), 1)
                n[0] += 1

            for m, v in ((ident, 0.0), (ident2, 0.0), (ones, 1.0), (hones, 1.0), (U16s, 1.0), (U64s, 1.0),
                         (U64i, 1.0), (L16s, 1.0), (Loff, 1.0)):
                pool.memset(m[:, :], v).then_inc(S("const_step"), 1)
                n[0] += 1
            sel(ident[:, :], ALU.not_equal, 1.0, 0, [[-1, P]], 1)
            sel(ident2[:, :], ALU.not_equal, 1.0, 0, [[-1, HD]], 1)
            sel(ident2[:, :], ALU.not_equal, 1.0, -HD, [[-1, HD]], 1)

            def blocks(m, b):
                v = m[:, :].rearrange("p (a b) -> p a b", b=b)
                sel(v, ALU.is_ge, 0.0, 0, [[-b, P // b], [0, b]], 1)
                sel(v, ALU.is_ge, 0.0, b - 1, [[b, P // b], [0, b]], -1)

            blocks(hones, HD)
            blocks(U16s, 16)
            sel(U16s[:, :], ALU.is_gt, 0.0, 0, [[1, P]], -1)
            blocks(U64s, CH)
            sel(U64s[:, :], ALU.is_gt, 0.0, 0, [[1, P]], -1)
            blocks(U64i, CH)
            sel(U64i[:, :], ALU.is_ge, 0.0, 0, [[1, P]], -1)
            blocks(L16s, 16)
            sel(L16s[:, :], ALU.is_gt, 0.0, 0, [[-1, P]], 1)
            blocks(Loff, CH)
            sel(Loff[:, :], ALU.is_gt, 0.0, 0, [[-1, P]], 1)
            pool.wait_ge(S("const_step"), n[0])
            pool.tensor_tensor(Loff[:, :], Loff[:, :], L16s[:, :], ALU.subtract).then_inc(S("const_ready"), 1)

        NORMS = [("mix0", NT), ("mem", M // P), ("cross0", NT), ("ffn0", NT), ("mix1", NT), ("cross1", NT),
                 ("ffn1", NT), ("final", NT)]
        NIDX = {n: j for j, (n, _) in enumerate(NORMS)}
        TILE0 = {n: sum(c for _, c in NORMS[:j]) for j, (n, _) in enumerate(NORMS)}
        TPOSE0 = {n: KC * j for j, (n, _) in enumerate(NORMS)}
        GAIN = {"mix0": 0, "cross0": 1, "ffn0": 2, "mix1": 3, "cross1": 4, "ffn1": 5, "mem": 6}

        def norm_act(act, name, src, tn, tile_ready):
            nt = dict(NORMS)[name]
            for t in range(nt):
                tile_ready(act, t)
                act.activation(tn[:, t, :], src[:, t, :], ACT.Square, accum_out=sumsq[:, t:t + 1])\
                    .then_inc(S("norm_squares"), 1)
            act.wait_ge(S("norm_mean"), NIDX[name] + 1)
            act.activation(rms[:, 0:nt], rms[:, 0:nt], ACT.Sqrt).then_inc(S("norm_root"), 1)

        def norm_vec(vec, name, src, tn):
            nt = dict(NORMS)[name]
            vec.wait_ge(S("norm_squares"), TILE0[name] + nt)
            vec.tensor_scalar(rms[:, 0:nt], sumsq[:, 0:nt], 1.0 / C, EPS, ALU.mult, ALU.add)\
                .then_inc(S("norm_mean"), 1)
            vec.wait_ge(S("norm_root"), NIDX[name] + 1)
            vec.reciprocal(rstd[:, 0:nt], rms[:, 0:nt]).then_inc(S("norm_recip"), 1)
            vec.wait_ge(S("norm_recip"), NIDX[name] + 1)
            for t in range(nt):
                vec.tensor_scalar(tn[:, t, :], src[:, t, :], rstd[:, t:t + 1], None, ALU.mult)\
                    .then_inc(S("norm_rows"), 1)

        def norm_pe(pe, name, tn):
            nt = dict(NORMS)[name]
            for k in range(KC):
                n = TPOSE0[name] + k
                if n >= 2:
                    pe.wait_ge(S("xT_act" if n % 2 == 0 else "xT_vec"), n // 2)
                for t in range(nt):
                    if k == 0:
                        pe.wait_ge(S("norm_rows"), TILE0[name] + t + 1)
                    ins = pe.transpose(PS[:, 6 + n % 2, P * t:P * t + P], tn[:, t, k::KC], ident[:, :])
                ins.then_inc(S("norm_turned"), 1)

        def xT_evac(eng, name, dst, which):
            nt = dict(NORMS)[name]
            for k in range(which, KC, 2):
                n = TPOSE0[name] + k
                eng.wait_ge(S("norm_turned"), n + 1)
                g = gainT[:, GAIN[name], k:k + 1]
                if which == 0:
                    eng.activation(dst[:, k, 0:nt * P], PS[:, 6 + n % 2, 0:nt * P], ACT.Copy, scale=g)\
                        .then_inc(S("xT_act"), 1)
                else:
                    eng.tensor_scalar(dst[:, k, 0:nt * P], PS[:, 6 + n % 2, 0:nt * P], g, None, ALU.mult)\
                        .then_inc(S("xT_vec"), 1)

        def xT_there(eng, name, k):
            n = TPOSE0[name] + k
            eng.wait_ge(S("xT_act" if n % 2 == 0 else "xT_vec"), n // 2 + 1)

        def bank_free(pe, g):
            if g >= NBANK:
                pe.wait_ge(S("proj_out_" + OWNER[g - NBANK]), groups_done(g - NBANK))

        def group_out(eng, g):
            eng.wait_ge(S("proj_filled"), g + 1)
            return PS[:, g % NBANK, :]

        def group_evacuated(eng, g):
            eng.wait_ge(S("proj_out_" + OWNER[g]), groups_done(g))

        def project_T(pe, g0, u0, xt, n, ready, chunks=8):
            for j in range(chunks):
                g = g0 + j
                u = u0 + j // 4
                if j % 4 == 0:
                    unit_arrived(pe, u)
                bank_free(pe, g)
                for k in range(KC):
                    if j == 0:
                        ready(pe, k)
                    ins = pe.matmul(PS[:, g % NBANK, 0:n], ring[:, u % RING, k, P * (j % 4):P * (j % 4) + P],
                                    xt[:, k, 0:n], start=(k == 0), stop=(k == KC - 1))
                ins.then_inc(S("proj_filled"), 1)

        def project_tok(pe, g0, u0, xt, ready, tiles=NT):
            for half in range(2):
                unit_arrived(pe, u0 + half)
                for t in range(tiles):
                    g = g0 + tiles * half + t
                    bank_free(pe, g)
                    for k in range(KC):
                        if half == 0 and t == 0:
                            ready(pe, k)
                        ins = pe.matmul(PS[:, g % NBANK, :], xt[:, k, P * t:P * t + P],
                                        ring[:, (u0 + half) % RING, k, :], start=(k == 0), stop=(k == KC - 1))
                    ins.then_inc(S("proj_filled"), 1)

        def evac_T(act, g0, dst, n=T, chunks=8):
            for j in range(chunks):
                act.activation(dst[:, j, 0:n], group_out(act, g0 + j)[:, 0:n], ACT.Copy).then_inc(S("proj_out_A"), 1)

        def evac_tok(act, g0, dst, tiles=NT):
            for half in range(2):
                for t in range(tiles):
                    act.activation(dst[:, t, 512 * half:512 * half + 512], group_out(act, g0 + tiles * half + t),
                                   ACT.Copy).then_inc(S("proj_out_A"), 1)

        def add_to_h(vec, g0, ready=None):
            for half in range(2):
                for t in range(NT):
                    if ready and half == 0:
                        ready(vec, t)
                    v = h[:, t, 512 * half:512 * half + 512]
                    vec.tensor_tensor(v, v, group_out(vec, g0 + NT * half + t), ALU.add)\
                        .then_inc(S("proj_out_V"), 1)

        MIXES = [("w1", 1), ("a1", 4), ("g1", 5), ("wr", 0), ("wk", 2), ("wv", 3)]
        LORA_AT = {"w1": (0, 64), "a1": (64, 64), "g1": (128, 128)}

        def rwkv_mix_vec(vec):
            vec.wait_ge(S("small_in"), SMALL)
            for k in range(KC):
                xT_there(vec, "mix0", k)
            vec.tensor_tensor(dx[:, :, 1:T], xT[:, :, 0:T - 1], xT[:, :, 1:T], ALU.subtract).then_inc(S("dx_ready"), 1)
            vec.tensor_scalar(dx[:, :, 0:1], xT[:, :, 0:1], -1.0, None, ALU.mult).then_inc(S("dx_ready"), 1)
            vec.wait_ge(S("dx_ready"), 2)
            for n, (name, i) in enumerate(MIXES):
                if n >= 2:
                    before = MIXES[n - 2][0]
                    vec.wait_ge(S("proj_filled"), FIRST[before] + dict((a, b) for a, b, _ in PLAN)[before])
                for k in range(KC):
                    vec.scalar_tensor_tensor(out=xm[n % 2][:, k, :], in0=dx[:, k, :], scalar=mixT[:, i, k:k + 1],
                                             in1=xT[:, k, :], op0=ALU.mult, op1=ALU.add).then_inc(S("mixed"), 1)

        def rwkv_proj_pe(pe):
            pe.wait_ge(S("small_in"), SMALL)
            pe.transpose(PS[:, 5, 0:40], prow[:, :], ident[0:40, 0:40]).then_inc(S("prm_turned"), 1)
            for n, (name, _) in enumerate(MIXES):
                def ready(e, k, n=n):
                    e.wait_ge(S("mixed"), KC * n + k + 1)
                x_ = xm[n % 2]
                g = FIRST[name]
                if name in LORA_AT:
                    o, m = LORA_AT[name]
                    bank_free(pe, g)
                    for k in range(KC):
                        ready(pe, k)
                        ins = pe.matmul(PS[0:m, g % NBANK, :], l1[:, k, o:o + m], x_[:, k, :],
                                        start=(k == 0), stop=(k == KC - 1))
                    ins.then_inc(S("proj_filled"), 1)
                elif name == "wv":
                    project_tok(pe, g, UNITS.index("wv"), x_, ready)
                else:
                    project_T(pe, g, UNITS.index(name), x_, T, ready)

        def rwkv_proj_act(act):
            act.activation(tw[0:HD, :], group_out(act, FIRST["w1"])[0:HD, :], ACT.Tanh).then_inc(S("proj_out_A"), 1)
            act.activation(ta[0:HD, :], group_out(act, FIRST["a1"])[0:HD, :], ACT.Copy).then_inc(S("proj_out_A"), 1)
            act.activation(sg1[:, :], group_out(act, FIRST["g1"]), ACT.Sigmoid).then_inc(S("proj_out_A"), 1)
            evac_T(act, FIRST["wr"], R_)
            evac_T(act, FIRST["wk"], K_)
            evac_tok(act, FIRST["wv"], V_)

        def prm_vec(vec):
            vec.wait_ge(S("prm_turned"), 1)
            vec.tensor_copy(prm[:, :, :], PS[:, 5, 0:40].rearrange("p (n j) -> p n j", n=5)).then_inc(S("prm_ready"), 1)
            vec.wait_ge(S("prm_ready"), 1)
            vec.tensor_scalar(one_ka[:, :], prm[:, 3, :], -1.0, 1.0, ALU.mult, ALU.add).then_inc(S("prm_ready"), 1)

        def rwkv_pre_pe(pe):
            group_evacuated(pe, FIRST["a1"])
            for j in range(KC):
                if j >= 2:
                    pe.wait_ge(S("pre_sig"), 2 * j - 2)
                else:
                    xT_there(pe, "mix0", 6 + j)
                    pe.wait_ge(S("prm_ready"), 1)
                pe.matmul(PS[:, 4 + 2 * (j % 2), :], w2s[0:HD, P * j:P * j + P], tw[0:HD, :], start=True, stop=True)
                pe.matmul(PS[:, 5 + 2 * (j % 2), :], a2s[0:HD, P * j:P * j + P], ta[0:HD, :], start=True, stop=True)\
                    .then_inc(S("pre_filled"), 1)
            pe.wait_ge(S("const_ready"), 1)
            for j in range(KC):
                pe.wait_ge(S("pre_sq"), j + 1)
                group_evacuated(pe, FIRST["wv"] + 7)
                if j >= 4:
                    pe.wait_ge(S("pre_norm"), j - 3)
                pe.matmul(PS[:, j % 4, :], hones[:, :], KK[:, j, :], start=True, stop=True).then_inc(S("pre_summed"), 1)

        def rwkv_pre_act(act):
            act.wait_ge(S("prm_ready"), 2)
            for j in range(KC):
                act.wait_ge(S("pre_filled"), j + 1)
                act.activation(SG[:, j, :], PS[:, 4 + 2 * (j % 2), :], ACT.Sigmoid, bias=prm[:, 0, j:j + 1])\
                    .then_inc(S("pre_sig"), 1)
                act.activation(AS[:, j, :], PS[:, 5 + 2 * (j % 2), :], ACT.Sigmoid, bias=prm[:, 1, j:j + 1])\
                    .then_inc(S("pre_sig"), 1)
            for j in range(KC):
                group_evacuated(act, FIRST["wk"] + j)
                act.activation(KK[:, j, :], K_[:, j, :], ACT.Square, scale=prm[:, 2, j:j + 1]).then_inc(S("pre_sq"), 1)
            act.wait_ge(S("pre_norm"), KC)
            act.activation(KK[:, :, :], KK[:, :, :], ACT.Sqrt).then_inc(S("pre_root"), 1)

        def rwkv_pre_vec(vec):
            for j in range(KC):
                vec.wait_ge(S("pre_summed"), j + 1)
                vec.tensor_scalar(KK[:, j, :], PS[:, j % 4, :], 1e-24, None, ALU.max).then_inc(S("pre_norm"), 1)
            vec.wait_ge(S("pre_root"), 1)
            vec.reciprocal(KK[:, :, :], KK[:, :, :]).then_inc(S("pre_recip"), 1)
            vec.wait_ge(S("pre_recip"), 1)
            for j in range(KC):
                vec.scalar_tensor_tensor(out=KK[:, j, :], in0=K_[:, j, :], scalar=prm[:, 2, j:j + 1],
                                         in1=KK[:, j, :], op0=ALU.mult, op1=ALU.mult).then_inc(S("kk_ready"), 1)
            vec.memset(notfirst, 1.0).then_inc(S("notfirst_ready"), 1)
            vec.wait_ge(S("notfirst_ready"), 1)
            vec.memset(split(notfirst, [NCH, CH])[:, :, 0:1], 0.0).then_inc(S("notfirst_ready"), 1)
            vec.wait_ge(S("notfirst_ready"), 2)

        def pair_pool(pool):
            pool.wait_ge(S("kk_ready"), KC)
            with pool.Fori(0, NPAIR) as i:
                pool.wait_ge(S("pair_begun"), i + 1)
                pool.tensor_tensor(bb, KK[:, i, :], AS[:, i, :], ALU.mult).then_inc(S("b_ready"), 1)
                pool.wait_ge(S("k2_step"), i + 1)
                pool.tensor_tensor(k2, k2, K_[:, i, :], ALU.mult).then_inc(S("k2_ready"), 1)
                pool.tensor_copy(Vp, vpair(i)).then_inc(S("vp_ready"), 1)
                pool.wait_ge(S("pe_ready"), 2 * i + 2)
                pool.wait_ge(S("k2_ready"), i + 1)
                pool.tensor_tensor(B2, bb, Pe, ALU.mult).then_inc(S("b2_ready"), 1)
                pool.tensor_tensor(K2, k2, Pe, ALU.mult).then_inc(S("b2_ready"), 1)

        def vpair(i):
            return V_.rearrange("p t (i n) -> p t i n", i=NPAIR)[:, :, i, :]

        def pair_act(act):
            act.wait_ge(S("kk_ready"), KC)
            with act.Fori(0, NPAIR) as i:
                act.wait_ge(S("pair_begun"), i + 1)
                act.activation(k2, AS[:, i, :], ACT.Identity, bias=one_ka[:, bass.ds(i, 1)],
                               scale=prm[:, 3, bass.ds(i, 1)]).then_inc(S("k2_step"), 1)
                act.wait_ge(S("sum_ready"), 3 * i + 1)
                act.activation(Pf, S_, ACT.Exp, scale=-DECAY_C).then_inc(S("pf_ready"), 1)
                act.activation(Pi, S_, ACT.Exp, scale=DECAY_C).then_inc(S("pi_ready"), 1)
                act.activation(PC[:, :], split(S_, [NCH, CH])[:, :, CH - 1], ACT.Exp, scale=-DECAY_C)\
                    .then_inc(S("pc_ready"), 1)
                act.wait_ge(S("sum_ready"), 3 * i + 2)
                act.activation(Pp, Pp, ACT.Exp, scale=-DECAY_C).then_inc(S("pe_ready"), 1)
                act.wait_ge(S("sum_ready"), 3 * i + 3)
                act.activation(Pe, Pe, ACT.Exp, scale=DECAY_C).then_inc(S("pe_ready"), 1)

                def evac(step, hh, dst, src):
                    n = FILL_NO[step, hh]
                    act.wait_ge(S("filled"), i * NFILL + n + 1)
                    act.activation(dst, src, ACT.Copy).then_inc(S("evac_A"), 1)

                for n, (step, hh, e) in enumerate(FILLS):
                    if e != "A":
                        continue
                    b = bank_of(n)
                    if step == "TA":
                        evac(step, hh, RHS4[:, :, :, 0:HD], bank(b, NT, 2, HD).rearrange("p t a d -> p a t d"))
                    elif step == "BN":
                        evac(step, hh, BN.rearrange("p t (i a) -> p t i a", a=2)[:, :, i, :],
                             PS[:, b, 0:8].rearrange("p (t a) -> p t a", a=2))
                    elif step == "WV":
                        evac(step, hh, RHS[hh][:, :, HD:P],
                             bank(b, NT, 2, HD)[:, :, hh, :])
                    elif step == "Y":
                        evac(step, hh, K_.rearrange("p i (t a n) -> p i t a n", t=NT, a=2)[:, i, :, hh, :],
                             bank(b, NT, P)[:, :, 0:HD])
                    else:
                        dst = {"TB": Bt, "TK": Kt, "H": parity(Hs, hh)}.get(step)
                        if dst is None:
                            dst = {"Q2": Q2, "Q2T": Q2T, "Q4": Q4, "Q4T": Q4T, "Q8": Q8, "X": Xm, "X2T": X2T}[step][hh]
                        src = bank(b, NT, P)[:, :, 0:HD] if step == "H" else bank(b, NT, P)
                        evac(step, hh, dst, src)

        def parity(m, q):
            return m.rearrange("p (t q) d -> p t q d", q=2)[:, :, q, :]

        RHS4 = ringW[:, 20 * 512:22 * 512].rearrange("p (a t n) -> p a t n", a=2, t=NT)

        def pair_vec(vec):
            mask = {"A": (U16s, U64i), "B": (U64s, U64i), "C": (L16s, Loff)}

            def over(m, n):
                return m[:, :].unsqueeze(1).to_broadcast([P, n, P])

            with vec.Fori(0, NPAIR) as i:
                with_credit(vec, i)
                vec.tensor_tensor_scan(S_, notfirst, SG[:, i, :], 0.0, ALU.mult, ALU.add).then_inc(S("sum_ready"), 1)
                vec.wait_ge(S("sum_ready"), 3 * i + 1)
                vec.tensor_tensor(Pp, S_, SG[:, i, :], ALU.subtract).then_inc(S("sum_ready"), 1)
                s3 = split(S_, [NCH, CH])
                vec.tensor_tensor(split(Pe, [NCH, CH]), s3, s3[:, :, CH - 1:CH].to_broadcast([P, NCH, CH]),
                                  ALU.subtract).then_inc(S("sum_ready"), 1)
                vec.wait_ge(S("pf_ready"), i + 1)
                vec.tensor_tensor(AR[:, 1, :], R_[:, i, :], Pf, ALU.mult).then_inc(S("ar_ready"), 1)
                vec.wait_ge(S("k2_ready"), i + 1)
                vec.wait_ge(S("pi_ready"), i + 1)
                vec.tensor_tensor(KT, k2, Pi, ALU.mult).then_inc(S("ar_ready"), 1)
                vec.tensor_tensor(BT, bb, Pi, ALU.mult).then_inc(S("ar_ready"), 1)
                vec.wait_ge(S("pe_ready"), 2 * i + 1)
                vec.scalar_tensor_tensor(out=AR[:, 0, :], in0=KK[:, i, :], scalar=-1.0, in1=Pp,
                                         op0=ALU.mult, op1=ALU.mult).then_inc(S("ar_ready"), 1)
                vec.scalar_tensor_tensor(out=RK, in0=R_[:, i, :], scalar=prm[:, 4, bass.ds(i, 1)], in1=k2,
                                         op0=ALU.mult, op1=ALU.mult).then_inc(S("ar_ready"), 1)
                vec.wait_ge(S("pc_ready"), i + 1)
                vec.tensor_tensor(dPC, ident2[:, :].unsqueeze(1).to_broadcast([P, NCH, HD]),
                                  PC[:, :].unsqueeze(2).to_broadcast([P, NCH, HD]), ALU.mult).then_inc(S("dpc_ready"), 1)

                own = i * NEV["V"]
                for n, (step, hh, e) in enumerate(FILLS):
                    if e != "V":
                        continue
                    b = bank_of(n)
                    vec.wait_ge(S("filled"), i * NFILL + n + 1)

                    def add(dst, src, old):
                        vec.tensor_tensor(dst, src, old, ALU.add).then_inc(S("evac_V"), 1)

                    def masked(dst, src, m, nt):
                        return vec.tensor_tensor(dst, src, over(m, nt), ALU.mult)

                    if step in ("A0", "A1", "B0", "B1"):
                        q = 2 * int(step[1])
                        left, right = (MdT, RBT) if step[0] == "A" else (WT, RKT)
                        ps = bank(b, 2, 2, P)
                        masked(left[hh][:, q:q + 2, :], ps[:, :, 0, :], mask[step[0]][0], 2)
                        masked(right[hh][:, q:q + 2, :], ps[:, :, 1, :], mask[step[0]][1], 2).then_inc(S("evac_V"), 1)
                    elif step == "CC":
                        masked(Md[hh], bank(b, NT, P), L16s, NT)
                        masked(Nf[hh], bank(b, NT, P), Loff, NT).then_inc(S("evac_V"), 1)
                        vec.wait_ge(S("evac_V"), own + evacs(n))
                        vec.tensor_tensor(Z[hh], MdT[hh], over(ident, NT), ALU.add).then_inc(S("z_begun"), 1)
                    elif step in ("Z2", "Z3", "Z4"):
                        if step == "Z2":
                            vec.wait_ge(S("z_begun"), 2 * i + hh + 1)
                        add(Z[hh], bank(b, NT, P), Z[hh])
                    elif step == "XT":
                        vec.tensor_copy(XT[hh], bank(b, NT, P)).then_inc(S("evac_V"), 1)
                    elif step == "R1":
                        vec.tensor_copy(RHS[hh], bank(b, NT, P)).then_inc(S("evac_V"), 1)
                    elif step in ("R2", "R3"):
                        add(RHS[hh], bank(b, NT, P), RHS[hh])
                    elif step == "RP":
                        add(Rpp, PS[:, b, :], AR[:, 1, :])
                    elif step == "G":
                        add(parity(GT, hh), bank(b, NT, P)[:, :, 0:HD], parity(dPC, hh))
                    else:
                        c = int(step[1:])
                        vec.wait_ge(S("evac_A"), i * NEV["A"] + evacs(FILL_NO["H", 1]))
                        r = slice(HD * hh, HD * hh + HD)
                        add(Hs[r, c, :], PS[r, b, 0:HD], Hs[r, c, :])

        def with_credit(vec, i):
            vec.wait_ge(S("pair_over"), i + 1)
            vec.nop().then_inc(S("pair_begun"), 1)

        def pair_pe(pe):
            pe.wait_ge(S("kk_ready"), KC)
            pe.nop().then_inc(S("pair_over"), 1)
            with pe.Fori(0, NPAIR) as i:
                def fill(step, hh):
                    n = FILL_NO[step, hh]
                    m = bank_before(n)
                    need = [FILL_NO[d] for d in NEEDS.get(step, lambda hh: [])(hh)] + ([m] if m is not None else [])
                    for e in "AV":
                        last = [evacs(m) for m in need if FILLS[m][2] == e]
                        if last:
                            pe.wait_ge(S("evac_" + e), i * NEV[e] + max(last))
                    return bank_of(n)

                def mm4(b, hh, lhs, rhs):
                    for t in range(NT):
                        ins = pe.matmul(PS[:, b, P * t:P * t + P], lhs[hh][:, t, :], rhs[hh][:, t, :],
                                        start=True, stop=True)
                    ins.then_inc(S("filled"), 1)

                def rows(v, hh, t):
                    return v[HD * hh:HD * hh + HD, P * t:P * t + P]

                for n, (step, hh, e) in enumerate(FILLS):
                    b = fill(step, hh)
                    if step in ("TA", "TB", "TK"):
                        src = {"TA": AR[:, 0, :], "TB": B2, "TK": K2}[step]
                        if step == "TA":
                            pe.wait_ge(S("ar_ready"), 5 * i + 5)
                        if step == "TB":
                            pe.wait_ge(S("b2_ready"), 2 * i + 2)
                        for t in range(NT):
                            ins = pe.transpose(PS[:, b, P * t:P * t + P], src[:, P * t:P * t + P], ident[:, :])
                        ins.then_inc(S("filled"), 1)
                    elif step == "BN":
                        for t in range(NT):
                            ins = pe.matmul(PS[:, b, 2 * t:2 * t + 2], RK[:, P * t:P * t + P], hones[:, 0::HD],
                                            start=True, stop=True)
                        ins.then_inc(S("filled"), 1)
                    elif step in ("A0", "A1", "B0", "B1"):
                        lhs = BT if step[0] == "A" else KT
                        for q in range(2):
                            t = 2 * int(step[1]) + q
                            ins = pe.matmul(bank(b, 2, 2, P)[:, q, :, :], rows(lhs, hh, t),
                                            AR[HD * hh:HD * hh + HD, :, P * t:P * t + P], start=True, stop=True)
                        ins.then_inc(S("filled"), 1)
                    elif step == "CC":
                        for t in range(NT):
                            ins = pe.matmul(PS[:, b, P * t:P * t + P], rows(AR[:, 0, :], hh, t), rows(BT, hh, t),
                                            start=True, stop=True)
                        ins.then_inc(S("filled"), 1)
                    elif step == "Q2":
                        mm4(b, hh, MdT, Md)
                    elif step == "Q2T":
                        mm4(b, hh, Md, MdT)
                    elif step == "WV":
                        pe.wait_ge(S("vp_ready"), i + 1)
                        for t in range(NT):
                            ins = pe.matmul(PS[:, b, P * t:P * t + P], WT[hh][:, t, :], Vp[:, t, :],
                                            start=True, stop=True)
                        ins.then_inc(S("filled"), 1)
                    elif step == "Q4":
                        pe.wait_ge(S("z_begun"), 2 * i + hh + 1)
                        mm4(b, hh, Q2T, Q2)
                    elif step == "Q4T":
                        mm4(b, hh, Q2, Q2T)
                    elif step == "Z2":
                        mm4(b, hh, Q2, Z)
                    elif step == "Q8":
                        mm4(b, hh, Q4T, Q4)
                    elif step == "Z3":
                        mm4(b, hh, Q4, Z)
                    elif step == "Z4":
                        mm4(b, hh, Q8, Z)
                    elif step == "X":
                        mm4(b, hh, Z, Nf)
                    elif step == "XT":
                        mm4(b, hh, Nf, Z)
                    elif step == "R1":
                        mm4(b, hh, Z, RHS)
                    elif step == "X2T":
                        mm4(b, hh, Xm, XT)
                    elif step == "R2":
                        mm4(b, hh, X2T, RHS)
                    elif step == "R3":
                        mm4(b, hh, XT, RHS)
                    elif step == "RP":
                        for a in range(2):
                            for t in range(NT):
                                ins = pe.matmul(PS[HD * a:HD * a + HD, b, P * t:P * t + P], RHS[a][:, t, 0:HD],
                                                RBT[a][:, t, :], start=True, stop=True)
                        ins.then_inc(S("filled"), 1)
                    elif step in ("G", "H"):
                        if step == "G":
                            pe.wait_ge(S("dpc_ready"), i + 1)
                        gate(pe)
                        r = slice(CH * hh, CH * hh + CH)
                        for t in range(NT):
                            for a in range(2):
                                o = PS[HD * a:HD * a + HD, b, P * t:P * t + HD]
                                cols = slice(HD * a, HD * a + HD)
                                if step == "G":
                                    ins = pe.matmul(o, RHS[a][r, t, 0:HD], Bt[r, t, cols], start=True, stop=True)
                                else:
                                    pe.matmul(o, Bt[r, t, cols], RHS[a][r, t, HD:P], start=True, stop=False)
                                    ins = pe.matmul(o, Kt[r, t, cols], Vp[r, t, cols], start=False, stop=True)
                        ins.then_inc(S("filled"), 1)
                    elif step[0] == "S":
                        c = int(step[1:])
                        gate(pe)
                        r = slice(HD * hh, HD * hh + HD)
                        pe.matmul(PS[r, b, 0:HD], GT[r, c, :], Hs[r, c - 1, :], start=True, stop=True)\
                            .then_inc(S("filled"), 1)
                    elif step == "Y":
                        cols = slice(HD * hh, HD * hh + HD)
                        for t in range(NT):
                            o = slice(P * t, P * t + HD)
                            pe.matmul(PS[:, b, o], RBT[hh][:, t, :], RHS[hh][:, t, HD:P], start=True, stop=False)
                            for c in (2 * t, 2 * t + 1):
                                if c == 0:
                                    continue
                                q = CH * (c % 2)
                                pe.matmul(PS[q:q + CH, b, o], Rpp[cols, P * t + q:P * t + q + CH],
                                          Hs[cols, c - 1, :], start=False, stop=False, skip_group_check=True)
                            ins = pe.matmul(PS[:, b, o], RKT[hh][:, t, :], Vp[:, t, cols], start=False, stop=True)
                        ins.then_inc(S("filled"), 1)
                pe.wait_ge(S("evac_A"), i * NEV["A"] + NEV["A"])
                pe.nop().then_inc(S("pair_over"), 1)

        GPRE = FIRST["gate"]

        def post_pool(pool):
            pool.wait_ge(S("evac_A"), NPAIR * NEV["A"])
            for i in range(NPAIR):
                v = vpair(i).rearrange("p t (a v) -> p t a v", a=2)
                pool.tensor_tensor(Vb[:, i, :, :].rearrange("p t (a v) -> p t a v", a=2), v,
                                   BN[:, :, 2 * i:2 * i + 2].unsqueeze(3).to_broadcast([P, NT, 2, HD]), ALU.mult)\
                    .then_inc(S("bonus_ready"), 1)

        def post_vec(vec):
            y64 = Yv.rearrange("p i t (a v) -> p (i t a) v", a=2)
            s64 = Ysq.rearrange("p i t (a v) -> p (i t a) v", a=2)
            st = S("post_step")

            def over_v(m):
                return m[:, :].unsqueeze(2).to_broadcast([P, 64, HD])

            def over_t(m):
                return m.rearrange("p (i n) -> p i n", i=NPAIR).unsqueeze(2).to_broadcast([P, NPAIR, NT, P])

            vec.wait_ge(S("evac_A"), NPAIR * NEV["A"])
            vec.tensor_reduce(mu[:, :], y64, AX.X, ALU.add).then_inc(st, 1)
            vec.wait_ge(st, 1)
            vec.tensor_scalar(mu[:, :], mu[:, :], 1.0 / HD, None, ALU.mult).then_inc(st, 1)
            vec.wait_ge(st, 2)
            vec.tensor_tensor(y64, y64, over_v(mu), ALU.subtract).then_inc(st, 1)
            vec.wait_ge(S("y_squared"), 1)
            vec.tensor_reduce(var[:, :], s64, AX.X, ALU.add).then_inc(st, 1)
            vec.wait_ge(st, 4)
            vec.tensor_scalar(var[:, :], var[:, :], 1.0 / HD, GN_EPS, ALU.mult, ALU.add).then_inc(st, 1)
            vec.wait_ge(S("y_root"), 1)
            vec.reciprocal(var[:, :], var[:, :]).then_inc(st, 1)
            vec.wait_ge(st, 6)
            vec.tensor_tensor(y64, y64, over_v(var), ALU.mult).then_inc(st, 1)
            vec.wait_ge(st, 7)
            vec.wait_ge(S("ln_in"), 32)
            vec.tensor_tensor(Yv, Yv, over_t(lnw), ALU.mult).then_inc(st, 1)
            vec.wait_ge(st, 8)
            vec.tensor_tensor(Yv, Yv, over_t(lnb), ALU.add).then_inc(st, 1)
            vec.wait_ge(st, 9)
            vec.wait_ge(S("bonus_ready"), NPAIR)
            vec.tensor_tensor(Yv, Yv, Vb, ALU.add).then_inc(st, 1)
            vec.wait_ge(st, 10)
            for half in range(2):
                for t in range(NT):
                    v = Yv[:, 4 * half:4 * half + 4, t, :]
                    g = GPRE + NT * half + t
                    vec.tensor_tensor(v, v, group_out(vec, g).rearrange("p (i n) -> p i n", i=4), ALU.mult)\
                        .then_inc(S("proj_out_V"), 1)

        def post_act(act):
            act.wait_ge(S("post_step"), 3)
            act.activation(Ysq, Yv, ACT.Square).then_inc(S("y_squared"), 1)
            act.wait_ge(S("post_step"), 5)
            act.activation(var[:, :], var[:, :], ACT.Sqrt).then_inc(S("y_root"), 1)
            for i in range(KC):
                act.wait_ge(S("y_turned"), i + 1)
                act.activation(YT[:, i, :], PS[:, 4 + i % 4, :], ACT.Copy).then_inc(S("yT_ready"), 1)

        def post_pe(pe):
            for half in range(2):
                for t in range(NT):
                    g = GPRE + NT * half + t
                    bank_free(pe, g)
                    pe.matmul(PS[:, g % NBANK, :], sg1[:, P * t:P * t + P], g2s[:, 512 * half:512 * half + 512],
                              start=True, stop=True).then_inc(S("proj_filled"), 1)
            for i in range(KC):
                group_evacuated(pe, GPRE + NT * (i // 4) + NT - 1)
                if i >= 4:
                    pe.wait_ge(S("yT_ready"), i - 3)
                for t in range(NT):
                    ins = pe.transpose(PS[:, 4 + i % 4, P * t:P * t + P], Yv[:, i, t, :], ident[:, :])
                ins.then_inc(S("y_turned"), 1)

            def ready(e, k):
                e.wait_ge(S("yT_ready"), k + 1)
            project_tok(pe, FIRST["rwo"], UNITS.index("rwo"), YT, ready)

        def x_back(vec, t):
            vec.wait_ge(S("x_again"), 16 * NT)

        def mem_pe(pe):
            norm_pe(pe, "mem", mem_tn)

            def ready(e, k):
                xT_there(e, "mem", k)
            u = UNITS.index("memkv")
            project_T(pe, FIRST["memk"], u, mem_xT, M, ready)
            project_tok(pe, FIRST["memv"], u + 2, mem_xT, lambda e, k: None, tiles=M // P)

        def mem_act(act):
            act.wait_ge(S("pair_over"), NPAIR + 1)
            norm_act(act, "mem", mem_rows, mem_tn, lambda e, t: e.wait_ge(S("mem_in"), 16 * (M // P)))
            xT_evac(act, "mem", mem_xT, 0)
            evac_T(act, FIRST["memk"], memK, n=M)
            evac_tok(act, FIRST["memv"], memV, tiles=M // P)

        def mem_vec(vec):
            norm_vec(vec, "mem", mem_rows, mem_tn)
            xT_evac(vec, "mem", mem_xT, 1)

        tnX = at(12, [NT, C])
        xTX = at(16, [KC, T])
        qT = at(20, [KC, T])
        oT = at(24, [KC, T])
        prob = [at(12 + x, [NT, M]) for x in range(2)]
        probT = [at(14 + x, [M // P, T]) for x in range(2)]
        xmax, xsum = sb("xmax", [P, 2, NT]), sb("xsum", [P, 2, NT])

        def h_tile_ready(name):
            return lambda e, t: group_evacuated(e, FIRST[name] + NT + t)

        def cross_pe(pe, l):
            xq, xv, xo = f"xq{l}", f"xv{l}", f"xo{l}"
            norm_pe(pe, f"cross{l}", tnX)
            project_T(pe, FIRST[xq], UNITS.index(xq), xTX, T, lambda e, k: xT_there(e, f"cross{l}", k))

            def scores(x):
                n = XH * l + x
                group_evacuated(pe, FIRST[xq] + 2 * x + 1)
                for b in range(2):
                    if n >= 1:
                        pe.wait_ge(S("x_exp"), NT * (n - 1) + 2 * b + 2)
                    for t in (2 * b, 2 * b + 1):
                        for k in range(2):
                            ins = pe.matmul(PS[:, 4 + b, M * (t % 2):M * (t % 2) + M],
                                            qT[:, 2 * x + k, P * t:P * t + P], memK[:, 2 * x + k, :],
                                            start=(k == 0), stop=(k == 1))
                    ins.then_inc(S("x_scored"), 1)

            scores(0)
            for x in range(XH):
                n = XH * l + x
                if x + 1 < XH:
                    scores(x + 1)
                for m in range(2):
                    if n >= 1:
                        pe.wait_ge(S("x_probT"), 2 * (n - 1) + m + 1)
                    if x == 0:
                        xT_there(pe, f"cross{l}", 6 + m)
                    for t in range(NT):
                        pe.wait_ge(S("x_prob"), NT * n + t + 1)
                        ins = pe.transpose(PS[:, 6 + m, P * t:P * t + P], prob[x % 2][:, t, P * m:P * m + P],
                                           ident[:, :])
                    ins.then_inc(S("x_turned"), 1)
                pe.wait_ge(S("x_probT"), 2 * n + 2)
                for v in range(2):
                    g = FIRST[xv] + 2 * x + v
                    bank_free(pe, g)
                    for m in range(2):
                        ins = pe.matmul(PS[:, g % NBANK, :], memV[:, m, XD * x + P * v:XD * x + P * v + P],
                                        probT[x % 2][:, m, :], start=(m == 0), stop=(m == 1))
                    ins.then_inc(S("proj_filled"), 1)
            project_tok(pe, FIRST[xo], UNITS.index(xo), oT, lambda e, k: group_evacuated(e, FIRST[xv] + k))

        def cross_act(act, l, before):
            norm_act(act, f"cross{l}", h, tnX, h_tile_ready(before))
            xT_evac(act, f"cross{l}", xTX, 0)
            evac_T(act, FIRST[f"xq{l}"], qT)

            def out(x):
                for v in range(2):
                    act.activation(oT[:, 2 * x + v, :], group_out(act, FIRST[f"xv{l}"] + 2 * x + v), ACT.Copy)\
                        .then_inc(S("proj_out_A"), 1)

            for x in range(XH):
                n = XH * l + x
                if x == 0:
                    act.wait_ge(S("norm_turned"), TPOSE0[f"cross{l}"] + KC)
                if x >= 2:
                    act.wait_ge(S("x_turned"), 2 * (n - 1))
                for t in range(NT):
                    act.wait_ge(S("x_nmax"), 2 * n + t // 2 + 1)
                    act.activation(prob[x % 2][:, t, :], PS[:, 4 + t // 2, M * (t % 2):M * (t % 2) + M], ACT.Exp,
                                   bias=xmax[:, x % 2, t:t + 1], scale=XSCALE,
                                   accum_out=xsum[:, x % 2, t:t + 1]).then_inc(S("x_exp"), 1)
                if x >= 1:
                    out(x - 1)
            out(XH - 1)

        def cross_vec(vec, l):
            norm_vec(vec, f"cross{l}", h, tnX)
            xT_evac(vec, f"cross{l}", xTX, 1)

            def maxima(x):
                n = XH * l + x
                if x >= 2:
                    vec.wait_ge(S("x_exp"), NT * (n - 1))
                for b in range(2):
                    vec.wait_ge(S("x_scored"), 2 * n + b + 1)
                    m = xmax[:, x % 2, 2 * b:2 * b + 2]
                    vec.tensor_reduce(m, bank(4 + b, 2, M), AX.X, ALU.max).then_inc(S("x_max"), 1)
                    vec.wait_ge(S("x_max"), 2 * n + b + 1)
                    vec.tensor_scalar(m, m, -XSCALE, None, ALU.mult).then_inc(S("x_nmax"), 1)

            maxima(0)
            for x in range(XH):
                n = XH * l + x
                if x + 1 < XH:
                    maxima(x + 1)
                vec.wait_ge(S("x_exp"), NT * n + NT)
                vec.reciprocal(xsum[:, x % 2, :], xsum[:, x % 2, :]).then_inc(S("x_recip"), 1)
                vec.wait_ge(S("x_recip"), n + 1)
                for t in range(NT):
                    vec.tensor_scalar(prob[x % 2][:, t, :], prob[x % 2][:, t, :], xsum[:, x % 2, t:t + 1], None,
                                      ALU.mult).then_inc(S("x_prob"), 1)
                for m in range(2):
                    vec.wait_ge(S("x_turned"), 2 * n + m + 1)
                    if x >= 2:
                        vec.wait_ge(S("proj_filled"), FIRST[f"xv{l}"] + 2 * (x - 1))
                    vec.tensor_copy(probT[x % 2][:, m, :], PS[:, 6 + m, :]).then_inc(S("x_probT"), 1)
            add_to_h(vec, FIRST[f"xo{l}"])

        tnS = at(0, [NT, C])
        oTS = at(0, [KC, T])
        xTS = at(4, [KC, T])
        qTS = at(8, [KC, T])
        kTS = at(12, [KC, T])
        vS = at(16, [NT, C])
        fail = [at(20 + 0.625 * b, [T + 8]) for b in range(2)]
        beta = [at(21.5 + 0.5 * b, [T]) for b in range(2)]
        attT = [at(22.5 + 2 * a, [NT, T]) for a in range(2)]
        qs, ks, vs = at(32, [T]), at(32.5, [T]), at(33, [NT, P])
        NU = 2 * NT

        def sb_proj_pe(pe):
            norm_pe(pe, "mix1", tnS)
            project_T(pe, FIRST["sq"], UNITS.index("sqkv"), xTS, T, lambda e, k: xT_there(e, "mix1", k))
            project_T(pe, FIRST["sk"], UNITS.index("sqkv") + 2, xTS, T, lambda e, k: None)
            project_tok(pe, FIRST["sv"], UNITS.index("sqkv") + 4, xTS, lambda e, k: None)

        def sb_proj_act(act):
            norm_act(act, "mix1", h, tnS, lambda e, t: e.wait_ge(S("h_moe0"), t + 1))
            xT_evac(act, "mix1", xTS, 0)
            evac_T(act, FIRST["sq"], qTS)
            evac_T(act, FIRST["sk"], kTS)
            evac_tok(act, FIRST["sv"], vS)

        def sb_pool(pool):
            group_evacuated(pool, FIRST["sv"] + 7)
            with pool.Fori(0, NPAIR) as i:
                pool.wait_ge(S("sb_out_done"), i + 1)
                pool.tensor_copy(qs, qTS[:, i, :]).then_inc(S("sb_copied"), 1)
                pool.tensor_copy(ks, kTS[:, i, :]).then_inc(S("sb_copied"), 1)
                pool.tensor_copy(vs, vS.rearrange("p t (i n) -> p t i n", i=NPAIR)[:, :, i, :]).then_inc(S("sb_copied"), 1)
                for n in range(NU):
                    nn = P * (n % NT + 1)
                    pool.wait_ge(S("sb_sig"), 2 * (NU * i + n) + 1)
                    gate(pool)
                    f = fail[n % 2][:, T - P:T]
                    pool.affine_select(out=f, in_=f, compare_op=ALU.is_gt, fill=1.0, base=0, pattern=[[-1, P]],
                                       channel_multiplier=1).then_inc(S("sb_cut"), 1)
                    pool.wait_ge(S("sb_sig"), 2 * (NU * i + n) + 2)
                    gate(pool)
                    b = beta[n % 2][:, nn - P:nn]
                    pool.affine_select(out=b, in_=b, compare_op=ALU.is_gt, fill=0.0, base=0, pattern=[[-1, P]],
                                       channel_multiplier=1).then_inc(S("sb_cut"), 1)

        def sb_act(act):
            with act.Fori(0, NPAIR) as i:
                for n in range(NU):
                    nn = P * (n % NT + 1)
                    act.wait_ge(S("sb_scored"), NU * i + n + 1)
                    act.wait_ge(S("sb_turned"), NU * i + n + 1)
                    act.activation(fail[n % 2][:, T - nn:T], PS[:, n % NT, 0:nn], ACT.Sigmoid, scale=-HD ** -0.5)\
                        .then_inc(S("sb_sig"), 1)
                    act.activation(beta[n % 2][:, 0:nn], PS[:, n % NT, 0:nn], ACT.Sigmoid, scale=HD ** -0.5)\
                        .then_inc(S("sb_sig"), 1)
                    if n == NT + 1 or n == NU - 1:
                        hh = int(n == NU - 1)
                        r = slice(HD * hh, HD * hh + HD)
                        act.wait_ge(S("sb_summed"), 2 * i + hh + 1 + 2)
                        act.activation(oTS[r, i, :], PS[r, 6 + hh, :], ACT.Copy).then_inc(S("sb_oT"), 1)

        def sb_vec(vec):
            vec.wait_ge(S("norm_turned"), TPOSE0["mix1"] + KC)
            for b in range(2):
                vec.memset(fail[b][:, T:T + 1], 1.0).then_inc(S("sb_ones"), 1)
            vec.wait_ge(S("sb_ones"), 2)
            with vec.Fori(0, NPAIR) as i:
                for n in range(NU):
                    nn = P * (n % NT + 1)
                    t, hh = n % NT, n // NT
                    f, b = fail[n % 2], beta[n % 2]
                    vec.wait_ge(S("sb_cut"), 2 * (NU * i + n) + 2)
                    rev = f[:, T - nn:T][:, ::-1]
                    vec.tensor_tensor_scan(rev, rev, rev, 1.0, ALU.mult, ALU.min).then_inc(S("sb_scan"), 1)
                    vec.wait_ge(S("sb_scan"), NU * i + n + 1)
                    vec.tensor_tensor(b[:, 0:nn], b[:, 0:nn], f[:, T - nn + 1:T + 1], ALU.mult).then_inc(S("sb_att"), 1)
                    if n >= 1:
                        sb_turn_out(vec, i, n - 1)
                sb_turn_out(vec, i, NU - 1)

        def sb_turn_out(vec, i, n):
            t, hh = n % NT, n // NT
            vec.wait_ge(S("sb_turned"), NU * i + n + 1 + 2)
            vec.wait_ge(S("sb_summed"), 2 * i + hh + 1)
            vec.tensor_copy(attT[hh][:, 0:t + 1, P * t:P * t + P], bank(4 + n % 2, NT, P)[:, 0:t + 1, :])\
                .then_inc(S("sb_attT"), 1)

        def sb_pe(pe):
            group_evacuated(pe, FIRST["sv"] + 7)
            pe.nop().then_inc(S("sb_turned"), 2)
            pe.nop().then_inc(S("sb_summed"), 2)
            pe.nop().then_inc(S("sb_out_done"), 1)
            with pe.Fori(0, NPAIR) as i:
                def score(n):
                    t, r = n % NT, slice(HD * (n // NT), HD * (n // NT) + HD)
                    if n >= NT:
                        pe.wait_ge(S("sb_sig"), 2 * (NU * i + n - NT) + 2)
                    pe.matmul(PS[:, t, 0:P * (t + 1)], qs[r, P * t:P * t + P], ks[r, 0:P * (t + 1)],
                              start=True, stop=True).then_inc(S("sb_scored"), 1)

                pe.wait_ge(S("sb_copied"), 3 * i + 3)
                for n in range(NT):
                    score(n)
                for n in range(NU):
                    t, hh = n % NT, n // NT
                    pe.wait_ge(S("sb_att"), NU * i + n + 1)
                    if n >= 2:
                        pe.wait_ge(S("sb_attT"), NU * i + n - 1)
                    for s in range(t + 1):
                        ins = pe.transpose(PS[:, 4 + n % 2, P * s:P * s + P], beta[n % 2][:, P * s:P * s + P],
                                           ident[:, :])
                    ins.then_inc(S("sb_turned"), 1)
                    if n + NT < NU:
                        score(n + NT)
                    if t == NT - 1:
                        pe.wait_ge(S("sb_attT"), NU * i + n + 1)
                        gate(pe)
                        r = slice(HD * hh, HD * hh + HD)
                        for s in range(NT):
                            ins = pe.matmul(PS[r, 6 + hh, P * s:T], vs[:, s, r], attT[hh][:, s, P * s:T],
                                            start=(s == 0), stop=(s == NT - 1))
                        ins.then_inc(S("sb_summed"), 1)
                pe.wait_ge(S("sb_oT"), 2 * i + 2)
                pe.nop().then_inc(S("sb_out_done"), 1)
            project_tok(pe, FIRST["so"], UNITS.index("so"), oTS, lambda e, k: None)

        tnE = at(12, [NT, C])
        xTE = at(16, [KC, T])
        w13 = [at(6 * a, [2, KC, F]) for a in range(2)]
        w2e = [at(6 * a + 4, [2, C]) for a in range(2)]
        xg = [at(20 + a, [C]) for a in range(2)]
        xgT = [at(22 + 0.5 * a, [KC, BLK]) for a in range(2)]
        sig = [at(23 + 0.25 * a, [F]) for a in range(2)]
        hid = [at(23.5 + 0.25 * a, [F]) for a in range(2)]
        ye = [at(24 + a, [C]) for a in range(2)]
        hidT = [at(26 + 0.125 * a, [2, BLK]) for a in range(2)]
        yg = [at(12 + n, [C]) for n in range(8)]
        wge = at(26.25, [KC, G + NE])
        bge = at(26.75, [G + NE])
        su = masks[:, 0, :]
        lg = at(27, [NT, G + NE])
        mel = at(27.25, [NT, NE])
        mel2 = at(27.375, [NT, NE])
        O1 = at(27.5, [NT, NE])
        O2 = at(27.625, [NT, NE])
        OO = at(27.75, [NT, NE])
        sc = at(27.875, [NT, NE])
        rk = at(32, [NT + 1, NE])
        cmp_ = at(32.25, [NT * NE * 7])
        qq = at(33.125, [NT, NE])
        bm = at(33.25, [NT, NE])
        sm = at(33.375, [NT, NE])
        tmp = at(33.5, [NT, NE])
        OS = [at(33.625 + 0.0625 * n, [BLK]) for n in range(2)]
        OB = [at(33.75 + 0.0625 * n, [BLK]) for n in range(2)]
        iob = masks[:, 1, 0:BLK]
        w32 = masks[:, 1, 64:96]
        e31 = masks[:, 1, 96:128]
        ov = masks[:, 2, 0:96].rearrange("p (a e) -> p a e", a=3)
        thr = masks[:, 2, 96:103]
        tokid = masks[:, 2, 104:108]
        c4 = masks[:, 3, 0:48].rearrange("p (n t) -> p n t", n=12)
        gmax, gsum, v1, v2, s1, ed, den, wA, wB = [c4[:, n, :] for n in range(9)]
        bs = masks[:, 3, 48:64].rearrange("p (n t) -> p n t", n=4)
        overf = masks[:, 3, 64:96]
        pos = sb("pos", [P, NT, 2], I32)
        table = sb("table", [BLK, NBLK], I32)
        over = sb("over", [P, 32], I32)
        xi = [sb(f"xi{a}", [BLK, 1], I32) for a in range(2)]
        NSTEP = 76

        def moe_constants(pool):
            pool.iota(iob[:, :], [[1, BLK]], base=0, channel_multiplier=0,
                      allow_small_or_imprecise_dtypes=True).then_inc(S("iota_ready"), 1)
            pool.iota(w32[:, :], [[-1, NE]], base=NE, channel_multiplier=0,
                      allow_small_or_imprecise_dtypes=True).then_inc(S("iota_ready"), 1)
            pool.iota(thr[:, :], [[BLK, 7]], base=BLK, channel_multiplier=0,
                      allow_small_or_imprecise_dtypes=True).then_inc(S("iota_ready"), 1)
            pool.iota(e31[:, :], [[-1, NE]], base=NE - 1, channel_multiplier=0,
                      allow_small_or_imprecise_dtypes=True).then_inc(S("iota_ready"), 1)
            pool.iota(tokid[:, :], [[P, NT]], base=0, channel_multiplier=1,
                      allow_small_or_imprecise_dtypes=True).then_inc(S("iota_ready"), 1)

            pool.memset(su[:, :], 1.0).then_inc(S("iota_ready"), 1)
            pool.wait_ge(S("iota_ready"), 6)
            pool.affine_select(out=su[:, :], in_=su[:, :], compare_op=ALU.is_gt, fill=0.0, base=0, pattern=[[1, P]],
                               channel_multiplier=-1).then_inc(S("iota_ready"), 1)

        def experts(w, l, k):
            return w[l].rearrange("g e (p k) f -> (g e) p k f", k=k)

        def moe_route_loads(sp, l):
            sp.wait_ge(S("proj_filled"), FIRST[f"xo{l}"] + 8)
            sp.dma_start(wge[:, :, 0:G], A["moe_wg"][l].rearrange("(p k) n -> p k n", k=KC)).then_inc(S("route_in"), 16)
            sp.dma_start(wge[:, :, G:], A["moe_we"][l].rearrange("(p k) n -> p k n", k=KC)).then_inc(S("route_in"), 16)
            sp.dma_start(bge[:, 0:G], bcast(A["moe_bg"][l])).then_inc(S("route_in"), 16)
            sp.dma_start(bge[:, G:], bcast(A["moe_be"][l])).then_inc(S("route_in"), 16)

        def moe_route_pe(pe, l):
            norm_pe(pe, f"ffn{l}", tnE)
            for k in range(KC):
                xT_there(pe, f"ffn{l}", k)
            pe.wait_ge(S("route_in"), 64 * (l + 1))
            for t in range(NT):
                for k in range(KC):
                    ins = pe.matmul(PS[:, 5, 64 * t:64 * t + G + NE], xTE[:, k, P * t:P * t + P], wge[:, k, :],
                                    start=(k == 0), stop=(k == KC - 1))
            ins.then_inc(S("logits"), 1)
            pe.wait_ge(S("chosen"), l + 1)
            pe.wait_ge(S("iota_ready"), 7)
            for t in range(NT + 1):
                for s in range(min(t, NT - 1) + 1):
                    ins = pe.matmul(PS[:, 4, NE * t:NE * t + NE], su[:, :] if s == t else ones[:, :], OO[:, s, :],
                                    start=(s == 0), stop=(s == min(t, NT - 1)))
            ins.then_inc(S("ranked"), 1)
            for n in range(8):
                pe.wait_ge(S("onehots"), 2 * (8 * l + n) + 2)
                pe.matmul(PS[0:BLK, 5, 0:NBLK], OS[n % 2], OB[n % 2][:, 0:NBLK], start=(n == 0), stop=(n == 7))\
                    .then_inc(S("tabled"), 1)

        def moe_route_act(act, l):
            norm_act(act, f"ffn{l}", h, tnE, h_tile_ready(f"xo{l}"))
            xT_evac(act, f"ffn{l}", xTE, 0)
            act.wait_ge(S("route_a"), 2 * l + 1)
            act.activation(sc[:, :, 0:G], mel2[:, :, 0:G], ACT.Exp).then_inc(S("route_exp"), 1)
            act.wait_ge(S("route_a"), 2 * l + 2)
            act.activation(ed, ed, ACT.Exp).then_inc(S("route_exp"), 1)

        def moe_route_vec(vec, l):
            norm_vec(vec, f"ffn{l}", h, tnE)
            xT_evac(vec, f"ffn{l}", xTE, 1)
            step = S("route_step")
            n = [l * 10000]
            done = [ROUTE_STEPS * l]

            def do(ins):
                ins.then_inc(step, 1)
                done[0] += 1
                vec.wait_ge(step, done[0])

            def wide(m, k):
                return m.unsqueeze(2).to_broadcast([P, NT, k])

            vec.wait_ge(S("iota_ready"), 7)
            vec.wait_ge(S("logits"), l + 1)
            do(vec.tensor_tensor(lg, PS[:, 5, 0:256].rearrange("p (t n) -> p t n", t=NT)[:, :, 0:G + NE],
                                 bge.unsqueeze(1).to_broadcast([P, NT, G + NE]), ALU.add))
            gl, el = lg[:, :, 0:G], lg[:, :, G:]
            do(vec.tensor_reduce(gmax, gl, AX.X, ALU.max))
            vec.tensor_tensor(mel2[:, :, 0:G], gl, wide(gmax, G), ALU.subtract).then_inc(S("route_a"), 1)
            do(vec.tensor_tensor(mel[:, :, 0:G], gl, wide(gmax, G), ALU.is_equal))
            do(vec.tensor_tensor(mel[:, :, 0:G], mel[:, :, 0:G], w32[:, 0:G].unsqueeze(1).to_broadcast([P, NT, G]),
                                 ALU.mult))
            do(vec.tensor_reduce(s1, mel[:, :, 0:G], AX.X, ALU.max))
            do(vec.tensor_tensor(mel[:, :, 0:G], mel[:, :, 0:G], wide(s1, G), ALU.is_equal))
            vec.wait_ge(S("route_exp"), 2 * l + 1)
            do(vec.tensor_reduce(gsum, sc[:, :, 0:G], AX.X, ALU.add))
            do(vec.tensor_scalar(tmp[:, :, 0:G], mel[:, :, 0:G], -1.0, BIG, ALU.add, ALU.mult))
            for t in range(NT):
                ins = vec.tensor_tensor(mel[:, t, :].rearrange("p (g e) -> p g e", g=G),
                                        el[:, t, :].rearrange("p (g e) -> p g e", g=G),
                                        tmp[:, t, 0:G].unsqueeze(2).to_broadcast([P, G, E]), ALU.add)
                if t == NT - 1:
                    do(ins)
            for O, v, m in ((O1, v1, mel), (O2, v2, mel2)):
                do(vec.tensor_reduce(v, m, AX.X, ALU.max))
                do(vec.tensor_tensor(O, m, wide(v, NE), ALU.is_equal))
                do(vec.tensor_tensor(O, O, w32[:, :].unsqueeze(1).to_broadcast([P, NT, NE]), ALU.mult))
                do(vec.tensor_reduce(s1, O, AX.X, ALU.max))
                do(vec.tensor_tensor(O, O, wide(s1, NE), ALU.is_equal))
                if O is O1:
                    do(vec.scalar_tensor_tensor(out=mel2, in0=O1, scalar=-2 * BIG, in1=mel, op0=ALU.mult, op1=ALU.add))
            vec.tensor_tensor(OO, O1, O2, ALU.add).then_inc(S("chosen"), 1)
            vec.tensor_tensor(ed, v2, v1, ALU.subtract).then_inc(S("route_a"), 1)
            vec.wait_ge(S("ranked"), l + 1)
            do(vec.tensor_copy(rk, PS[:, 4, 0:(NT + 1) * NE].rearrange("p (t e) -> p t e", t=NT + 1)))
            rank, count = rk[:, 0:NT, :].rearrange("p t e -> p (t e)"), rk[:, NT, :]
            c3 = cmp_.rearrange("p (a b) -> p a b", b=7)
            th = thr[:, :].unsqueeze(1)
            do(vec.tensor_tensor(c3[:, 0:NE, :], count.unsqueeze(2).to_broadcast([P, NE, 7]),
                                 th.to_broadcast([P, NE, 7]), ALU.is_gt))
            do(vec.tensor_reduce(ov[:, 0, :], c3[:, 0:NE, :], AX.X, ALU.add))
            do(vec.tensor_tensor_scan(ov[:, 1, :], ones[:, 0:NE], ov[:, 0, :], 0.0, ALU.mult, ALU.add))
            do(vec.tensor_tensor(ov[:, 2, :], ov[:, 1, :], ov[:, 0, :], ALU.subtract))
            do(vec.tensor_tensor(ov[:, 2, :], ov[:, 2, :], e31[:, :], ALU.add))
            c4_ = cmp_[:, 0:16 * NE].rearrange("p (a b) -> p a b", b=NE)
            do(vec.tensor_tensor(c4_, ov[:, 1, :].unsqueeze(1).to_broadcast([P, 16, NE]),
                                 iob[:, 0:16].unsqueeze(2).to_broadcast([P, 16, NE]), ALU.is_le))
            do(vec.tensor_reduce(overf[:, 0:16], c4_, AX.X, ALU.add))
            do(vec.tensor_scalar(overf[:, 0:16], overf[:, 0:16], float(NE - 1), None, ALU.min))
            do(vec.tensor_copy(overf[:, 16:17], ov[:, 1, NE - 1:NE]))
            vec.tensor_copy(over[:, 0:17], overf[:, 0:17]).then_inc(S("over_known"), 1)
            do(vec.tensor_tensor(c3, rank.unsqueeze(2).to_broadcast([P, NT * NE, 7]),
                                 th.to_broadcast([P, NT * NE, 7]), ALU.is_ge))
            do(vec.tensor_reduce(qq.rearrange("p t e -> p (t e)"), c3, AX.X, ALU.add))
            do(vec.scalar_tensor_tensor(out=sm, in0=qq, scalar=-float(BLK), in1=rk[:, 0:NT, :], op0=ALU.mult, op1=ALU.add))
            do(vec.tensor_tensor(bm, qq, ov[:, 2, :].unsqueeze(1).to_broadcast([P, NT, NE]), ALU.add))
            do(vec.tensor_scalar(qq, qq, 0.0, None, ALU.is_gt))
            do(vec.tensor_tensor(bm, bm, qq, ALU.mult))
            do(vec.tensor_tensor(bm, bm, e31[:, :].unsqueeze(1).to_broadcast([P, NT, NE]), ALU.subtract))
            do(vec.tensor_scalar(bm, bm, float(NE - 1), None, ALU.add))
            for k, O in enumerate((O1, O2)):
                for j, m in enumerate((bm, sm)):
                    do(vec.tensor_tensor(tmp, O, m, ALU.mult))
                    do(vec.tensor_reduce(bs[:, 2 * j + k, :], tmp, AX.X, ALU.add))
            if l:
                vec.wait_ge(S("yg_in3"), 32)
            do(vec.scalar_tensor_tensor(out=c4[:, 9:11, :], in0=bs[:, 0:2, :], scalar=float(BLK), in1=bs[:, 2:4, :],
                                        op0=ALU.mult, op1=ALU.add))
            vec.tensor_copy(pos[:, :, :].rearrange("p t k -> p k t"), c4[:, 9:11, :]).then_inc(S("pos_known"), 1)
            for m in range(8):
                k, t = m // NT, m % NT
                if m >= 2:
                    vec.wait_ge(S("tabled"), 8 * l + m - 1)
                vec.tensor_scalar(OS[m % 2], iob[:, :], bs[:, 2 + k, t:t + 1], None, ALU.is_equal)\
                    .then_inc(S("onehots"), 1)
                vec.tensor_scalar(OB[m % 2], iob[:, :], bs[:, k, t:t + 1], tokid[:, t:t + 1], ALU.is_equal, ALU.mult)\
                    .then_inc(S("onehots"), 1)
            vec.wait_ge(S("tabled"), 8 * l + 8)
            vec.tensor_copy(table[:, :], PS[0:BLK, 5, 0:NBLK]).then_inc(S("table_ready"), 1)
            vec.wait_ge(S("route_exp"), 2 * l + 2)
            do(vec.tensor_scalar(den, ed, 1.0, None, ALU.add))
            do(vec.tensor_tensor(den, den, gsum, ALU.mult))
            do(vec.reciprocal(wA, den))
            do(vec.tensor_tensor(wB, wA, ed, ALU.mult))
            assert done[0] == ROUTE_STEPS * (l + 1), done[0] - ROUTE_STEPS * l
        ROUTE_STEPS = 51

        def moe_rows_out(sp, l):
            for t in range(NT):
                sp.wait_ge(S("norm_rows"), TILE0[f"ffn{l}"] + t + 1)
                sp.dma_start(scratch["rows"][P * t:P * t + P, :], tnE[:, t, :]).then_inc(S("rows_out"), 16)

        CREDIT = NE // 2 + 1

        def load_up(sp, l, e, a, sem):
            sp.dma_start(w13[a][:, 0, :, :], experts(A["moe_w1"], l, KC)[e]).then_inc(sem, 16)
            sp.dma_start(w13[a][:, 1, :, :], experts(A["moe_w3"], l, KC)[e]).then_inc(sem, 16)

        def load_down(sp, l, e, a, sem):
            sp.dma_start(w2e[a], experts(A["moe_w2"], l, 2)[e]).then_inc(sem, 16)

        def moe_first_loads(sp, l):
            sp.wait_ge(S("proj_filled"), FIRST["so" if l else "rwo"] + 8)
            for a in range(2):
                load_up(sp, l, a, a, S(f"w13_in{a}"))
                load_down(sp, l, a, a, S(f"w2_in{a}"))

        def moe_loads(sp, l):
            with sp.Fori(1, NE // 2) as i:
                for a in range(2):
                    sp.wait_ge(S(f"up_done{a}"), NE // 2 * l + i)
                    load_up(sp, l, 2 * i + a, a, S(f"w13_in{a}"))
                    sp.wait_ge(S(f"down_done{a}"), NE // 2 * l + i)
                    load_down(sp, l, 2 * i + a, a, S(f"w2_in{a}"))

        def moe_pool(pool, l):
            pool.wait_ge(S("table_ready"), l + 1)
            pool.wait_ge(S("rows_out"), 16 * NT * (l + 1))
            with pool.Fori(0, NE // 2) as i:
                for a in range(2):
                    pool.wait_ge(S(f"xg_free{a}"), CREDIT * l + i + 1)
                    pool.tensor_copy(xi[a][:, :], table[:, bass.ds(2 * i + a, 1)]).then_inc(S(f"xi_ready{a}"), 1)
                    pool.wait_ge(S(f"xi_ready{a}"), NE // 2 * l + i + 1)
                    gate(pool)
                    pool.indirect_dma_start(out=xg[a][0:BLK, :], out_offset=None, in_=scratch["rows"],
                                            in_offset=bass.IndirectOffsetOnAxis(ap=xi[a][:, 0:1], axis=0))\
                        .then_inc(S(f"xg_in{a}"), 16)

        def moe_combine_pool(pool, l):
            pool.wait_ge(S("pos_known"), l + 1)
            for a in range(2):
                pool.wait_ge(S(f"ye_out{a}"), 16 * CREDIT * (l + 1))
            pool.wait_ge(S("over_done"), l + 1)
            pool.wait_ge(S("spare_filled"), 32)
            for t in range(NT):
                for k in range(2):
                    pool.indirect_dma_start(out=yg[2 * t + k], out_offset=None, in_=scratch["blocks"],
                                            in_offset=bass.IndirectOffsetOnAxis(ap=pos[:, t, k:k + 1], axis=0))\
                        .then_inc(S(f"yg_in{t}"), 16)

        def moe_combine_vec(vec, l):
            for t in range(NT):
                vec.wait_ge(S(f"yg_in{t}"), 32 * (l + 1))
                for k, w in enumerate((wA, wB)):
                    if k:
                        vec.wait_ge(S("h_half"), NT * l + t + 1)
                    vec.scalar_tensor_tensor(out=h[:, t, :], in0=yg[2 * t + k], scalar=w[:, t:t + 1], in1=h[:, t, :],
                                             op0=ALU.mult, op1=ALU.add)\
                        .then_inc(S("h_half") if k == 0 else S(f"h_moe{l}"), 1)

        def turn_rows(pe, a):
            for k in range(KC):
                ins = pe.transpose(PS[:, a, BLK * k:BLK * k + BLK], xg[a][0:BLK, k::KC], ident[0:BLK, 0:BLK])
            return ins

        def xgT_out(vec, l, a):
            return vec.tensor_tensor(xgT[a], bank(a, KC, BLK),
                                     gainT[:, GAIN[f"ffn{l}"], :].unsqueeze(2).to_broadcast([P, KC, BLK]), ALU.mult)

        def up(pe, a):
            for k in range(KC):
                ins = pe.matmul(bank(2 + a, 2, F)[0:BLK, :, :], xgT[a][:, k, :], w13[a][:, :, k, :],
                                start=(k == 0), stop=(k == KC - 1))
            return ins

        def sig_out(act, a):
            return act.activation(sig[a][0:BLK, :], PS[0:BLK, 2 + a, 0:F], ACT.Sigmoid)

        def silu_half(vec, a):
            return vec.tensor_tensor(hid[a][0:BLK, :], PS[0:BLK, 2 + a, 0:F], sig[a][0:BLK, :], ALU.mult)

        def hid_out(vec, a):
            return vec.tensor_tensor(hid[a][0:BLK, :], PS[0:BLK, 2 + a, F:2 * F], hid[a][0:BLK, :], ALU.mult)

        def turn_hid(pe, a):
            for k in range(2):
                ins = pe.transpose(PS[:, 4 + a, BLK * k:BLK * k + BLK], hid[a][0:BLK, k::2], ident[0:BLK, 0:BLK])
            return ins

        def hidT_out(act, a):
            return act.activation(hidT[a], PS[:, 4 + a, 0:2 * BLK].rearrange("p (k n) -> p k n", k=2), ACT.Copy)

        def down(pe, a, half):
            for k in range(2):
                ins = pe.matmul(PS[0:BLK, 6 + half, :], hidT[a][:, k, :], w2e[a][:, k, 512 * half:512 * half + 512],
                                start=(k == 0), stop=(k == 1))
            return ins

        def ye_half(a, half):
            return ye[a][0:BLK, 512 * half:512 * half + 512], PS[0:BLK, 6 + half, :]

        def moe_pe(pe, l):
            L = CREDIT * l
            NB = NE * l
            pe.wait_ge(S("table_ready"), l + 1)
            for a in range(2):
                pe.nop().then_inc(S(f"xg_free{a}"), 1)
            with pe.Fori(0, NE // 2) as i:
                for a in range(2):
                    pe.wait_ge(S(f"xg_in{a}"), 16 * (NE // 2 * l + i + 1))
                    gate(pe)
                    turn_rows(pe, a).then_inc(S(f"xg_free{a}"), 1)
                for a in range(2):
                    pe.wait_ge(S("xgT_ready"), NB + 2 * i + a + 1)
                    pe.wait_ge(S(f"w13_in{a}"), 32 * (NE // 2 * l + i + 1))
                    up(pe, a).then_inc(S(f"up_done{a}"), 1)
                for a in range(2):
                    pe.wait_ge(S("hid_ready"), NB + 2 * i + a + 1)
                    gate(pe)
                    turn_hid(pe, a).then_inc(S("hid_turned"), 1)
                    pe.wait_ge(S(f"w2_in{a}"), 16 * (NE // 2 * l + i + 1))
                    pe.wait_ge(S("hidT_ready"), NB + 2 * i + a + 1)
                    pe.wait_ge(S("ye_a"), NB + l + 2 * i + a + 1)
                    gate(pe)
                    down(pe, a, 0).then_inc(S("down_half"), 1)
                    pe.wait_ge(S("ye_v"), NB + l + 2 * i + a + 1)
                    gate(pe)
                    down(pe, a, 1).then_inc(S(f"down_done{a}"), 1)

        def moe_act(act, l):
            NB = NE * l
            act.wait_ge(S("table_ready"), l + 1)
            act.nop().then_inc(S("ye_a"), 1)
            for a in range(2):
                act.nop().then_inc(S(f"ye_out{a}"), 16)
            with act.Fori(0, NE // 2) as i:
                for a in range(2):
                    act.wait_ge(S(f"up_done{a}"), NE // 2 * l + i + 1)
                    sig_out(act, a).then_inc(S("sig_ready"), 1)
                for a in range(2):
                    act.wait_ge(S("hid_turned"), NB + 2 * i + a + 1)
                    hidT_out(act, a).then_inc(S("hidT_ready"), 1)
                    act.wait_ge(S("down_half"), NB + 2 * i + a + 1)
                    act.wait_ge(S(f"ye_out{a}"), 16 * (NE // 2 * l + l + i + 1))
                    d, s = ye_half(a, 0)
                    act.activation(d, s, ACT.Copy).then_inc(S("ye_a"), 1)
                    act.wait_ge(S("ye_v"), NB + l + 2 * i + a + 2)
                    act.wait_ge(S("ye_a"), NB + l + 2 * i + a + 2)
                    act.dma_start(scratch["blocks"].rearrange("(b r) c -> b r c", r=BLK)[2 * i + a], ye[a][0:BLK, :])\
                        .then_inc(S(f"ye_out{a}"), 16)

        def moe_vec(vec, l):
            NB = NE * l
            vec.nop().then_inc(S("ye_v"), 1)
            with vec.Fori(0, NE // 2) as i:
                for a in range(2):
                    vec.wait_ge(S(f"xg_free{a}"), CREDIT * l + i + 2)
                    xgT_out(vec, l, a).then_inc(S("xgT_ready"), 1)
                for a in range(2):
                    vec.wait_ge(S("sig_ready"), NB + 2 * i + a + 1)
                    silu_half(vec, a).then_inc(S("silu_ready"), 1)
                    vec.wait_ge(S("silu_ready"), NB + 2 * i + a + 1)
                    hid_out(vec, a).then_inc(S("hid_ready"), 1)
                for a in range(2):
                    vec.wait_ge(S(f"down_done{a}"), NE // 2 * l + i + 1)
                    vec.wait_ge(S(f"ye_out{a}"), 16 * (NE // 2 * l + l + i + 1))
                    d, s = ye_half(a, 1)
                    vec.tensor_copy(d, s).then_inc(S("ye_v"), 1)

        def further(eng, l, body):
            eng.wait_ge(S("over_known"), l + 1)
            n = eng.value_load(over[0:1, 16:17], min_val=0, max_val=NOVER)
            with eng.Fori(0, NOVER) as j:
                with eng.If(j < n):
                    body(j, lambda k: eng.wait_ge(S(f"over_step{l}"), j * NSTEP + k))

        def further_pool(pool, l):
            st = S(f"over_step{l}")

            def body(j, at_step):
                at_step(1)
                pool.tensor_copy(xi[0][:, :], table[:, bass.ds(NE + j, 1)]).then_inc(st, 1)
                at_step(2)
                gate(pool)
                pool.indirect_dma_start(out=xg[0][0:BLK, :], out_offset=None, in_=scratch["rows"],
                                        in_offset=bass.IndirectOffsetOnAxis(ap=xi[0][:, 0:1], axis=0))\
                    .then_inc(S(f"over_gathered{l}"), 16)
            further(pool, l, body)

        def further_sp(sp, l):
            st = S(f"over_step{l}")
            for a in range(2):
                sp.wait_ge(S(f"ye_out{a}"), 16 * (NE // 2 + 1) * (l + 1))
            sp.nop().then_inc(st, 1)

            def body(j, at_step):
                e = sp.value_load(over[0:1, bass.ds(j, 1)], min_val=0, max_val=NE - 1)
                at_step(2)
                load_up(sp, l, e, 0, st)
                load_down(sp, l, e, 0, st)
                at_step(61)
                sp.dma_start(scratch["blocks"].rearrange("(b r) c -> b r c", r=BLK)[NE + j], ye[0][0:BLK, :])\
                    .then_inc(st, 16)
                at_step(77)
                gate(sp)
            further(sp, l, body)
            sp.nop().then_inc(S("over_done"), 1)

        def further_pe(pe, l):
            st = S(f"over_step{l}")

            def step(at_step, k):
                at_step(k)
                gate(pe)

            def body(j, at_step):
                pe.wait_ge(S(f"over_gathered{l}"), 16 * (j + 1))
                step(at_step, 50)
                turn_rows(pe, 0).then_inc(st, 1)
                step(at_step, 52)
                up(pe, 0).then_inc(st, 1)
                step(at_step, 56)
                turn_hid(pe, 0).then_inc(st, 1)
                step(at_step, 58)
                down(pe, 0, 0)
                down(pe, 0, 1).then_inc(st, 1)
            further(pe, l, body)

        def further_act(act, l):
            st = S(f"over_step{l}")

            def body(j, at_step):
                at_step(53)
                sig_out(act, 0).then_inc(st, 1)
                at_step(57)
                hidT_out(act, 0).then_inc(st, 1)
                at_step(59)
                d, s = ye_half(0, 0)
                act.activation(d, s, ACT.Copy).then_inc(st, 1)
            further(act, l, body)

        def further_vec(vec, l):
            st = S(f"over_step{l}")

            def body(j, at_step):
                at_step(51)
                xgT_out(vec, l, 0).then_inc(st, 1)
                at_step(54)
                silu_half(vec, 0).then_inc(st, 1)
                at_step(55)
                hid_out(vec, 0).then_inc(st, 1)
                at_step(60)
                d, s = ye_half(0, 1)
                vec.tensor_copy(d, s).then_inc(st, 1)
            further(vec, l, body)

        tnF = at(0, [NT, C])
        gF = at(4, [C])

        def final_act(act):
            norm_act(act, "final", h, tnF, lambda e, t: e.wait_ge(S("h_moe1"), t + 1))

        def final_vec(vec):
            norm_vec(vec, "final", h, tnF)
            vec.wait_ge(S("final_gain_in"), 16)
            for t in range(NT):
                vec.wait_ge(S("norm_rows"), TILE0["final"] + t + 1)
                vec.tensor_tensor(tnF[:, t, :], tnF[:, t, :], gF, ALU.mult).then_inc(S("result"), 1)

        def final_sp(sp):
            sp.wait_ge(S("over_done"), 2)
            sp.dma_start(gF, bcast(A["norm_final"])).then_inc(S("final_gain_in"), 16)
            for t in range(NT):
                sp.wait_ge(S("result"), t + 1)
                sp.dma_start(out[0, P * t:P * t + P, :], tnF[:, t, :]).then_inc(S("result_out"), 16)
            sp.wait_ge(S("result_out"), 16 * NT)

        block = ctx.enter_context(nc.Block())

        def at_unit(name):
            return UNITS.index(name)

        @block.sync
        def _(sp):
            loads_first(sp)
            load_units(sp, 0, 6)
            spare = scratch["blocks"][NE * BLK:NBLK * BLK, :]
            sp.dma_start(spare[0:T, :], A["x"][0]).then_inc(S("spare_filled"), 16)
            sp.dma_start(spare[T:NOVER * BLK, :], A["x"][0, 0:NOVER * BLK - T, :]).then_inc(S("spare_filled"), 16)
            loads_after_pairs(sp)
            load_units(sp, 6, at_unit("xo0"))
            moe_first_loads(sp, 0)
            load_units(sp, at_unit("xo0"), at_unit("sqkv") + 1)
            moe_route_loads(sp, 0)
            load_units(sp, at_unit("sqkv") + 1, at_unit("sqkv") + 3)
            moe_rows_out(sp, 0)
            moe_loads(sp, 0)
            further_sp(sp, 0)
            load_units(sp, at_unit("sqkv") + 3, at_unit("xo1"))
            moe_first_loads(sp, 1)
            load_units(sp, at_unit("xo1"), len(UNITS))
            moe_route_loads(sp, 1)
            moe_rows_out(sp, 1)
            moe_loads(sp, 1)
            further_sp(sp, 1)
            final_sp(sp)

        @block.gpsimd
        def _(pool):
            constants(pool)
            pair_pool(pool)
            post_pool(pool)
            moe_constants(pool)
            for l in range(2):
                if l == 1:
                    sb_pool(pool)
                moe_pool(pool, l)
                further_pool(pool, l)
                moe_combine_pool(pool, l)

        @block.scalar
        def _(act):
            norm_act(act, "mix0", h, tn0, lambda e, t: e.wait_ge(S(f"x_in{t}"), 16))
            act.wait_ge(S("small_in"), SMALL)
            xT_evac(act, "mix0", xT, 0)
            rwkv_proj_act(act)
            rwkv_pre_act(act)
            pair_act(act)
            mem_act(act)
            post_act(act)
            for l in range(2):
                if l == 1:
                    sb_proj_act(act)
                    sb_act(act)
                cross_act(act, l, "so" if l else "rwo")
                moe_route_act(act, l)
                moe_act(act, l)
                further_act(act, l)
            final_act(act)

        @block.tensor
        def _(pe):
            pe.wait_ge(S("const_ready"), 1)
            norm_pe(pe, "mix0", tn0)
            rwkv_proj_pe(pe)
            rwkv_pre_pe(pe)
            pair_pe(pe)
            mem_pe(pe)
            post_pe(pe)
            for l in range(2):
                if l == 1:
                    sb_proj_pe(pe)
                    sb_pe(pe)
                cross_pe(pe, l)
                moe_route_pe(pe, l)
                moe_pe(pe, l)
                further_pe(pe, l)

        @block.vector
        def _(vec):
            for t in range(NT):
                vec.wait_ge(S(f"x_in{t}"), 16)
            norm_vec(vec, "mix0", h, tn0)
            vec.wait_ge(S("small_in"), SMALL)
            xT_evac(vec, "mix0", xT, 1)
            prm_vec(vec)
            rwkv_mix_vec(vec)
            rwkv_pre_vec(vec)
            pair_vec(vec)
            mem_vec(vec)
            post_vec(vec)
            add_to_h(vec, FIRST["rwo"], x_back)
            for l in range(2):
                if l == 1:
                    norm_vec(vec, "mix1", h, tnS)
                    xT_evac(vec, "mix1", xTS, 1)
                    sb_vec(vec)
                    add_to_h(vec, FIRST["so"])
                cross_vec(vec, l)
                moe_route_vec(vec, l)
                moe_vec(vec, l)
                further_vec(vec, l)
                moe_combine_vec(vec, l)
            final_vec(vec)

_INS = ["x", "mem", "norm_mix", "norm_cross", "norm_ffn", "norm_mem", "norm_final",
        "rw_mix", "rw_wr", "rw_wk", "rw_wv", "rw_w0", "rw_w1", "rw_w2", "rw_a0", "rw_a1", "rw_a2",
        "rw_g1", "rw_g2", "rw_kk", "rw_ka", "rw_rk", "rw_lnx_w", "rw_lnx_b", "rw_wo",
        "sb_wqkv", "sb_wo", "xa_wq", "xa_wkv", "xa_wo",
        "moe_wg", "moe_bg", "moe_we", "moe_be", "moe_w1", "moe_w3", "moe_w2"]


def kernel(**inputs):
    import numpy as _np
    import concourse.bacc as _bacc
    from concourse.bass_utils import run_bass_kernel_spmd as _run

    nc = _bacc.Bacc("TRN2", target_bir_lowering=False, num_devices=1)
    arrays, aps = {}, {}
    for name in _INS:
        a = _np.ascontiguousarray(inputs[name])
        arrays[f"in_{name}"] = a
        aps[name] = nc.dram_tensor(f"in_{name}", a.shape, mybir.dt.from_np(a.dtype), kind="ExternalInput").ap()
    out = nc.dram_tensor("out_0", (1, T, C), F32, kind="ExternalOutput").ap()
    scratch = {
        "rows": nc.dram_tensor("normed_rows", (T, C), F32, kind="Internal").ap(),
        "blocks": nc.dram_tensor("expert_rows", (NBLK * BLK, C), F32, kind="Internal").ap(),
    }
    trunk(nc, aps, out, scratch)
    r = _run(nc, [arrays], core_ids=[0])
    return r.results[0]["out_0"]
```

```python
from contextlib import ExitStack

import concourse.bass as bass
from concourse import mybir

F32 = mybir.dt.float32
I32 = mybir.dt.int32
ALU = mybir.AluOpType
ACT = mybir.ActivationFunctionType
AX = mybir.AxisListType

P = 128
C = 1024
T = 512
NT = T // P
KC = C // P
NPAIR = KC
HD = 64
CH = 64
NCH = T // CH
M = 256
XH = 4
XD = C // XH
G, E = 4, 8
NE = G * E
F = 256
BLK = 64
NOVER = (2 * T - NE) // BLK
NBLK = NE + NOVER
EPS = 1e-6
GN_EPS = 64e-5
DECAY_C = float(2.718281828459045 ** -0.5)
XSCALE = float(XD) ** -0.5
BIG = 1e30

RING = 3

PLAN = [
    ("w1", 1, "A"), ("a1", 1, "A"), ("g1", 1, "A"),
    ("wr", 8, "A"), ("wk", 8, "A"), ("wv", 8, "A"),
    ("memk", 8, "A"), ("memv", 4, "A"),
    ("gate", 8, "V"), ("rwo", 8, "V"),
    ("xq0", 8, "A"), ("xv0", 8, "A"), ("xo0", 8, "V"),
    ("sq", 8, "A"), ("sk", 8, "A"), ("sv", 8, "A"), ("so", 8, "V"),
    ("xq1", 8, "A"), ("xv1", 8, "A"), ("xo1", 8, "V"),
]
FIRST, OWNER = {}, []
for _name, _n, _eng in PLAN:
    FIRST[_name] = len(OWNER)
    OWNER += [_eng[_g % len(_eng)] for _g in range(_n)]
NBANK = 4


def groups_done(g):
    return OWNER[:g + 1].count(OWNER[g])


UNITS = ["wr", "wr", "wk", "wk", "wv", "wv",
         "memkv", "memkv", "memkv", "memkv", "rwo", "rwo", "xq0", "xq0", "xo0", "xo0",
         "sqkv", "sqkv", "sqkv", "sqkv", "sqkv", "sqkv", "so", "so",
         "xq1", "xq1", "xo1", "xo1"]

FILLS = [("TA", 0, "A"), ("TV", 1, "A"), ("TB", 0, "A"), ("TK", 1, "A"), ("BN", 0, "V")]
for _s, _e in [("A0", "V"), ("A1", "V"), ("CC", "V"), ("B0", "V"), ("B1", "V"),
               ("Q2", "A"), ("Q2T", "A"), ("WV", "A"),
               ("Q4", "A"), ("Q4T", "A"), ("Z2", "V"),
               ("Q8", "A"), ("Z3", "V"), ("Z4", "V"),
               ("X", "A"), ("XT", "V"), ("R1", "V"),
               ("X2T", "A"), ("R2", "V"), ("R3", "V")]:
    FILLS += [(_s, 0, _e), (_s, 1, _e)]
FILLS += [("G", 0, "V"), ("G", 1, "V"), ("H", 0, "A"), ("H", 1, "A"), ("RP", 0, "V")]
FILLS += [(f"S{_c}", 0, "V") for _c in range(1, NCH - 1)]
FILLS += [("Y", 1, "A")]
FILL_NO = {(s, h): n for n, (s, h, e) in enumerate(FILLS)}
NFILL = len(FILLS)


def bank_of(n):
    h = FILLS[n][1]
    return 4 * h + sum(1 for s in FILLS[:n] if s[1] == h) % 4


def bank_before(n):
    h = FILLS[n][1]
    mine = [m for m in range(n) if FILLS[m][1] == h]
    return mine[-4] if len(mine) >= 4 else None


def evacs(n):
    return sum(1 for s in FILLS[:n + 1] if s[2] == FILLS[n][2])


NEV = {e: sum(1 for s in FILLS if s[2] == e) for e in "AV"}

NEEDS = {
    "Q2": lambda h: [("CC", h)], "Q2T": lambda h: [("CC", h)], "WV": lambda h: [("B1", h), ("TV", 1)],
    "Q4": lambda h: [("Q2T", h)], "Q4T": lambda h: [("Q2T", h)], "Z2": lambda h: [("Q2", h)],
    "Q8": lambda h: [("Q4T", h)], "Z3": lambda h: [("Z2", h), ("Q4", h)], "Z4": lambda h: [("Q8", h), ("Z3", h)],
    "X": lambda h: [("Z4", h)], "XT": lambda h: [("Z4", h)], "R1": lambda h: [("Z4", h), ("WV", h)],
    "X2T": lambda h: [("X", h), ("XT", h)], "R2": lambda h: [("X2T", h), ("R1", h)],
    "R3": lambda h: [("R2", h)], "G": lambda h: [("R3", 1), ("TB", 0)], "H": lambda h: [("R3", 1), ("TK", 1)],
    "RP": lambda h: [("R3", 1)],
    "S1": lambda h: [("G", 1), ("H", 1)], "Y": lambda h: [("R3", 0), ("R3", 1)],
}
for _c in range(2, NCH - 1):
    NEEDS[f"S{_c}"] = lambda h, c=_c: [(f"S{c - 1}", 0)]


def trunk(nc, A, out, scratch):
    ctx = ExitStack()
    with ctx:
        def sb(name, shape, dt=F32):
            return ctx.enter_context(nc.sbuf_tensor(name, shape, dt))

        sems = {}

        def S(name):
            if name not in sems:
                sems[name] = ctx.enter_context(nc.semaphore(name))
            return sems[name]

        def gate(eng):
            eng.nop().then_inc(S("gates"), 1)

        PS = ctx.enter_context(nc.psum_tensor("PS", [P, 8, 512], F32))

        def bank(b, *shape):
            v = PS[:, b, :]
            if len(shape) == 2:
                v = v.rearrange("p (a b) -> p a b", a=shape[0])
            if len(shape) == 3:
                v = v.rearrange("p (a b c) -> p a b c", a=shape[0], b=shape[1])
            return v

        h = sb("h", [P, NT, C])
        ring = sb("ring", [P, RING, KC, 512])
        ident = sb("ident", [P, P])
        ones = sb("ones", [P, P])
        gainT = sb("gainT", [P, 7, KC])
        sumsq = sb("sumsq", [P, NT])
        rms = sb("rms", [P, NT])
        rstd = sb("rstd", [P, NT])
        ARENA = 34 * 1024
        arena = sb("arena", [P, ARENA])

        def at(k1024, shape):
            n = 1
            for s in shape:
                n *= s
            o = int(k1024 * 1024)
            assert o + n <= ARENA, (o, n)
            return split(arena[:, o:o + n], shape)

        def split(v, shape):
            if len(shape) == 1:
                return v
            names = "abcd"[:len(shape)]
            return v.rearrange(f"p ({' '.join(names)}) -> p {' '.join(names)}",
                               **{names[j]: shape[j] for j in range(len(shape))})

        K_ = at(0, [KC, T])
        R_ = at(4, [KC, T])
        V_ = at(8, [KC, T])
        xT = at(12, [KC, T])
        dx = at(16, [KC, T])
        xm = [at(20, [KC, T]), at(24, [KC, T])]
        tn0 = at(24, [NT, C])
        KK = at(12, [KC, T])
        SG = at(16, [KC, T])
        AS = at(20, [KC, T])
        l1 = at(28, [KC, 256])
        w2s = at(30, [C])
        a2s = at(31, [C])
        g2s = at(32, [C])
        sg1 = at(33, [T])
        tw = at(33.5, [T])
        mixT = sb("mixT", [P, 6, KC])
        prow = sb("prow", [7 * KC, P])
        prm = sb("prm", [P, 7, KC])
        one_ka = sb("one_ka", [P, KC])
        hones = sb("hones", [P, P])
        masks = sb("masks", [P, 5, P])
        U16s, U64s, U64i, L16s, Loff = [masks[:, n, :] for n in range(5)]
        ident2 = sb("ident2", [P, HD])
        PC = sb("PC", [P, NCH])
        gn_eps = sb("gn_eps", [P, 1])

        hW = h[:, :, :].rearrange("p t c -> p (t c)")
        S_ = hW[:, 0:512]
        Pe = hW[:, 512:1024]
        Pp = hW[:, 1024:1536]
        Pi = hW[:, 1536:2048]
        Pf = hW[:, 2048:2560]
        bb = hW[:, 2560:3072]
        notfirst = hW[:, 3072:3584]
        ta = hW[:, 3584:4096]
        VTp = ta
        k2 = at(24, [T])
        AR = at(24.5, [2, T])
        B2 = at(26.5, [T])
        K2 = at(27, [T])
        RK = at(27.5, [T])
        Bt = at(28, [NT, P])
        Kt = at(28.5, [NT, P])
        Vp = at(29, [NT, P])
        Rpp = at(29.5, [T])
        GT = at(30, [NCH, P])
        Hs = at(31, [NCH, P])
        dPC = at(33.5, [NCH, HD])
        ringW = ring[:, :, :, :].rearrange("p r k n -> p (r k n)")
        BT = [at(25.5, [T]), ringW[:, 22 * 512:23 * 512]]
        KT = [at(26, [T]), ringW[:, 23 * 512:24 * 512]]

        def mat(slot, hh):
            o = (2 * slot + hh) * 512
            return split(ringW[:, o:o + 512], [NT, P])

        MdT, Md, Nf, RBT, RKT, WT, Q2, Q2T, Z, XT, RHS = [[mat(s, hh) for hh in range(2)] for s in range(11)]
        Q4, Q4T, Xm, X2T, Q8 = MdT, Md, WT, Q2, Q2T

        YT = at(0, [KC, T])
        Ysq = at(16, [KC, T])
        Ysd = at(20, [KC, T])
        mem_rows = at(26, [M // P, C])
        mem_tn = at(14, [M // P, C])
        mem_xT = at(24, [KC, M])
        memK = at(28, [KC, M])
        memV = at(30, [M // P, C])

        def src8(w):
            return w.rearrange("(p k) n -> p k n", k=KC)

        def srcn(w):
            return w.rearrange("(k p) n -> p k n", p=P)

        def unit_source(u):
            name = UNITS[u]
            i = u - UNITS.index(name)
            if name in ("wr", "wk", "wv"):
                w = src8(A["rw_" + name][0])
            elif name == "rwo":
                w = srcn(A["rw_wo"][0])
            elif name == "memkv":
                w = src8(A["xa_wkv"])
            elif name == "sqkv":
                w = src8(A["sb_wqkv"][0])
            elif name == "so":
                w = srcn(A["sb_wo"][0])
            elif name[:2] == "xq":
                w = src8(A["xa_wq"][int(name[2])])
            else:
                w = srcn(A["xa_wo"][int(name[2])])
            return w[:, :, 512 * i:512 * i + 512]

        def unit_last_group(u):
            name = UNITS[u]
            i = u - UNITS.index(name)
            if name == "memkv":
                return FIRST["memk"] + 4 * i + 3 if i < 2 else FIRST["memv"] + 2 * (i - 2) + 1
            if name == "sqkv":
                return FIRST["sq"] + 4 * i + 3
            return FIRST[name] + 4 * i + 3

        def load_units(sp, u0, u1):
            for u in range(u0, u1):
                if u >= RING:
                    sp.wait_ge(S("proj_filled"), unit_last_group(u - RING) + 1)
                sp.dma_start(ring[:, u % RING, :, :], unit_source(u)).then_inc(S(f"unit_in{u % RING}"), 16)

        def unit_arrived(eng, u):
            eng.wait_ge(S(f"unit_in{u % RING}"), 16 * (u // RING + 1))

        def ldnat(a):
            return a.rearrange("(j p) -> j p", p=P)

        def loads_first(sp):
            for t in range(NT):
                sp.dma_start(h[:, t, :], A["x"][0, P * t:P * t + P, :]).then_inc(S(f"x_in{t}"), 16)
            for n, g in enumerate([A["norm_mix"][0], A["norm_cross"][0], A["norm_ffn"][0], A["norm_mix"][1],
                                   A["norm_cross"][1], A["norm_ffn"][1], A["norm_mem"]]):
                sp.dma_start(gainT[:, n, :], g.rearrange("(p k) -> p k", k=KC)).then_inc(S("small_in"), 16)
            sp.dma_start(mixT[:, :, :], A["rw_mix"][0].rearrange("i (p k) -> p i k", k=KC)).then_inc(S("small_in"), 16)
            for n, g in enumerate([A["rw_w0"][0], A["rw_a0"][0], A["rw_kk"][0], A["rw_ka"][0]]):
                sp.dma_start(prow[8 * n:8 * n + 8, :], ldnat(g)).then_inc(S("small_in"), 16)
            sp.dma_start(prow[32:40, :], A["rw_rk"][0].rearrange("(j a) n -> j (a n)", a=2)).then_inc(S("small_in"), 16)
            for n, g in enumerate([A["rw_lnx_w"][0], A["rw_lnx_b"][0]]):
                sp.dma_start(prow[40 + 8 * n:48 + 8 * n, :], ldnat(g)).then_inc(S("small_in"), 16)
            sp.dma_start(l1[:, :, 0:64], src8(A["rw_w1"][0])).then_inc(S("small_in"), 16)
            sp.dma_start(l1[:, :, 64:128], src8(A["rw_a1"][0])).then_inc(S("small_in"), 16)
            sp.dma_start(l1[:, :, 128:256], src8(A["rw_g1"][0])).then_inc(S("small_in"), 16)
            sp.dma_start(w2s[0:HD, :], A["rw_w2"][0]).then_inc(S("small_in"), 16)
            sp.dma_start(a2s[0:HD, :], A["rw_a2"][0]).then_inc(S("small_in"), 16)
            sp.dma_start(g2s[:, :], A["rw_g2"][0]).then_inc(S("small_in"), 16)
        SMALL = 16 * (7 + 1 + 7 + 6)

        def loads_after_pairs(sp):
            sp.wait_ge(S("filled"), NPAIR * NFILL)
            for t in range(NT):
                sp.dma_start(h[:, t, :], A["x"][0, P * t:P * t + P, :]).then_inc(S("x_again"), 16)
            for m in range(M // P):
                sp.dma_start(mem_rows[:, m, :], A["mem"][0, P * m:P * m + P, :]).then_inc(S("mem_in"), 16)

        def bcast(v):
            return bass.AP(tensor=v.tensor, offset=v.offset, ap=[[0, P]] + [list(x) for x in v.ap])

        def constants(pool):
            n = [0]

            def sel(m, op, fill, base, pattern, cm, view=None):
                pool.wait_ge(S("const_step"), n[0])
                v = m if view is None else view
                pool.affine_select(out=v, in_=v, compare_op=op, fill=fill, base=base, pattern=pattern,
                                   channel_multiplier=cm).then_inc(S("const_step"), 1)
                n[0] += 1

            pool.memset(gn_eps[:, :], GN_EPS).then_inc(S("const_step"), 1)
            n[0] += 1
            for m, v in ((ident, 0.0), (ident2, 0.0), (ones, 1.0), (hones, 1.0), (U16s, 1.0), (U64s, 1.0),
                         (U64i, 1.0), (L16s, 1.0), (Loff, 1.0)):
                pool.memset(m[:, :], v).then_inc(S("const_step"), 1)
                n[0] += 1
            sel(ident[:, :], ALU.not_equal, 1.0, 0, [[-1, P]], 1)
            sel(ident2[:, :], ALU.not_equal, 1.0, 0, [[-1, HD]], 1)
            sel(ident2[:, :], ALU.not_equal, 1.0, -HD, [[-1, HD]], 1)

            def blocks(m, b):
                v = m[:, :].rearrange("p (a b) -> p a b", b=b)
                sel(v, ALU.is_ge, 0.0, 0, [[-b, P // b], [0, b]], 1)
                sel(v, ALU.is_ge, 0.0, b - 1, [[b, P // b], [0, b]], -1)

            blocks(hones, HD)
            blocks(U16s, 16)
            sel(U16s[:, :], ALU.is_gt, 0.0, 0, [[1, P]], -1)
            blocks(U64s, CH)
            sel(U64s[:, :], ALU.is_gt, 0.0, 0, [[1, P]], -1)
            blocks(U64i, CH)
            sel(U64i[:, :], ALU.is_ge, 0.0, 0, [[1, P]], -1)
            blocks(L16s, 16)
            sel(L16s[:, :], ALU.is_gt, 0.0, 0, [[-1, P]], 1)
            blocks(Loff, CH)
            sel(Loff[:, :], ALU.is_gt, 0.0, 0, [[-1, P]], 1)
            pool.wait_ge(S("const_step"), n[0])
            pool.tensor_tensor(Loff[:, :], Loff[:, :], L16s[:, :], ALU.subtract).then_inc(S("const_ready"), 1)

        NORMS = [("mix0", NT), ("mem", M // P), ("cross0", NT), ("ffn0", NT), ("mix1", NT), ("cross1", NT),
                 ("ffn1", NT), ("final", NT)]
        NIDX = {n: j for j, (n, _) in enumerate(NORMS)}
        TILE0 = {n: sum(c for _, c in NORMS[:j]) for j, (n, _) in enumerate(NORMS)}
        TPOSE0 = {n: KC * j for j, (n, _) in enumerate(NORMS)}
        GAIN = {"mix0": 0, "cross0": 1, "ffn0": 2, "mix1": 3, "cross1": 4, "ffn1": 5, "mem": 6}

        def norm_act(act, name, src, tn, tile_ready):
            nt = dict(NORMS)[name]
            for t in range(nt):
                tile_ready(act, t)
                act.activation(tn[:, t, :], src[:, t, :], ACT.Square, accum_out=sumsq[:, t:t + 1])\
                    .then_inc(S("norm_squares"), 1)
            act.wait_ge(S("norm_mean"), NIDX[name] + 1)
            act.activation(rms[:, 0:nt], rms[:, 0:nt], ACT.Sqrt).then_inc(S("norm_root"), 1)

        def norm_vec(vec, name, src, tn):
            nt = dict(NORMS)[name]
            vec.wait_ge(S("norm_squares"), TILE0[name] + nt)
            vec.tensor_scalar(rms[:, 0:nt], sumsq[:, 0:nt], 1.0 / C, EPS, ALU.mult, ALU.add)\
                .then_inc(S("norm_mean"), 1)
            vec.wait_ge(S("norm_root"), NIDX[name] + 1)
            vec.reciprocal(rstd[:, 0:nt], rms[:, 0:nt]).then_inc(S("norm_recip"), 1)
            vec.wait_ge(S("norm_recip"), NIDX[name] + 1)
            for t in range(nt):
                vec.tensor_scalar(tn[:, t, :], src[:, t, :], rstd[:, t:t + 1], None, ALU.mult)\
                    .then_inc(S("norm_rows"), 1)

        def norm_pe(pe, name, tn):
            nt = dict(NORMS)[name]
            for k in range(KC):
                n = TPOSE0[name] + k
                if n >= 2:
                    pe.wait_ge(S("xT_act" if n % 2 == 0 else "xT_vec"), n // 2)
                for t in range(nt):
                    if k == 0:
                        pe.wait_ge(S("norm_rows"), TILE0[name] + t + 1)
                    ins = pe.transpose(PS[:, 6 + n % 2, P * t:P * t + P], tn[:, t, k::KC], ident[:, :])
                ins.then_inc(S("norm_turned"), 1)

        def xT_evac(eng, name, dst, which):
            nt = dict(NORMS)[name]
            for k in range(which, KC, 2):
                n = TPOSE0[name] + k
                eng.wait_ge(S("norm_turned"), n + 1)
                g = gainT[:, GAIN[name], k:k + 1]
                if which == 0:
                    eng.activation(dst[:, k, 0:nt * P], PS[:, 6 + n % 2, 0:nt * P], ACT.Copy, scale=g)\
                        .then_inc(S("xT_act"), 1)
                else:
                    eng.tensor_scalar(dst[:, k, 0:nt * P], PS[:, 6 + n % 2, 0:nt * P], g, None, ALU.mult)\
                        .then_inc(S("xT_vec"), 1)

        def xT_there(eng, name, k):
            n = TPOSE0[name] + k
            eng.wait_ge(S("xT_act" if n % 2 == 0 else "xT_vec"), n // 2 + 1)

        def bank_free(pe, g):
            if g >= NBANK:
                pe.wait_ge(S("proj_out_" + OWNER[g - NBANK]), groups_done(g - NBANK))

        def group_out(eng, g):
            eng.wait_ge(S("proj_filled"), g + 1)
            return PS[:, g % NBANK, :]

        def group_evacuated(eng, g):
            eng.wait_ge(S("proj_out_" + OWNER[g]), groups_done(g))

        def project_T(pe, g0, u0, xt, n, ready, chunks=8):
            for j in range(chunks):
                g = g0 + j
                u = u0 + j // 4
                if j % 4 == 0:
                    unit_arrived(pe, u)
                bank_free(pe, g)
                for k in range(KC):
                    if j == 0:
                        ready(pe, k)
                    ins = pe.matmul(PS[:, g % NBANK, 0:n], ring[:, u % RING, k, P * (j % 4):P * (j % 4) + P],
                                    xt[:, k, 0:n], start=(k == 0), stop=(k == KC - 1))
                ins.then_inc(S("proj_filled"), 1)

        def project_tok(pe, g0, u0, xt, ready, tiles=NT):
            for half in range(2):
                unit_arrived(pe, u0 + half)
                for t in range(tiles):
                    g = g0 + tiles * half + t
                    bank_free(pe, g)
                    for k in range(KC):
                        if half == 0 and t == 0:
                            ready(pe, k)
                        ins = pe.matmul(PS[:, g % NBANK, :], xt[:, k, P * t:P * t + P],
                                        ring[:, (u0 + half) % RING, k, :], start=(k == 0), stop=(k == KC - 1))
                    ins.then_inc(S("proj_filled"), 1)

        def evac_T(act, g0, dst, n=T, chunks=8):
            for j in range(chunks):
                act.activation(dst[:, j, 0:n], group_out(act, g0 + j)[:, 0:n], ACT.Copy).then_inc(S("proj_out_A"), 1)

        def evac_tok(act, g0, dst, tiles=NT):
            for half in range(2):
                for t in range(tiles):
                    act.activation(dst[:, t, 512 * half:512 * half + 512], group_out(act, g0 + tiles * half + t),
                                   ACT.Copy).then_inc(S("proj_out_A"), 1)

        def add_to_h(vec, g0, ready=None):
            for half in range(2):
                for t in range(NT):
                    if ready and half == 0:
                        ready(vec, t)
                    v = h[:, t, 512 * half:512 * half + 512]
                    vec.tensor_tensor(v, v, group_out(vec, g0 + NT * half + t), ALU.add)\
                        .then_inc(S("proj_out_V"), 1)

        MIXES = [("w1", 1), ("a1", 4), ("g1", 5), ("wr", 0), ("wk", 2), ("wv", 3)]
        LORA_AT = {"w1": (0, 64), "a1": (64, 64), "g1": (128, 128)}

        def rwkv_mix_vec(vec):
            vec.wait_ge(S("small_in"), SMALL)
            for k in range(KC):
                xT_there(vec, "mix0", k)
            vec.tensor_tensor(dx[:, :, 1:T], xT[:, :, 0:T - 1], xT[:, :, 1:T], ALU.subtract).then_inc(S("dx_ready"), 1)
            vec.tensor_scalar(dx[:, :, 0:1], xT[:, :, 0:1], -1.0, None, ALU.mult).then_inc(S("dx_ready"), 1)
            vec.wait_ge(S("dx_ready"), 2)
            for n, (name, i) in enumerate(MIXES):
                if n >= 2:
                    before = MIXES[n - 2][0]
                    vec.wait_ge(S("proj_filled"), FIRST[before] + dict((a, b) for a, b, _ in PLAN)[before])
                for k in range(KC):
                    vec.scalar_tensor_tensor(out=xm[n % 2][:, k, :], in0=dx[:, k, :], scalar=mixT[:, i, k:k + 1],
                                             in1=xT[:, k, :], op0=ALU.mult, op1=ALU.add).then_inc(S("mixed"), 1)

        def rwkv_proj_pe(pe):
            pe.wait_ge(S("small_in"), SMALL)
            pe.transpose(PS[:, 5, 0:7 * KC], prow[:, :], ident[0:7 * KC, 0:7 * KC]).then_inc(S("prm_turned"), 1)
            for n, (name, _) in enumerate(MIXES):
                def ready(e, k, n=n):
                    e.wait_ge(S("mixed"), KC * n + k + 1)
                x_ = xm[n % 2]
                g = FIRST[name]
                if name in LORA_AT:
                    o, m = LORA_AT[name]
                    bank_free(pe, g)
                    for k in range(KC):
                        ready(pe, k)
                        ins = pe.matmul(PS[0:m, g % NBANK, :], l1[:, k, o:o + m], x_[:, k, :],
                                        start=(k == 0), stop=(k == KC - 1))
                    ins.then_inc(S("proj_filled"), 1)
                else:
                    project_T(pe, g, UNITS.index(name), x_, T, ready)

        def rwkv_proj_act(act):
            act.activation(tw[0:HD, :], group_out(act, FIRST["w1"])[0:HD, :], ACT.Tanh).then_inc(S("proj_out_A"), 1)
            act.activation(ta[0:HD, :], group_out(act, FIRST["a1"])[0:HD, :], ACT.Copy).then_inc(S("proj_out_A"), 1)
            act.activation(sg1[:, :], group_out(act, FIRST["g1"]), ACT.Sigmoid).then_inc(S("proj_out_A"), 1)
            evac_T(act, FIRST["wr"], R_)
            evac_T(act, FIRST["wk"], K_)
            evac_T(act, FIRST["wv"], V_)

        def prm_vec(vec):
            vec.wait_ge(S("prm_turned"), 1)
            vec.tensor_copy(prm[:, :, :], PS[:, 5, 0:7 * KC].rearrange("p (n j) -> p n j", n=7)).then_inc(S("prm_ready"), 1)
            vec.wait_ge(S("prm_ready"), 1)
            vec.tensor_scalar(one_ka[:, :], prm[:, 3, :], -1.0, 1.0, ALU.mult, ALU.add).then_inc(S("prm_ready"), 1)

        def rwkv_pre_pe(pe):
            group_evacuated(pe, FIRST["a1"])
            for j in range(KC):
                if j >= 2:
                    pe.wait_ge(S("pre_sig"), 2 * j - 2)
                else:
                    xT_there(pe, "mix0", 6 + j)
                    pe.wait_ge(S("prm_ready"), 1)
                pe.matmul(PS[:, 4 + 2 * (j % 2), :], w2s[0:HD, P * j:P * j + P], tw[0:HD, :], start=True, stop=True)
                pe.matmul(PS[:, 5 + 2 * (j % 2), :], a2s[0:HD, P * j:P * j + P], ta[0:HD, :], start=True, stop=True)\
                    .then_inc(S("pre_filled"), 1)
            pe.wait_ge(S("const_ready"), 1)
            for j in range(KC):
                pe.wait_ge(S("pre_sq"), j + 1)
                group_evacuated(pe, FIRST["wv"] + 7)
                if j >= 4:
                    pe.wait_ge(S("pre_norm"), j - 3)
                pe.matmul(PS[:, j % 4, :], hones[:, :], KK[:, j, :], start=True, stop=True).then_inc(S("pre_summed"), 1)

        def rwkv_pre_act(act):
            act.wait_ge(S("prm_ready"), 2)
            for j in range(KC):
                act.wait_ge(S("pre_filled"), j + 1)
                act.activation(SG[:, j, :], PS[:, 4 + 2 * (j % 2), :], ACT.Sigmoid, bias=prm[:, 0, j:j + 1])\
                    .then_inc(S("pre_sig"), 1)
                act.activation(AS[:, j, :], PS[:, 5 + 2 * (j % 2), :], ACT.Sigmoid, bias=prm[:, 1, j:j + 1])\
                    .then_inc(S("pre_sig"), 1)
            for j in range(KC):
                group_evacuated(act, FIRST["wk"] + j)
                act.activation(KK[:, j, :], K_[:, j, :], ACT.Square, scale=prm[:, 2, j:j + 1]).then_inc(S("pre_sq"), 1)
            act.wait_ge(S("pre_norm"), KC)
            act.activation(KK[:, :, :], KK[:, :, :], ACT.Sqrt).then_inc(S("pre_root"), 1)

        def rwkv_pre_vec(vec):
            for j in range(KC):
                vec.wait_ge(S("pre_summed"), j + 1)
                vec.tensor_scalar(KK[:, j, :], PS[:, j % 4, :], 1e-24, None, ALU.max).then_inc(S("pre_norm"), 1)
            vec.wait_ge(S("pre_root"), 1)
            vec.reciprocal(KK[:, :, :], KK[:, :, :]).then_inc(S("pre_recip"), 1)
            vec.wait_ge(S("pre_recip"), 1)
            for j in range(KC):
                vec.scalar_tensor_tensor(out=KK[:, j, :], in0=K_[:, j, :], scalar=prm[:, 2, j:j + 1],
                                         in1=KK[:, j, :], op0=ALU.mult, op1=ALU.mult).then_inc(S("kk_ready"), 1)
            vec.memset(notfirst, 1.0).then_inc(S("notfirst_ready"), 1)
            vec.wait_ge(S("notfirst_ready"), 1)
            vec.memset(split(notfirst, [NCH, CH])[:, :, 0:1], 0.0).then_inc(S("notfirst_ready"), 1)
            vec.wait_ge(S("notfirst_ready"), 2)

        NP2 = 6
        TK_FILLED = FILL_NO["TK", 1] + 1

        def half(hh):
            return slice(HD * hh, HD * hh + HD)

        def pair_pool(pool):
            pool.wait_ge(S("proj_filled"), FIRST["wv"] + 8)
            pool.wait_ge(S("pre_filled"), KC)
            for hh in range(2):
                if hh:
                    pool.wait_ge(S("zeros_ready"), 2)
                pool.memset(BT[hh][half(1 - hh), :], 0.0).then_inc(S("zeros_ready"), 1)
                pool.memset(KT[hh][half(1 - hh), :], 0.0).then_inc(S("zeros_ready"), 1)
            pool.wait_ge(S("zeros_ready"), 4)
            pool.memset(GT, 0.0).then_inc(S("zeros_ready"), 1)
            pool.memset(Hs, 0.0).then_inc(S("zeros_ready"), 1)

            def prepare(j, first=False):
                if not first:
                    pool.wait_ge(S("p2_ready"), NP2 * j)
                    pool.wait_ge(S("b2_ready"), 2 * j)
                pool.tensor_tensor(bb, KK[:, j, :], AS[:, j, :], ALU.mult).then_inc(S("b_ready"), 1)
                pool.wait_ge(S("k2_step"), j + 1)
                pool.tensor_tensor(k2, k2, K_[:, j, :], ALU.mult).then_inc(S("k2_ready"), 1)
                if not first:
                    pool.wait_ge(S("filled"), (j - 1) * NFILL + TK_FILLED)
                pool.tensor_copy(VTp, V_[:, j, :]).then_inc(S("vt_ready"), 1)
                pool.wait_ge(S("pe_ready"), 2 * j + 2)
                pool.wait_ge(S("b_ready"), j + 1)
                pool.tensor_tensor(B2, bb, Pe, ALU.mult).then_inc(S("b2_ready"), 1)
                pool.wait_ge(S("k2_ready"), j + 1)
                pool.tensor_tensor(K2, k2, Pe, ALU.mult).then_inc(S("b2_ready"), 1)

            pool.wait_ge(S("kk_ready"), KC)
            prepare(0, True)
            with pool.Fori(1, NPAIR) as j:
                prepare(j)

        def parity(m, q, hh):
            return m.rearrange("p (t q) d -> p t q d", q=2)[half(hh), :, q, half(hh)]

        RHS4 = ringW[:, 20 * 512:22 * 512].rearrange("p (a t n) -> p a t n", a=2, t=NT)

        def next_prepared(eng, body):
            with eng.Fori(0, NPAIR - 1) as i:
                body(i, i + 1)
            body(NPAIR - 1, None)

        def pair_act(act):
            def prepare(j, first=False):
                if not first:
                    act.wait_ge(S("p2_ready"), NP2 * j)
                    act.wait_ge(S("b2_ready"), 2 * j)
                act.activation(k2, AS[:, j, :], ACT.Identity, bias=one_ka[:, bass.ds(j, 1)],
                               scale=prm[:, 3, bass.ds(j, 1)]).then_inc(S("k2_step"), 1)
                if not first:
                    act.wait_ge(S("r_ready"), j)
                act.wait_ge(S("sum_ready"), 3 * j + 1)
                act.activation(Pf, S_, ACT.Exp, scale=-DECAY_C).then_inc(S("pf_ready"), 1)
                act.activation(Pi, S_, ACT.Exp, scale=DECAY_C).then_inc(S("pi_ready"), 1)
                if not first:
                    act.wait_ge(S("dpc_ready"), j)
                act.activation(PC[:, :], split(S_, [NCH, CH])[:, :, CH - 1], ACT.Exp, scale=-DECAY_C)\
                    .then_inc(S("pc_ready"), 1)
                act.wait_ge(S("sum_ready"), 3 * j + 2)
                act.activation(Pp, Pp, ACT.Exp, scale=-DECAY_C).then_inc(S("pe_ready"), 1)
                act.wait_ge(S("sum_ready"), 3 * j + 3)
                act.activation(Pe, Pe, ACT.Exp, scale=DECAY_C).then_inc(S("pe_ready"), 1)

            def body(i, following):
                def evac(step, hh, dst, src, last=True):
                    n = FILL_NO[step, hh]
                    act.wait_ge(S("filled"), i * NFILL + n + 1)
                    ins = act.activation(dst, src, ACT.Copy)
                    if last:
                        ins.then_inc(S("evac_A"), 1)

                for n, (step, hh, e) in enumerate(FILLS):
                    if e != "A":
                        continue
                    b = bank_of(n)
                    if step == "TA":
                        evac(step, hh, RHS4[:, :, :, 0:HD], bank(b, NT, 2, HD).rearrange("p t a d -> p a t d"))
                    elif step == "WV":
                        evac(step, hh, RHS[hh][:, :, HD:P],
                             bank(b, NT, 2, HD)[:, :, hh, :])
                    elif step == "Y":
                        evac(step, hh, K_[:, i, :], PS[:, b, :])
                    elif step == "H":
                        for a in range(2):
                            evac(step, hh, parity(Hs, hh, a), bank(b, NT, P)[half(a), :, 0:HD], last=(a == 1))
                    else:
                        dst = {"TB": Bt, "TK": Kt, "TV": Vp}.get(step)
                        if dst is None:
                            dst = {"Q2": Q2, "Q2T": Q2T, "Q4": Q4, "Q4T": Q4T, "Q8": Q8, "X": Xm, "X2T": X2T}[step][hh]
                        evac(step, hh, dst, bank(b, NT, P))
                    if step == "TK" and following is not None:
                        prepare(following)

            act.wait_ge(S("kk_ready"), KC)
            act.wait_ge(S("zeros_ready"), NZERO)
            prepare(0, True)
            next_prepared(act, body)
        NZERO = 6

        def pair_vec(vec):
            mask = {"A": (U16s, U64i), "B": (U64s, U64i), "C": (L16s, Loff)}

            def over(m, n):
                return m[:, :].unsqueeze(1).to_broadcast([P, n, P])

            def sums(j, first=False):
                if not first:
                    vec.wait_ge(S("pc_ready"), j)
                    vec.wait_ge(S("pe_ready"), 2 * j)
                    vec.wait_ge(S("b2_ready"), 2 * j)
                    vec.wait_ge(S("p2_ready"), NP2 * j)
                vec.tensor_tensor_scan(S_, notfirst, SG[:, j, :], 0.0, ALU.mult, ALU.add).then_inc(S("sum_ready"), 1)
                vec.wait_ge(S("sum_ready"), 3 * j + 1)
                vec.tensor_tensor(Pp, S_, SG[:, j, :], ALU.subtract).then_inc(S("sum_ready"), 1)
                s3 = split(S_, [NCH, CH])
                vec.tensor_tensor(split(Pe, [NCH, CH]), s3, s3[:, :, CH - 1:CH].to_broadcast([P, NCH, CH]),
                                  ALU.subtract).then_inc(S("sum_ready"), 1)

            def factors(j):
                vec.wait_ge(S("k2_ready"), j + 1)
                vec.wait_ge(S("pi_ready"), j + 1)
                for hh in range(2):
                    r = half(hh)
                    vec.tensor_tensor(KT[hh][r, :], k2[r, :], Pi[r, :], ALU.mult).then_inc(S("p2_ready"), 1)
                    vec.tensor_tensor(BT[hh][r, :], bb[r, :], Pi[r, :], ALU.mult).then_inc(S("p2_ready"), 1)
                vec.wait_ge(S("pe_ready"), 2 * j + 1)
                vec.scalar_tensor_tensor(out=AR[:, 0, :], in0=KK[:, j, :], scalar=-1.0, in1=Pp,
                                         op0=ALU.mult, op1=ALU.mult).then_inc(S("p2_ready"), 1)
                vec.scalar_tensor_tensor(out=RK, in0=R_[:, j, :], scalar=prm[:, 4, bass.ds(j, 1)], in1=k2,
                                         op0=ALU.mult, op1=ALU.mult).then_inc(S("p2_ready"), 1)

            def late_factors(j):
                vec.wait_ge(S("pf_ready"), j + 1)
                vec.tensor_tensor(AR[:, 1, :], R_[:, j, :], Pf, ALU.mult).then_inc(S("r_ready"), 1)
                vec.wait_ge(S("pc_ready"), j + 1)
                vec.tensor_tensor(dPC, ident2[:, :].unsqueeze(1).to_broadcast([P, NCH, HD]),
                                  PC[:, :].unsqueeze(2).to_broadcast([P, NCH, HD]), ALU.mult).then_inc(S("dpc_ready"), 1)

            def body(i, following):
                own = i * NEV["V"]
                if following is not None:
                    sums(following)
                for n, (step, hh, e) in enumerate(FILLS):
                    if e != "V":
                        continue
                    b = bank_of(n)
                    vec.wait_ge(S("filled"), i * NFILL + n + 1)

                    def add(dst, src, old):
                        vec.tensor_tensor(dst, src, old, ALU.add).then_inc(S("evac_V"), 1)

                    def masked(dst, src, m, nt):
                        return vec.tensor_tensor(dst, src, over(m, nt), ALU.mult)

                    if step == "BN":
                        vec.tensor_tensor(V_[:, i, :], V_[:, i, :], PS[:, b, :], ALU.mult).then_inc(S("evac_V"), 1)
                    elif step in ("A0", "A1", "B0", "B1"):
                        q = 2 * int(step[1])
                        left, right = (MdT, RBT) if step[0] == "A" else (WT, RKT)
                        ps = bank(b, 2, 2, P)
                        masked(left[hh][:, q:q + 2, :], ps[:, :, 0, :], mask[step[0]][0], 2)
                        masked(right[hh][:, q:q + 2, :], ps[:, :, 1, :], mask[step[0]][1], 2).then_inc(S("evac_V"), 1)
                    elif step == "CC":
                        masked(Md[hh], bank(b, NT, P), L16s, NT)
                        masked(Nf[hh], bank(b, NT, P), Loff, NT).then_inc(S("evac_V"), 1)
                        vec.wait_ge(S("evac_V"), own + evacs(n))
                        vec.tensor_tensor(Z[hh], MdT[hh], over(ident, NT), ALU.add).then_inc(S("z_begun"), 1)
                    elif step in ("Z2", "Z3", "Z4"):
                        if step == "Z2":
                            vec.wait_ge(S("z_begun"), 2 * i + hh + 1)
                        add(Z[hh], bank(b, NT, P), Z[hh])
                    elif step == "XT":
                        vec.tensor_copy(XT[hh], bank(b, NT, P)).then_inc(S("evac_V"), 1)
                    elif step == "R1":
                        vec.tensor_copy(RHS[hh], bank(b, NT, P)).then_inc(S("evac_V"), 1)
                    elif step in ("R2", "R3"):
                        add(RHS[hh], bank(b, NT, P), RHS[hh])
                    elif step == "RP":
                        add(Rpp, PS[:, b, :], AR[:, 1, :])
                    elif step == "G":
                        for a in range(2):
                            ins = vec.tensor_tensor(parity(GT, hh, a), bank(b, NT, P)[half(a), :, 0:HD],
                                                    dPC.rearrange("p (t q) d -> p t q d", q=2)[half(a), :, hh, :],
                                                    ALU.add)
                        ins.then_inc(S("evac_V"), 1)
                    else:
                        c = int(step[1:])
                        vec.wait_ge(S("evac_A"), i * NEV["A"] + evacs(FILL_NO["H", 1]))
                        add(Hs[:, c, :], PS[:, b, 0:P], Hs[:, c, :])
                    if (step, hh) == ("B1", 1) and following is not None:
                        factors(following)
                if following is not None:
                    late_factors(following)

            vec.wait_ge(S("zeros_ready"), NZERO)
            sums(0, True)
            factors(0)
            late_factors(0)
            next_prepared(vec, body)

        def pair_pe(pe):
            pe.wait_ge(S("kk_ready"), KC)
            pe.wait_ge(S("zeros_ready"), NZERO)
            pe.nop().then_inc(S("banks_clear"), 1)
            with pe.Fori(0, NPAIR) as i:
                def fill(step, hh):
                    n = FILL_NO[step, hh]
                    m = bank_before(n)
                    need = [FILL_NO[d] for d in NEEDS.get(step, lambda hh: [])(hh)] + ([m] if m is not None else [])
                    for e in "AV":
                        last = [evacs(m) for m in need if FILLS[m][2] == e]
                        if last:
                            pe.wait_ge(S("evac_" + e), i * NEV[e] + max(last))
                    return bank_of(n)

                def mm4(b, lhs, rhs):
                    for t in range(NT):
                        ins = pe.matmul(PS[:, b, P * t:P * t + P], lhs[:, t, :], rhs[:, t, :], start=True, stop=True)
                    ins.then_inc(S("filled"), 1)

                pe.wait_ge(S("banks_clear"), i + 1)
                yb = bank_of(FILL_NO["Y", 1])
                AT = split(AR[:, 0, :], [NT, P])
                products = {"Q2": (MdT, Md), "Q2T": (Md, MdT), "WV": (WT, [Vp, Vp]), "Q4": (Q2T, Q2),
                            "Q4T": (Q2, Q2T), "Z2": (Q2, Z), "Q8": (Q4T, Q4), "Z3": (Q4, Z), "Z4": (Q8, Z),
                            "X": (Z, Nf), "XT": (Nf, Z), "R1": (Z, RHS), "X2T": (Xm, XT), "R2": (X2T, RHS),
                            "R3": (XT, RHS), "CC": ([AT, AT], [split(m, [NT, P]) for m in BT])}

                def y_local(t):
                    o = slice(P * t, P * t + P)
                    for a in range(2):
                        pe.matmul(PS[half(a), yb, o], RHS[a][:, t, HD:P], RBT[a][:, t, :], start=(t == 0), stop=False,
                                  skip_group_check=True)
                    for a in range(2):
                        pe.matmul(PS[half(a), yb, o], Vp[:, t, half(a)], RKT[a][:, t, :], start=False, stop=False,
                                  skip_group_check=True)

                for n, (step, hh, e) in enumerate(FILLS):
                    if step == "S1":
                        fill("Y", 1)
                    b = fill(step, hh)
                    if step in ("TA", "TB", "TK", "TV"):
                        src = {"TA": AR[:, 0, :], "TB": B2, "TK": K2, "TV": VTp}[step]
                        if step == "TA":
                            pe.wait_ge(S("p2_ready"), NP2 * i + NP2)
                        if step == "TV":
                            pe.wait_ge(S("vt_ready"), i + 1)
                        if step == "TB":
                            pe.wait_ge(S("b2_ready"), 2 * i + 2)
                        for t in range(NT):
                            ins = pe.transpose(PS[:, b, P * t:P * t + P], src[:, P * t:P * t + P], ident[:, :])
                        ins.then_inc(S("filled"), 1)
                    elif step == "BN":
                        pe.matmul(PS[:, b, :], hones[:, :], RK, start=True, stop=True).then_inc(S("filled"), 1)
                    elif step in ("A0", "A1", "B0", "B1"):
                        if step == "A0":
                            pe.wait_ge(S("r_ready"), i + 1)
                        lhs = (BT if step[0] == "A" else KT)[hh]
                        for q in range(2):
                            t = 2 * int(step[1]) + q
                            ins = pe.matmul(bank(b, 2, 2, P)[:, q, :, :], lhs[:, P * t:P * t + P],
                                            AR[:, :, P * t:P * t + P], start=True, stop=True)
                        ins.then_inc(S("filled"), 1)
                    elif step in products:
                        if step == "Q4":
                            pe.wait_ge(S("z_begun"), 2 * i + hh + 1)
                        mm4(b, products[step][0][hh], products[step][1][hh])
                    elif step == "RP":
                        for t in range(NT):
                            for a in range(2):
                                ins = pe.matmul(PS[half(a), b, P * t:P * t + P], RHS[a][:, t, 0:HD],
                                                RBT[a][:, t, :], start=True, stop=True)
                        ins.then_inc(S("filled"), 1)
                    elif step in ("G", "H"):
                        if step == "G":
                            pe.wait_ge(S("dpc_ready"), i + 1)
                        gate(pe)
                        r = slice(CH * hh, CH * hh + CH)
                        for t in range(NT):
                            for a in range(2):
                                o = PS[half(a), b, P * t:P * t + HD]
                                if step == "G":
                                    ins = pe.matmul(o, RHS[a][r, t, 0:HD], Bt[r, t, half(a)], start=True, stop=True)
                                else:
                                    pe.matmul(o, Bt[r, t, half(a)], RHS[a][r, t, HD:P], start=True, stop=False)
                                    ins = pe.matmul(o, Kt[r, t, half(a)], Vp[r, t, half(a)], start=False, stop=True)
                        ins.then_inc(S("filled"), 1)
                    elif step[0] == "S":
                        c = int(step[1:])
                        pe.matmul(PS[:, b, 0:P], GT[:, c, :], Hs[:, c - 1, :], start=True, stop=True)\
                            .then_inc(S("filled"), 1)
                        if c <= NT:
                            y_local(c - 1)
                    elif step == "Y":
                        for c in range(1, NCH):
                            if c == 1:
                                pe.wait_ge(S("evac_V"), i * NEV["V"] + evacs(FILL_NO["RP", 0]))
                            if c == NCH - 1:
                                pe.wait_ge(S("evac_V"), i * NEV["V"] + evacs(FILL_NO[f"S{NCH - 2}", 0]))
                            ins = pe.matmul(PS[:, yb, CH * c:CH * c + CH], Hs[:, c - 1, :], Rpp[:, CH * c:CH * c + CH],
                                            start=False, stop=(c == NCH - 1), skip_group_check=True)
                        ins.then_inc(S("filled"), 1)
                pe.wait_ge(S("evac_A"), i * NEV["A"] + NEV["A"])
                pe.nop().then_inc(S("banks_clear"), 1)

        GPRE = FIRST["gate"]

        def gn_pe(pe):
            pe.wait_ge(S("evac_A"), NPAIR * NEV["A"])
            pe.wait_ge(S("evac_V"), NPAIR * NEV["V"])
            for j in range(KC):
                if j >= 2:
                    pe.wait_ge(S("gn_centred"), j - 1)
                pe.matmul(PS[:, 4 + j % 2, :], hones[:, :], YT[:, j, :], start=True, stop=True).then_inc(S("gn_summed"), 1)
            for j in range(KC):
                pe.wait_ge(S("gn_squared"), j + 1)
                if j >= 2:
                    pe.wait_ge(S("gn_root"), j - 1)
                else:
                    pe.wait_ge(S("gn_centred"), KC - 1 + j)
                pe.matmul(PS[:, 4 + j % 2, :], hones[:, :], Ysq[:, j, :], start=True, stop=True).then_inc(S("gn_summed"), 1)

        def gn_act(act):
            for j in range(KC):
                act.wait_ge(S("gn_centred"), j + 1)
                act.activation(Ysq[:, j, :], YT[:, j, :], ACT.Square).then_inc(S("gn_squared"), 1)

            for j in range(KC):
                act.wait_ge(S("gn_summed"), KC + j + 1)
                act.activation(Ysd[:, j, :], PS[:, 4 + j % 2, :], ACT.Sqrt, scale=1.0 / HD, bias=gn_eps[:, :])\
                    .then_inc(S("gn_root"), 1)

        def gn_vec(vec):
            for j in range(KC):
                vec.wait_ge(S("gn_summed"), j + 1)
                vec.scalar_tensor_tensor(out=YT[:, j, :], in0=PS[:, 4 + j % 2, :], scalar=-1.0 / HD, in1=YT[:, j, :],
                                         op0=ALU.mult, op1=ALU.add).then_inc(S("gn_centred"), 1)

        def post_vec(vec):
            st = S("post_step")
            for j in range(KC):
                vec.wait_ge(S("gn_root"), j + 1)
                vec.reciprocal(Ysd[:, j, :], Ysd[:, j, :]).then_inc(S("gn_recip"), 1)
            for j in range(KC):
                vec.wait_ge(S("gn_recip"), j + 1)
                vec.tensor_tensor(YT[:, j, :], YT[:, j, :], Ysd[:, j, :], ALU.mult).then_inc(st, 1)
            for j in range(KC):
                vec.wait_ge(st, j + 1)
                vec.tensor_scalar(YT[:, j, :], YT[:, j, :], prm[:, 5, j:j + 1], prm[:, 6, j:j + 1],
                                  ALU.mult, ALU.add).then_inc(st, 1)
            for j in range(KC):
                vec.wait_ge(st, KC + j + 1)
                vec.tensor_tensor(YT[:, j, :], YT[:, j, :], V_[:, j, :], ALU.add).then_inc(st, 1)
            for j in range(KC):
                vec.wait_ge(st, 2 * KC + j + 1)
                vec.tensor_tensor(YT[:, j, :], YT[:, j, :], group_out(vec, GPRE + j), ALU.mult)\
                    .then_inc(S("proj_out_V"), 1)

        def post_pe(pe):
            for j in range(KC):
                bank_free(pe, GPRE + j)
                pe.matmul(PS[:, (GPRE + j) % NBANK, :], g2s[:, P * j:P * j + P], sg1[:, :], start=True, stop=True)\
                    .then_inc(S("proj_filled"), 1)

            project_tok(pe, FIRST["rwo"], UNITS.index("rwo"), YT, lambda e, k: group_evacuated(e, GPRE + k))

        def x_back(vec, t):
            vec.wait_ge(S("x_again"), 16 * NT)


        def mem_pe(pe):
            norm_pe(pe, "mem", mem_tn)

            def ready(e, k):
                xT_there(e, "mem", k)
            u = UNITS.index("memkv")
            project_T(pe, FIRST["memk"], u, mem_xT, M, ready)
            project_tok(pe, FIRST["memv"], u + 2, mem_xT, lambda e, k: None, tiles=M // P)

        def mem_act(act):
            act.wait_ge(S("filled"), NPAIR * NFILL)
            norm_act(act, "mem", mem_rows, mem_tn, lambda e, t: e.wait_ge(S("mem_in"), 16 * (M // P)))
            xT_evac(act, "mem", mem_xT, 0)
            evac_T(act, FIRST["memk"], memK, n=M)
            evac_tok(act, FIRST["memv"], memV, tiles=M // P)

        def mem_vec(vec):
            norm_vec(vec, "mem", mem_rows, mem_tn)
            xT_evac(vec, "mem", mem_xT, 1)

        tnX = at(12, [NT, C])
        xTX = at(16, [KC, T])
        qT = at(20, [KC, T])
        oT = at(24, [KC, T])
        prob = [at(12 + x, [NT, M]) for x in range(2)]
        probT = [at(14 + x, [M // P, T]) for x in range(2)]
        xmax, xsum = sb("xmax", [P, 2, NT]), sb("xsum", [P, 2, NT])

        def h_tile_ready(name):
            return lambda e, t: group_evacuated(e, FIRST[name] + NT + t)

        def cross_pe(pe, l):
            xq, xv, xo = f"xq{l}", f"xv{l}", f"xo{l}"
            norm_pe(pe, f"cross{l}", tnX)
            project_T(pe, FIRST[xq], UNITS.index(xq), xTX, T, lambda e, k: xT_there(e, f"cross{l}", k))

            def scores(x):
                n = XH * l + x
                group_evacuated(pe, FIRST[xq] + 2 * x + 1)
                for b in range(2):
                    if n >= 1:
                        pe.wait_ge(S("x_exp"), NT * (n - 1) + 2 * b + 2)
                    for t in (2 * b, 2 * b + 1):
                        for k in range(2):
                            ins = pe.matmul(PS[:, 4 + b, M * (t % 2):M * (t % 2) + M],
                                            qT[:, 2 * x + k, P * t:P * t + P], memK[:, 2 * x + k, :],
                                            start=(k == 0), stop=(k == 1))
                    ins.then_inc(S("x_scored"), 1)

            scores(0)
            for x in range(XH):
                n = XH * l + x
                if x + 1 < XH:
                    scores(x + 1)
                for m in range(2):
                    if n >= 1:
                        pe.wait_ge(S("x_probT"), 2 * (n - 1) + m + 1)
                    if x == 0:
                        xT_there(pe, f"cross{l}", 6 + m)
                    for t in range(NT):
                        pe.wait_ge(S("x_prob"), NT * n + t + 1)
                        ins = pe.transpose(PS[:, 6 + m, P * t:P * t + P], prob[x % 2][:, t, P * m:P * m + P],
                                           ident[:, :])
                    ins.then_inc(S("x_turned"), 1)
                pe.wait_ge(S("x_probT"), 2 * n + 2)
                for v in range(2):
                    g = FIRST[xv] + 2 * x + v
                    bank_free(pe, g)
                    for m in range(2):
                        ins = pe.matmul(PS[:, g % NBANK, :], memV[:, m, XD * x + P * v:XD * x + P * v + P],
                                        probT[x % 2][:, m, :], start=(m == 0), stop=(m == 1))
                    ins.then_inc(S("proj_filled"), 1)
            project_tok(pe, FIRST[xo], UNITS.index(xo), oT, lambda e, k: group_evacuated(e, FIRST[xv] + k))

        def cross_act(act, l, before):
            norm_act(act, f"cross{l}", h, tnX, h_tile_ready(before))
            xT_evac(act, f"cross{l}", xTX, 0)
            evac_T(act, FIRST[f"xq{l}"], qT)

            def out(x):
                for v in range(2):
                    act.activation(oT[:, 2 * x + v, :], group_out(act, FIRST[f"xv{l}"] + 2 * x + v), ACT.Copy)\
                        .then_inc(S("proj_out_A"), 1)

            for x in range(XH):
                n = XH * l + x
                if x == 0:
                    act.wait_ge(S("norm_turned"), TPOSE0[f"cross{l}"] + KC)
                if x >= 2:
                    act.wait_ge(S("x_turned"), 2 * (n - 1))
                for t in range(NT):
                    act.wait_ge(S("x_nmax"), 2 * n + t // 2 + 1)
                    act.activation(prob[x % 2][:, t, :], PS[:, 4 + t // 2, M * (t % 2):M * (t % 2) + M], ACT.Exp,
                                   bias=xmax[:, x % 2, t:t + 1], scale=XSCALE,
                                   accum_out=xsum[:, x % 2, t:t + 1]).then_inc(S("x_exp"), 1)
                if x >= 1:
                    out(x - 1)
            out(XH - 1)

        def cross_vec(vec, l):
            norm_vec(vec, f"cross{l}", h, tnX)
            xT_evac(vec, f"cross{l}", xTX, 1)

            def maxima(x):
                n = XH * l + x
                if x >= 2:
                    vec.wait_ge(S("x_exp"), NT * (n - 1))
                for b in range(2):
                    vec.wait_ge(S("x_scored"), 2 * n + b + 1)
                    m = xmax[:, x % 2, 2 * b:2 * b + 2]
                    vec.tensor_reduce(m, bank(4 + b, 2, M), AX.X, ALU.max).then_inc(S("x_max"), 1)
                    vec.wait_ge(S("x_max"), 2 * n + b + 1)
                    vec.tensor_scalar(m, m, -XSCALE, None, ALU.mult).then_inc(S("x_nmax"), 1)

            maxima(0)
            for x in range(XH):
                n = XH * l + x
                if x + 1 < XH:
                    maxima(x + 1)
                vec.wait_ge(S("x_exp"), NT * n + NT)
                vec.reciprocal(xsum[:, x % 2, :], xsum[:, x % 2, :]).then_inc(S("x_recip"), 1)
                vec.wait_ge(S("x_recip"), n + 1)
                for t in range(NT):
                    vec.tensor_scalar(prob[x % 2][:, t, :], prob[x % 2][:, t, :], xsum[:, x % 2, t:t + 1], None,
                                      ALU.mult).then_inc(S("x_prob"), 1)
                for m in range(2):
                    vec.wait_ge(S("x_turned"), 2 * n + m + 1)
                    if x >= 2:
                        vec.wait_ge(S("proj_filled"), FIRST[f"xv{l}"] + 2 * (x - 1))
                    vec.tensor_copy(probT[x % 2][:, m, :], PS[:, 6 + m, :]).then_inc(S("x_probT"), 1)
            add_to_h(vec, FIRST[f"xo{l}"])

        tnS = at(0, [NT, C])
        oTS = at(0, [KC, T])
        xTS = at(4, [KC, T])
        qTS = at(8, [KC, T])
        kTS = at(12, [KC, T])
        vS = at(16, [NT, C])
        fail = [at(20 + 0.625 * b, [T + 8]) for b in range(2)]
        beta = [at(21.5 + 0.5 * b, [T]) for b in range(2)]
        attT = [at(22.5 + 2 * a, [NT, T]) for a in range(2)]
        qs, ks, vs = at(32, [T]), at(32.5, [T]), at(33, [NT, P])
        NU = 2 * NT

        def sb_proj_pe(pe):
            norm_pe(pe, "mix1", tnS)
            project_T(pe, FIRST["sq"], UNITS.index("sqkv"), xTS, T, lambda e, k: xT_there(e, "mix1", k))
            project_T(pe, FIRST["sk"], UNITS.index("sqkv") + 2, xTS, T, lambda e, k: None)
            project_tok(pe, FIRST["sv"], UNITS.index("sqkv") + 4, xTS, lambda e, k: None)

        def sb_proj_act(act):
            norm_act(act, "mix1", h, tnS, lambda e, t: e.wait_ge(S("h_moe0"), t + 1))
            xT_evac(act, "mix1", xTS, 0)
            evac_T(act, FIRST["sq"], qTS)
            evac_T(act, FIRST["sk"], kTS)
            evac_tok(act, FIRST["sv"], vS)

        def sb_pool(pool):
            group_evacuated(pool, FIRST["sv"] + 7)
            with pool.Fori(0, NPAIR) as i:
                pool.wait_ge(S("sb_out_done"), i + 1)
                pool.tensor_copy(qs, qTS[:, i, :]).then_inc(S("sb_copied"), 1)
                pool.tensor_copy(ks, kTS[:, i, :]).then_inc(S("sb_copied"), 1)
                pool.tensor_copy(vs, vS.rearrange("p t (i n) -> p t i n", i=NPAIR)[:, :, i, :]).then_inc(S("sb_copied"), 1)
                for n in range(NU):
                    nn = P * (n % NT + 1)
                    pool.wait_ge(S("sb_sig"), 2 * (NU * i + n) + 1)
                    gate(pool)
                    f = fail[n % 2][:, T - P:T]
                    pool.affine_select(out=f, in_=f, compare_op=ALU.is_gt, fill=1.0, base=0, pattern=[[-1, P]],
                                       channel_multiplier=1).then_inc(S("sb_cut"), 1)
                    pool.wait_ge(S("sb_sig"), 2 * (NU * i + n) + 2)
                    gate(pool)
                    b = beta[n % 2][:, nn - P:nn]
                    pool.affine_select(out=b, in_=b, compare_op=ALU.is_gt, fill=0.0, base=0, pattern=[[-1, P]],
                                       channel_multiplier=1).then_inc(S("sb_cut"), 1)

        def sb_act(act):
            with act.Fori(0, NPAIR) as i:
                for n in range(NU):
                    nn = P * (n % NT + 1)
                    act.wait_ge(S("sb_scored"), NU * i + n + 1)
                    act.wait_ge(S("sb_turned"), NU * i + n + 1)
                    act.activation(fail[n % 2][:, T - nn:T], PS[:, n % NT, 0:nn], ACT.Sigmoid, scale=-HD ** -0.5)\
                        .then_inc(S("sb_sig"), 1)
                    act.activation(beta[n % 2][:, 0:nn], PS[:, n % NT, 0:nn], ACT.Sigmoid, scale=HD ** -0.5)\
                        .then_inc(S("sb_sig"), 1)
                    if n == NT + 1 or n == NU - 1:
                        hh = int(n == NU - 1)
                        r = slice(HD * hh, HD * hh + HD)
                        act.wait_ge(S("sb_summed"), 2 * i + hh + 1 + 2)
                        act.activation(oTS[r, i, :], PS[r, 6 + hh, :], ACT.Copy).then_inc(S("sb_oT"), 1)

        def sb_vec(vec):
            vec.wait_ge(S("norm_turned"), TPOSE0["mix1"] + KC)
            for b in range(2):
                vec.memset(fail[b][:, T:T + 1], 1.0).then_inc(S("sb_ones"), 1)
            vec.wait_ge(S("sb_ones"), 2)
            with vec.Fori(0, NPAIR) as i:
                for n in range(NU):
                    nn = P * (n % NT + 1)
                    t, hh = n % NT, n // NT
                    f, b = fail[n % 2], beta[n % 2]
                    vec.wait_ge(S("sb_cut"), 2 * (NU * i + n) + 2)
                    rev = f[:, T - nn:T][:, ::-1]
                    vec.tensor_tensor_scan(rev, rev, rev, 1.0, ALU.mult, ALU.min).then_inc(S("sb_scan"), 1)
                    vec.wait_ge(S("sb_scan"), NU * i + n + 1)
                    vec.tensor_tensor(b[:, 0:nn], b[:, 0:nn], f[:, T - nn + 1:T + 1], ALU.mult).then_inc(S("sb_att"), 1)
                    if n >= 1:
                        sb_turn_out(vec, i, n - 1)
                sb_turn_out(vec, i, NU - 1)

        def sb_turn_out(vec, i, n):
            t, hh = n % NT, n // NT
            vec.wait_ge(S("sb_turned"), NU * i + n + 1 + 2)
            vec.wait_ge(S("sb_summed"), 2 * i + hh + 1)
            vec.tensor_copy(attT[hh][:, 0:t + 1, P * t:P * t + P], bank(4 + n % 2, NT, P)[:, 0:t + 1, :])\
                .then_inc(S("sb_attT"), 1)

        def sb_pe(pe):
            group_evacuated(pe, FIRST["sv"] + 7)
            pe.nop().then_inc(S("sb_turned"), 2)
            pe.nop().then_inc(S("sb_summed"), 2)
            pe.nop().then_inc(S("sb_out_done"), 1)
            with pe.Fori(0, NPAIR) as i:
                def score(n):
                    t, r = n % NT, slice(HD * (n // NT), HD * (n // NT) + HD)
                    if n >= NT:
                        pe.wait_ge(S("sb_sig"), 2 * (NU * i + n - NT) + 2)
                    pe.matmul(PS[:, t, 0:P * (t + 1)], qs[r, P * t:P * t + P], ks[r, 0:P * (t + 1)],
                              start=True, stop=True).then_inc(S("sb_scored"), 1)

                pe.wait_ge(S("sb_copied"), 3 * i + 3)
                for n in range(NT):
                    score(n)
                for n in range(NU):
                    t, hh = n % NT, n // NT
                    pe.wait_ge(S("sb_att"), NU * i + n + 1)
                    if n >= 2:
                        pe.wait_ge(S("sb_attT"), NU * i + n - 1)
                    for s in range(t + 1):
                        ins = pe.transpose(PS[:, 4 + n % 2, P * s:P * s + P], beta[n % 2][:, P * s:P * s + P],
                                           ident[:, :])
                    ins.then_inc(S("sb_turned"), 1)
                    if n + NT < NU:
                        score(n + NT)
                    if t == NT - 1:
                        pe.wait_ge(S("sb_attT"), NU * i + n + 1)
                        gate(pe)
                        r = slice(HD * hh, HD * hh + HD)
                        for s in range(NT):
                            ins = pe.matmul(PS[r, 6 + hh, P * s:T], vs[:, s, r], attT[hh][:, s, P * s:T],
                                            start=(s == 0), stop=(s == NT - 1))
                        ins.then_inc(S("sb_summed"), 1)
                pe.wait_ge(S("sb_oT"), 2 * i + 2)
                pe.nop().then_inc(S("sb_out_done"), 1)
            project_tok(pe, FIRST["so"], UNITS.index("so"), oTS, lambda e, k: None)

        tnE = at(12, [NT, C])
        xTE = at(16, [KC, T])
        ringS = ring[:, :, :, :].rearrange("p r k n -> p (r k n)")

        def slot(p, a):
            return arena[:, 6144 * a:6144 * a + 6144] if p == 0 else ringS[:, 6144 * a:6144 * a + 6144]

        w13 = [[split(slot(p, a)[:, 0:4096], [2, KC, F]) for a in range(2)] for p in range(2)]
        w2e = [[split(slot(p, a)[:, 4096:6144], [2, C]) for a in range(2)] for p in range(2)]
        xg = [at(20 + p, [C]) for p in range(2)]
        xgT = [at(22 + p, [KC, P]) for p in range(2)]
        ye = [at(24 + p, [C]) for p in range(2)]
        sig = at(27, [F])
        hid = at(27.25, [F])
        hidT = at(27.5, [2, P])
        yg = [at(12 + n, [C]) for n in range(8)]
        wge = at(26.25, [KC, G + NE])
        bge = at(26.75, [G + NE])
        su = masks[:, 0, :]
        lg = at(27, [NT, G + NE])
        mel = at(27.25, [NT, NE])
        mel2 = at(27.375, [NT, NE])
        O1 = at(27.5, [NT, NE])
        O2 = at(27.625, [NT, NE])
        OO = at(27.75, [NT, NE])
        sc = at(27.875, [NT, NE])
        rk = at(32, [NT + 1, NE])
        cmp_ = at(32.25, [NT * NE * 7])
        qq = at(33.125, [NT, NE])
        bm = at(33.25, [NT, NE])
        sm = at(33.375, [NT, NE])
        tmp = at(33.5, [NT, NE])
        cm = at(33.625, [NT, NE])
        OS = [at(33.75 + 0.125 * n, [P]) for n in range(2)]
        OB = [at(26.875 + 0.03125 * n, [32]) for n in range(2)]
        iob = hones[:, :]
        w32 = masks[:, 1, 64:96]
        e2 = masks[:, 1, 96:128]
        ov = masks[:, 2, 0:96].rearrange("p (a e) -> p a e", a=3)
        thr = masks[:, 2, 96:103]
        eh = masks[:, 4, 0:32]
        ep = masks[:, 4, 32:64]
        tokid = masks[:, 2, 104:108]
        c4 = masks[:, 3, 0:48].rearrange("p (n t) -> p n t", n=12)
        gmax, gsum, v1, v2, s1, ed, den, wA, wB = [c4[:, n, :] for n in range(9)]
        bs = masks[:, 4, 64:88].rearrange("p (n t) -> p n t", n=6)
        overf = masks[:, 3, 64:96]
        pos = sb("pos", [P, NT, 2], I32)
        NPE = NE // 2
        NCOL = NPE + NOVER
        table = sb("table", [P, NCOL], I32)
        over = sb("over", [P, 32], I32)
        xi = [sb(f"xi{a}", [P, 1], I32) for a in range(2)]
        NSTEP = 76

        def moe_constants(pool):
            pool.wait_ge(S("gn_root"), KC)
            pool.iota(iob, [[1, P]], base=0, channel_multiplier=0,
                      allow_small_or_imprecise_dtypes=True).then_inc(S("iota_ready"), 1)
            pool.iota(w32[:, :], [[-1, NE]], base=NE, channel_multiplier=0,
                      allow_small_or_imprecise_dtypes=True).then_inc(S("iota_ready"), 1)
            pool.iota(thr[:, :], [[BLK, 7]], base=BLK, channel_multiplier=0,
                      allow_small_or_imprecise_dtypes=True).then_inc(S("iota_ready"), 1)
            for m, pattern in ((e2, [[2, NPE], [0, 2]]), (eh, [[1, NPE], [0, 2]]), (ep, [[0, NPE], [BLK, 2]])):
                pool.iota(m.rearrange("p (a b) -> p a b", b=2), pattern, base=0, channel_multiplier=0,
                          allow_small_or_imprecise_dtypes=True).then_inc(S("iota_ready"), 1)
            pool.iota(tokid[:, :], [[P, NT]], base=0, channel_multiplier=1,
                      allow_small_or_imprecise_dtypes=True).then_inc(S("iota_ready"), 1)

            pool.memset(su[:, :], 1.0).then_inc(S("iota_ready"), 1)
            pool.wait_ge(S("iota_ready"), 8)
            pool.affine_select(out=su[:, :], in_=su[:, :], compare_op=ALU.is_gt, fill=0.0, base=0, pattern=[[1, P]],
                               channel_multiplier=-1).then_inc(S("iota_ready"), 1)

        def experts(w, l, k):
            return w[l].rearrange("g e (p k) f -> (g e) p k f", k=k)

        def moe_route_loads(sp, l):
            sp.wait_ge(S("proj_filled"), FIRST[f"xo{l}"] + 8)
            sp.dma_start(wge[:, :, 0:G], A["moe_wg"][l].rearrange("(p k) n -> p k n", k=KC)).then_inc(S("route_in"), 16)
            sp.dma_start(wge[:, :, G:], A["moe_we"][l].rearrange("(p k) n -> p k n", k=KC)).then_inc(S("route_in"), 16)
            sp.dma_start(bge[:, 0:G], bcast(A["moe_bg"][l])).then_inc(S("route_in"), 16)
            sp.dma_start(bge[:, G:], bcast(A["moe_be"][l])).then_inc(S("route_in"), 16)

        def moe_route_pe(pe, l):
            norm_pe(pe, f"ffn{l}", tnE)
            for k in range(KC):
                xT_there(pe, f"ffn{l}", k)
            pe.wait_ge(S("route_in"), 64 * (l + 1))
            for t in range(NT):
                for k in range(KC):
                    ins = pe.matmul(PS[:, 5, 64 * t:64 * t + G + NE], xTE[:, k, P * t:P * t + P], wge[:, k, :],
                                    start=(k == 0), stop=(k == KC - 1))
            ins.then_inc(S("logits"), 1)
            pe.wait_ge(S("chosen"), l + 1)
            pe.wait_ge(S("iota_ready"), 9)
            for t in range(NT + 1):
                for s in range(min(t, NT - 1) + 1):
                    ins = pe.matmul(PS[:, 4, NE * t:NE * t + NE], su[:, :] if s == t else ones[:, :], OO[:, s, :],
                                    start=(s == 0), stop=(s == min(t, NT - 1)))
            ins.then_inc(S("ranked"), 1)
            for n in range(8):
                pe.wait_ge(S("onehots"), 2 * (8 * l + n) + 2)
                pe.matmul(PS[:, 5, 0:NCOL], OS[n % 2], OB[n % 2][:, 0:NCOL], start=(n == 0), stop=(n == 7))\
                    .then_inc(S("tabled"), 1)

        def moe_route_act(act, l):
            norm_act(act, f"ffn{l}", h, tnE, h_tile_ready(f"xo{l}"))
            xT_evac(act, f"ffn{l}", xTE, 0)
            act.wait_ge(S("route_a"), 2 * l + 1)
            act.activation(sc[:, :, 0:G], mel2[:, :, 0:G], ACT.Exp).then_inc(S("route_exp"), 1)
            act.wait_ge(S("route_a"), 2 * l + 2)
            act.activation(ed, ed, ACT.Exp).then_inc(S("route_exp"), 1)

        def moe_route_vec(vec, l):
            norm_vec(vec, f"ffn{l}", h, tnE)
            xT_evac(vec, f"ffn{l}", xTE, 1)
            step = S("route_step")
            n = [l * 10000]
            done = [ROUTE_STEPS * l]

            def do(ins):
                ins.then_inc(step, 1)
                done[0] += 1
                vec.wait_ge(step, done[0])

            def wide(m, k):
                return m.unsqueeze(2).to_broadcast([P, NT, k])

            vec.wait_ge(S("iota_ready"), 9)
            vec.wait_ge(S("logits"), l + 1)
            do(vec.tensor_tensor(lg, PS[:, 5, 0:256].rearrange("p (t n) -> p t n", t=NT)[:, :, 0:G + NE],
                                 bge.unsqueeze(1).to_broadcast([P, NT, G + NE]), ALU.add))
            gl, el = lg[:, :, 0:G], lg[:, :, G:]
            do(vec.tensor_reduce(gmax, gl, AX.X, ALU.max))
            vec.tensor_tensor(mel2[:, :, 0:G], gl, wide(gmax, G), ALU.subtract).then_inc(S("route_a"), 1)
            do(vec.tensor_tensor(mel[:, :, 0:G], gl, wide(gmax, G), ALU.is_equal))
            do(vec.tensor_tensor(mel[:, :, 0:G], mel[:, :, 0:G], w32[:, 0:G].unsqueeze(1).to_broadcast([P, NT, G]),
                                 ALU.mult))
            do(vec.tensor_reduce(s1, mel[:, :, 0:G], AX.X, ALU.max))
            do(vec.tensor_tensor(mel[:, :, 0:G], mel[:, :, 0:G], wide(s1, G), ALU.is_equal))
            vec.wait_ge(S("route_exp"), 2 * l + 1)
            do(vec.tensor_reduce(gsum, sc[:, :, 0:G], AX.X, ALU.add))
            do(vec.tensor_scalar(tmp[:, :, 0:G], mel[:, :, 0:G], -1.0, BIG, ALU.add, ALU.mult))
            for t in range(NT):
                ins = vec.tensor_tensor(mel[:, t, :].rearrange("p (g e) -> p g e", g=G),
                                        el[:, t, :].rearrange("p (g e) -> p g e", g=G),
                                        tmp[:, t, 0:G].unsqueeze(2).to_broadcast([P, G, E]), ALU.add)
                if t == NT - 1:
                    do(ins)
            for O, v, m in ((O1, v1, mel), (O2, v2, mel2)):
                do(vec.tensor_reduce(v, m, AX.X, ALU.max))
                do(vec.tensor_tensor(O, m, wide(v, NE), ALU.is_equal))
                do(vec.tensor_tensor(O, O, w32[:, :].unsqueeze(1).to_broadcast([P, NT, NE]), ALU.mult))
                do(vec.tensor_reduce(s1, O, AX.X, ALU.max))
                do(vec.tensor_tensor(O, O, wide(s1, NE), ALU.is_equal))
                if O is O1:
                    do(vec.scalar_tensor_tensor(out=mel2, in0=O1, scalar=-2 * BIG, in1=mel, op0=ALU.mult, op1=ALU.add))
            vec.tensor_tensor(OO, O1, O2, ALU.add).then_inc(S("chosen"), 1)
            vec.tensor_tensor(ed, v2, v1, ALU.subtract).then_inc(S("route_a"), 1)
            vec.wait_ge(S("ranked"), l + 1)
            do(vec.tensor_copy(rk, PS[:, 4, 0:(NT + 1) * NE].rearrange("p (t e) -> p t e", t=NT + 1)))
            rank, count = rk[:, 0:NT, :].rearrange("p t e -> p (t e)"), rk[:, NT, :]
            c3 = cmp_.rearrange("p (a b) -> p a b", b=7)
            th = thr[:, :].unsqueeze(1)
            do(vec.tensor_tensor(c3[:, 0:NE, :], count.unsqueeze(2).to_broadcast([P, NE, 7]),
                                 th.to_broadcast([P, NE, 7]), ALU.is_gt))
            do(vec.tensor_reduce(ov[:, 0, :], c3[:, 0:NE, :], AX.X, ALU.add))
            do(vec.tensor_tensor_scan(ov[:, 1, :], ones[:, 0:NE], ov[:, 0, :], 0.0, ALU.mult, ALU.add))
            do(vec.tensor_tensor(ov[:, 2, :], ov[:, 1, :], ov[:, 0, :], ALU.subtract))
            do(vec.tensor_scalar(ov[:, 2, :], ov[:, 2, :], float(NE - 1), None, ALU.add))
            c4_ = cmp_[:, 0:16 * NE].rearrange("p (a b) -> p a b", b=NE)
            do(vec.tensor_tensor(c4_, ov[:, 1, :].unsqueeze(1).to_broadcast([P, 16, NE]),
                                 iob[:, 0:16].unsqueeze(2).to_broadcast([P, 16, NE]), ALU.is_le))
            do(vec.tensor_reduce(overf[:, 0:16], c4_, AX.X, ALU.add))
            do(vec.tensor_scalar(overf[:, 0:16], overf[:, 0:16], float(NE - 1), None, ALU.min))
            do(vec.tensor_copy(overf[:, 16:17], ov[:, 1, NE - 1:NE]))
            vec.tensor_copy(over[:, 0:17], overf[:, 0:17]).then_inc(S("over_known"), 1)
            do(vec.tensor_tensor(c3, rank.unsqueeze(2).to_broadcast([P, NT * NE, 7]),
                                 th.to_broadcast([P, NT * NE, 7]), ALU.is_ge))
            do(vec.tensor_reduce(qq.rearrange("p t e -> p (t e)"), c3, AX.X, ALU.add))
            def by_expert(m):
                return m.unsqueeze(1).to_broadcast([P, NT, NE])

            do(vec.scalar_tensor_tensor(out=sm, in0=qq, scalar=-float(BLK), in1=rk[:, 0:NT, :], op0=ALU.mult, op1=ALU.add))
            do(vec.tensor_tensor(bm, qq, by_expert(ov[:, 2, :]), ALU.add))
            do(vec.tensor_scalar(qq, qq, 0.0, None, ALU.is_gt))
            do(vec.tensor_scalar(cm, bm, -float(NPE), None, ALU.add))
            for m, first in ((bm, e2), (cm, eh)):
                do(vec.tensor_tensor(m, m, by_expert(first), ALU.subtract))
                do(vec.tensor_tensor(m, m, qq, ALU.mult))
                do(vec.tensor_tensor(m, m, by_expert(first), ALU.add))
            do(vec.tensor_scalar(qq, qq, -1.0, 1.0, ALU.mult, ALU.add))
            do(vec.tensor_tensor(qq, qq, by_expert(ep), ALU.mult))
            do(vec.tensor_tensor(sm, sm, qq, ALU.add))
            for k, O in enumerate((O1, O2)):
                for j, m in enumerate((bm, sm, cm)):
                    do(vec.tensor_tensor(tmp, O, m, ALU.mult))
                    do(vec.tensor_reduce(bs[:, 2 * j + k, :], tmp, AX.X, ALU.add))
            if l:
                vec.wait_ge(S("yg_in3"), 32)
            do(vec.scalar_tensor_tensor(out=c4[:, 9:11, :], in0=bs[:, 0:2, :], scalar=float(BLK), in1=bs[:, 2:4, :],
                                        op0=ALU.mult, op1=ALU.add))
            vec.tensor_copy(pos[:, :, :].rearrange("p t k -> p k t"), c4[:, 9:11, :]).then_inc(S("pos_known"), 1)
            for m in range(8):
                k, t = m // NT, m % NT
                if m >= 2:
                    vec.wait_ge(S("tabled"), 8 * l + m - 1)
                vec.tensor_scalar(OS[m % 2], iob, bs[:, 2 + k, t:t + 1], None, ALU.is_equal)\
                    .then_inc(S("onehots"), 1)
                vec.tensor_scalar(OB[m % 2], iob[:, 0:32], bs[:, 4 + k, t:t + 1], tokid[:, t:t + 1], ALU.is_equal, ALU.mult)\
                    .then_inc(S("onehots"), 1)
            vec.wait_ge(S("tabled"), 8 * l + 8)
            vec.tensor_copy(table[:, :], PS[:, 5, 0:NCOL]).then_inc(S("table_ready"), 1)
            vec.wait_ge(S("route_exp"), 2 * l + 2)
            do(vec.tensor_scalar(den, ed, 1.0, None, ALU.add))
            do(vec.tensor_tensor(den, den, gsum, ALU.mult))
            do(vec.reciprocal(wA, den))
            do(vec.tensor_tensor(wB, wA, ed, ALU.mult))
            assert done[0] == ROUTE_STEPS * (l + 1), done[0] - ROUTE_STEPS * l
        ROUTE_STEPS = 62

        def moe_rows_out(sp, l):
            for t in range(NT):
                sp.wait_ge(S("norm_rows"), TILE0[f"ffn{l}"] + t + 1)
                sp.dma_start(scratch["rows"][P * t:P * t + P, :], tnE[:, t, :]).then_inc(S("rows_out"), 16)

        def load_up(sp, l, e, w, sem):
            sp.dma_start(w[:, 0, :, :], experts(A["moe_w1"], l, KC)[e]).then_inc(sem, 16)
            sp.dma_start(w[:, 1, :, :], experts(A["moe_w3"], l, KC)[e]).then_inc(sem, 16)

        def load_down(sp, l, e, w, sem):
            sp.dma_start(w, experts(A["moe_w2"], l, 2)[e]).then_inc(sem, 16)

        def load_pair(sp, l, n, p):
            for a in range(2):
                load_up(sp, l, 2 * n + a, w13[p][a], S(f"w13_in{p}"))
            for a in range(2):
                load_down(sp, l, 2 * n + a, w2e[p][a], S(f"w2_in{p}"))

        def moe_first_loads(sp, l):
            sp.wait_ge(S("proj_filled"), FIRST["so" if l else "rwo"] + 8)
            load_pair(sp, l, 0, 0)

        def moe_loads(sp, l):
            sp.wait_ge(S("proj_filled"), FIRST[f"xo{l}"] + 8)
            load_pair(sp, l, 1, 1)
            with sp.Fori(1, NPE // 2) as j:
                for p in range(2):
                    sp.wait_ge(S("up_done"), NPE * l + 2 * j + p - 1)
                    for a in range(2):
                        load_up(sp, l, 4 * j + 2 * p + a, w13[p][a], S(f"w13_in{p}"))
                    sp.wait_ge(S("down_done"), NPE * l + 2 * j + p - 1)
                    for a in range(2):
                        load_down(sp, l, 4 * j + 2 * p + a, w2e[p][a], S(f"w2_in{p}"))

        def gather(pool, p, rows):
            return pool.indirect_dma_start(out=xg[p][0:rows, :], out_offset=None, in_=scratch["rows"],
                                           in_offset=bass.IndirectOffsetOnAxis(ap=xi[p][0:rows, 0:1], axis=0))

        def moe_pool(pool, l):
            pool.wait_ge(S("table_ready"), l + 1)
            pool.wait_ge(S("rows_out"), 16 * NT * (l + 1))
            with pool.Fori(0, NPE // 2) as j:
                for p in range(2):
                    pool.wait_ge(S(f"xg_free{p}"), (NPE // 2 + 1) * l + j + 1)
                    pool.tensor_copy(xi[p][:, :], table[:, bass.ds(2 * j + p, 1)]).then_inc(S(f"xi_ready{p}"), 1)
                    pool.wait_ge(S(f"xi_ready{p}"), NPE // 2 * l + j + 1)
                    gate(pool)
                    gather(pool, p, P).then_inc(S(f"xg_in{p}"), 16)

        def moe_combine_pool(pool, l):
            pool.wait_ge(S("pos_known"), l + 1)
            for p in range(2):
                pool.wait_ge(S(f"ye_out{p}"), 16 * (NPE // 2 + 1) * (l + 1))
            pool.wait_ge(S("over_done"), l + 1)
            pool.wait_ge(S("spare_filled"), 32)
            for t in range(NT):
                for k in range(2):
                    pool.indirect_dma_start(out=yg[2 * t + k], out_offset=None, in_=scratch["blocks"],
                                            in_offset=bass.IndirectOffsetOnAxis(ap=pos[:, t, k:k + 1], axis=0))\
                        .then_inc(S(f"yg_in{t}"), 16)

        def moe_combine_vec(vec, l):
            for t in range(NT):
                vec.wait_ge(S(f"yg_in{t}"), 32 * (l + 1))
                for k, w in enumerate((wA, wB)):
                    if k:
                        vec.wait_ge(S("h_half"), NT * l + t + 1)
                    vec.scalar_tensor_tensor(out=h[:, t, :], in0=yg[2 * t + k], scalar=w[:, t:t + 1], in1=h[:, t, :],
                                             op0=ALU.mult, op1=ALU.add)\
                        .then_inc(S("h_half") if k == 0 else S(f"h_moe{l}"), 1)

        def turn_rows(pe, p, rows):
            for k in range(KC):
                ins = pe.transpose(bank(k // 4, 4, P)[:, k % 4, 0:rows], xg[p][0:rows, k::KC], ident[0:rows, 0:rows])
            return ins

        def xgT_out(vec, l, p, rows):
            for b in range(2):
                ins = vec.tensor_tensor(xgT[p][:, 4 * b:4 * b + 4, 0:rows], bank(b, 4, P)[:, :, 0:rows],
                                        gainT[:, GAIN[f"ffn{l}"], 4 * b:4 * b + 4].unsqueeze(2)
                                        .to_broadcast([P, 4, rows]), ALU.mult)
            return ins

        def up(pe, p, n):
            for k in range(KC):
                for a in range(n):
                    r = slice(BLK * a, BLK * a + BLK)
                    ins = pe.matmul(bank(2, 2, F)[r, :, :], xgT[p][:, k, r], w13[p][a][:, :, k, :],
                                    start=(k == 0), stop=(k == KC - 1))
            return ins

        def sig_out(act, rows):
            return act.activation(sig[0:rows, :], PS[0:rows, 2, 0:F], ACT.Sigmoid)

        def silu_half(vec, rows):
            return vec.tensor_tensor(hid[0:rows, :], PS[0:rows, 2, 0:F], sig[0:rows, :], ALU.mult)

        def hid_out(vec, rows):
            return vec.tensor_tensor(hid[0:rows, :], PS[0:rows, 2, F:2 * F], hid[0:rows, :], ALU.mult)

        def turn_hid(pe, rows):
            for k in range(2):
                ins = pe.transpose(PS[:, 4, P * k:P * k + rows], hid[0:rows, k::2], ident[0:rows, 0:rows])
            return ins

        def hidT_out(act, rows):
            return act.activation(hidT[:, :, 0:rows], bank(4, 4, P)[:, 0:2, 0:rows], ACT.Copy)

        def down(pe, p, n, half):
            for k in range(2):
                for a in range(n):
                    r = slice(BLK * a, BLK * a + BLK)
                    ins = pe.matmul(PS[r, 6 + half, :], hidT[:, k, r],
                                    w2e[p][a][:, k, 512 * half:512 * half + 512], start=(k == 0), stop=(k == 1))
            return ins

        def ye_half(p, rows, half):
            return ye[p][0:rows, 512 * half:512 * half + 512], PS[0:rows, 6 + half, :]

        def last_peeled(eng, body):
            with eng.Fori(0, NPE // 2 - 1) as j:
                for p in range(2):
                    body(j, p, False)
            body(NPE // 2 - 1, 0, False)
            body(NPE // 2 - 1, 1, True)

        def moe_pe(pe, l):
            def turn(j, p):
                pe.wait_ge(S(f"xg_in{p}"), 16 * (NPE // 2 * l + j + 1))
                gate(pe)
                turn_rows(pe, p, P).then_inc(S(f"xg_free{p}"), 1)

            def body(j, p, last):
                n = NPE * l + 2 * j + p
                pe.wait_ge(S("xgT_ready"), n + 1)
                pe.wait_ge(S(f"w13_in{p}"), 64 * (NPE // 2 * l + j + 1))
                gate(pe)
                up(pe, p, 2).then_inc(S("up_done"), 1)
                if not last:
                    turn(j + p, 1 - p)
                pe.wait_ge(S("hid_ready"), n + 1)
                gate(pe)
                turn_hid(pe, P).then_inc(S("hid_turned"), 1)
                pe.wait_ge(S(f"w2_in{p}"), 32 * (NPE // 2 * l + j + 1))
                pe.wait_ge(S("hidT_ready"), n + 1)
                pe.wait_ge(S("ye_a"), n + l + 1)
                gate(pe)
                down(pe, p, 2, 0).then_inc(S("down_half"), 1)
                pe.wait_ge(S("ye_v"), n + l + 1)
                gate(pe)
                down(pe, p, 2, 1).then_inc(S("down_done"), 1)

            pe.wait_ge(S("table_ready"), l + 1)
            for p in range(2):
                pe.nop().then_inc(S(f"xg_free{p}"), 1)
            turn(0, 0)
            last_peeled(pe, body)

        def moe_act(act, l):
            def body(j, p, last):
                n = NPE * l + 2 * j + p
                act.wait_ge(S("up_done"), n + 1)
                sig_out(act, P).then_inc(S("sig_ready"), 1)
                act.wait_ge(S("hid_turned"), n + 1)
                hidT_out(act, P).then_inc(S("hidT_ready"), 1)
                act.wait_ge(S("down_half"), n + 1)
                act.wait_ge(S(f"ye_out{p}"), 16 * (NPE // 2 * l + l + j + 1))
                d, s = ye_half(p, P, 0)
                act.activation(d, s, ACT.Copy).then_inc(S("ye_a"), 1)
                act.wait_ge(S("ye_v"), n + l + 2)
                act.wait_ge(S("ye_a"), n + l + 2)
                act.dma_start(scratch["blocks"][0:NE * BLK, :].rearrange("(b r) c -> b r c", r=P)[2 * j + p], ye[p])\
                    .then_inc(S(f"ye_out{p}"), 16)

            act.wait_ge(S("table_ready"), l + 1)
            act.nop().then_inc(S("ye_a"), 1)
            for p in range(2):
                act.nop().then_inc(S(f"ye_out{p}"), 16)
            last_peeled(act, body)

        def moe_vec(vec, l):
            def turned(j, p):
                vec.wait_ge(S(f"xg_free{p}"), (NPE // 2 + 1) * l + j + 2)
                xgT_out(vec, l, p, P).then_inc(S("xgT_ready"), 1)

            def body(j, p, last):
                n = NPE * l + 2 * j + p
                vec.wait_ge(S("sig_ready"), n + 1)
                silu_half(vec, P).then_inc(S("silu_ready"), 1)
                vec.wait_ge(S("silu_ready"), n + 1)
                hid_out(vec, P).then_inc(S("hid_ready"), 1)
                if not last:
                    turned(j + p, 1 - p)
                vec.wait_ge(S("down_done"), n + 1)
                vec.wait_ge(S(f"ye_out{p}"), 16 * (NPE // 2 * l + l + j + 1))
                d, s = ye_half(p, P, 1)
                vec.tensor_copy(d, s).then_inc(S("ye_v"), 1)

            vec.nop().then_inc(S("ye_v"), 1)
            turned(0, 0)
            last_peeled(vec, body)

        def further(eng, l, body):
            eng.wait_ge(S("over_known"), l + 1)
            n = eng.value_load(over[0:1, 16:17], min_val=0, max_val=NOVER)
            with eng.Fori(0, NOVER) as j:
                with eng.If(j < n):
                    body(j, lambda k: eng.wait_ge(S(f"over_step{l}"), j * NSTEP + k))

        def further_pool(pool, l):
            st = S(f"over_step{l}")

            def body(j, at_step):
                at_step(1)
                pool.tensor_copy(xi[0][:, :], table[:, bass.ds(NPE + j, 1)]).then_inc(st, 1)
                at_step(2)
                gate(pool)
                gather(pool, 0, BLK).then_inc(S(f"over_gathered{l}"), 16)
            further(pool, l, body)

        def further_sp(sp, l):
            st = S(f"over_step{l}")
            for p in range(2):
                sp.wait_ge(S(f"ye_out{p}"), 16 * (NPE // 2 + 1) * (l + 1))
            sp.nop().then_inc(st, 1)

            def body(j, at_step):
                e = sp.value_load(over[0:1, bass.ds(j, 1)], min_val=0, max_val=NE - 1)
                at_step(2)
                load_up(sp, l, e, w13[0][0], st)
                load_down(sp, l, e, w2e[0][0], st)
                at_step(61)
                sp.dma_start(scratch["blocks"].rearrange("(b r) c -> b r c", r=BLK)[NE + j], ye[0][0:BLK, :])\
                    .then_inc(st, 16)
                at_step(77)
                gate(sp)
            further(sp, l, body)
            sp.nop().then_inc(S("over_done"), 1)

        def further_pe(pe, l):
            st = S(f"over_step{l}")

            def step(at_step, k):
                at_step(k)
                gate(pe)

            def body(j, at_step):
                pe.wait_ge(S(f"over_gathered{l}"), 16 * (j + 1))
                step(at_step, 50)
                turn_rows(pe, 0, BLK).then_inc(st, 1)
                step(at_step, 52)
                up(pe, 0, 1).then_inc(st, 1)
                step(at_step, 56)
                turn_hid(pe, BLK).then_inc(st, 1)
                step(at_step, 58)
                down(pe, 0, 1, 0)
                down(pe, 0, 1, 1).then_inc(st, 1)
            further(pe, l, body)

        def further_act(act, l):
            st = S(f"over_step{l}")

            def body(j, at_step):
                at_step(53)
                sig_out(act, BLK).then_inc(st, 1)
                at_step(57)
                hidT_out(act, BLK).then_inc(st, 1)
                at_step(59)
                d, s = ye_half(0, BLK, 0)
                act.activation(d, s, ACT.Copy).then_inc(st, 1)
            further(act, l, body)

        def further_vec(vec, l):
            st = S(f"over_step{l}")

            def body(j, at_step):
                at_step(51)
                xgT_out(vec, l, 0, BLK).then_inc(st, 1)
                at_step(54)
                silu_half(vec, BLK).then_inc(st, 1)
                at_step(55)
                hid_out(vec, BLK).then_inc(st, 1)
                at_step(60)
                d, s = ye_half(0, BLK, 1)
                vec.tensor_copy(d, s).then_inc(st, 1)
            further(vec, l, body)

        tnF = at(0, [NT, C])
        gF = at(4, [C])

        def final_act(act):
            norm_act(act, "final", h, tnF, lambda e, t: e.wait_ge(S("h_moe1"), t + 1))

        def final_vec(vec):
            norm_vec(vec, "final", h, tnF)
            vec.wait_ge(S("final_gain_in"), 16)
            for t in range(NT):
                vec.wait_ge(S("norm_rows"), TILE0["final"] + t + 1)
                vec.tensor_tensor(tnF[:, t, :], tnF[:, t, :], gF, ALU.mult).then_inc(S("result"), 1)

        def final_sp(sp):
            sp.wait_ge(S("over_done"), 2)
            sp.dma_start(gF, bcast(A["norm_final"])).then_inc(S("final_gain_in"), 16)
            for t in range(NT):
                sp.wait_ge(S("result"), t + 1)
                sp.dma_start(out[0, P * t:P * t + P, :], tnF[:, t, :]).then_inc(S("result_out"), 16)
            sp.wait_ge(S("result_out"), 16 * NT)

        block = ctx.enter_context(nc.Block())

        def at_unit(name):
            return UNITS.index(name)

        @block.sync
        def _(sp):
            loads_first(sp)
            load_units(sp, 0, 6)
            spare = scratch["blocks"][NE * BLK:NBLK * BLK, :]
            sp.dma_start(spare[0:T, :], A["x"][0]).then_inc(S("spare_filled"), 16)
            sp.dma_start(spare[T:NOVER * BLK, :], A["x"][0, 0:NOVER * BLK - T, :]).then_inc(S("spare_filled"), 16)
            loads_after_pairs(sp)
            load_units(sp, 6, at_unit("xo0"))
            moe_first_loads(sp, 0)
            load_units(sp, at_unit("xo0"), at_unit("sqkv"))
            moe_route_loads(sp, 0)
            moe_rows_out(sp, 0)
            moe_loads(sp, 0)
            further_sp(sp, 0)
            load_units(sp, at_unit("sqkv"), at_unit("xo1"))
            moe_first_loads(sp, 1)
            load_units(sp, at_unit("xo1"), len(UNITS))
            moe_route_loads(sp, 1)
            moe_rows_out(sp, 1)
            moe_loads(sp, 1)
            further_sp(sp, 1)
            final_sp(sp)

        @block.gpsimd
        def _(pool):
            constants(pool)
            pair_pool(pool)
            moe_constants(pool)
            for l in range(2):
                if l == 1:
                    sb_pool(pool)
                moe_pool(pool, l)
                further_pool(pool, l)
                moe_combine_pool(pool, l)

        @block.scalar
        def _(act):
            norm_act(act, "mix0", h, tn0, lambda e, t: e.wait_ge(S(f"x_in{t}"), 16))
            act.wait_ge(S("small_in"), SMALL)
            xT_evac(act, "mix0", xT, 0)
            rwkv_proj_act(act)
            rwkv_pre_act(act)
            pair_act(act)
            gn_act(act)
            mem_act(act)
            for l in range(2):
                if l == 1:
                    sb_proj_act(act)
                    sb_act(act)
                cross_act(act, l, "so" if l else "rwo")
                moe_route_act(act, l)
                moe_act(act, l)
                further_act(act, l)
            final_act(act)

        @block.tensor
        def _(pe):
            pe.wait_ge(S("const_ready"), 1)
            norm_pe(pe, "mix0", tn0)
            rwkv_proj_pe(pe)
            rwkv_pre_pe(pe)
            pair_pe(pe)
            gn_pe(pe)
            mem_pe(pe)
            post_pe(pe)
            for l in range(2):
                if l == 1:
                    sb_proj_pe(pe)
                    sb_pe(pe)
                cross_pe(pe, l)
                moe_route_pe(pe, l)
                moe_pe(pe, l)
                further_pe(pe, l)

        @block.vector
        def _(vec):
            for t in range(NT):
                vec.wait_ge(S(f"x_in{t}"), 16)
            norm_vec(vec, "mix0", h, tn0)
            vec.wait_ge(S("small_in"), SMALL)
            xT_evac(vec, "mix0", xT, 1)
            prm_vec(vec)
            rwkv_mix_vec(vec)
            rwkv_pre_vec(vec)
            pair_vec(vec)
            gn_vec(vec)
            mem_vec(vec)
            post_vec(vec)
            add_to_h(vec, FIRST["rwo"], x_back)
            for l in range(2):
                if l == 1:
                    norm_vec(vec, "mix1", h, tnS)
                    xT_evac(vec, "mix1", xTS, 1)
                    sb_vec(vec)
                    add_to_h(vec, FIRST["so"])
                cross_vec(vec, l)
                moe_route_vec(vec, l)
                moe_vec(vec, l)
                further_vec(vec, l)
                moe_combine_vec(vec, l)
            final_vec(vec)

_INS = ["x", "mem", "norm_mix", "norm_cross", "norm_ffn", "norm_mem", "norm_final",
        "rw_mix", "rw_wr", "rw_wk", "rw_wv", "rw_w0", "rw_w1", "rw_w2", "rw_a0", "rw_a1", "rw_a2",
        "rw_g1", "rw_g2", "rw_kk", "rw_ka", "rw_rk", "rw_lnx_w", "rw_lnx_b", "rw_wo",
        "sb_wqkv", "sb_wo", "xa_wq", "xa_wkv", "xa_wo",
        "moe_wg", "moe_bg", "moe_we", "moe_be", "moe_w1", "moe_w3", "moe_w2"]


def kernel(**inputs):
    import numpy as _np
    import concourse.bacc as _bacc
    from concourse.bass_utils import run_bass_kernel_spmd as _run

    nc = _bacc.Bacc("TRN2", target_bir_lowering=False, num_devices=1)
    arrays, aps = {}, {}
    for name in _INS:
        a = _np.ascontiguousarray(inputs[name])
        arrays[f"in_{name}"] = a
        aps[name] = nc.dram_tensor(f"in_{name}", a.shape, mybir.dt.from_np(a.dtype), kind="ExternalInput").ap()
    out = nc.dram_tensor("out_0", (1, T, C), F32, kind="ExternalOutput").ap()
    scratch = {
        "rows": nc.dram_tensor("normed_rows", (T, C), F32, kind="Internal").ap(),
        "blocks": nc.dram_tensor("expert_rows", (NBLK * BLK, C), F32, kind="Internal").ap(),
    }
    trunk(nc, aps, out, scratch)
    r = _run(nc, [arrays], core_ids=[0])
    return r.results[0]["out_0"]
```

```python
from contextlib import ExitStack

import concourse.bass as bass
from concourse import mybir

F32 = mybir.dt.float32
I32 = mybir.dt.int32
ALU = mybir.AluOpType
ACT = mybir.ActivationFunctionType
AX = mybir.AxisListType

P = 128
C = 1024
T = 512
NT = T // P
KC = C // P
NPAIR = KC
HD = 64
CH = 64
NCH = T // CH
M = 256
XH = 4
XD = C // XH
G, E = 4, 8
NE = G * E
F = 256
BLK = 64
NOVER = (2 * T - NE) // BLK
NBLK = NE + NOVER
EPS = 1e-6
GN_EPS = 64e-5
DECAY_C = float(2.718281828459045 ** -0.5)
XSCALE = float(XD) ** -0.5
BIG = 1e30

RING = 3

PLAN = [
    ("w1", 1, "A"), ("a1", 1, "A"), ("g1", 1, "A"),
    ("wr", 8, "A"), ("wk", 8, "A"), ("wv", 8, "A"),
    ("memk", 8, "A"), ("memv", 4, "A"),
    ("gate", 8, "V"), ("rwo", 8, "V"),
    ("xq0", 8, "A"), ("xv0", 8, "A"), ("xo0", 8, "V"),
    ("sq", 8, "A"), ("sk", 8, "A"), ("sv", 8, "A"), ("so", 8, "V"),
    ("xq1", 8, "A"), ("xv1", 8, "A"), ("xo1", 8, "V"),
]
FIRST, OWNER = {}, []
for _name, _n, _eng in PLAN:
    FIRST[_name] = len(OWNER)
    OWNER += [_eng[_g % len(_eng)] for _g in range(_n)]
NBANK = 4


def groups_done(g):
    return OWNER[:g + 1].count(OWNER[g])


UNITS = ["wr", "wr", "wk", "wk", "wv", "wv",
         "memkv", "memkv", "memkv", "memkv", "rwo", "rwo", "xq0", "xq0", "xo0", "xo0",
         "sqkv", "sqkv", "sqkv", "sqkv", "sqkv", "sqkv", "so", "so",
         "xq1", "xq1", "xo1", "xo1"]

FILLS = [("TA", 0, "A"), ("TV", 1, "A"), ("TB", 0, "A"), ("TK", 1, "A"), ("BN", 0, "V")]
for _s, _e in [("A0", "V"), ("A1", "V"), ("CC", "V"), ("B0", "V"), ("B1", "V"),
               ("Q2", "A"), ("Q2T", "A"), ("WV", "A"),
               ("Q4", "A"), ("Q4T", "A"), ("Z2", "V"),
               ("Q8", "A"), ("Z3", "V"), ("Z4", "V"),
               ("X", "A"), ("XT", "V"), ("R1", "V"),
               ("X2T", "A"), ("R2", "V"), ("R3", "V")]:
    FILLS += [(_s, 0, _e), (_s, 1, _e)]
FILLS += [("G", 0, "V"), ("G", 1, "V"), ("H", 0, "A"), ("H", 1, "A"), ("RP", 0, "V")]
FILLS += [(f"S{_c}", 0, "V") for _c in range(1, NCH - 1)]
FILLS += [("Y", 1, "A")]
FILL_NO = {(s, h): n for n, (s, h, e) in enumerate(FILLS)}
NFILL = len(FILLS)


def bank_of(n):
    h = FILLS[n][1]
    return 4 * h + sum(1 for s in FILLS[:n] if s[1] == h) % 4


def bank_before(n):
    h = FILLS[n][1]
    mine = [m for m in range(n) if FILLS[m][1] == h]
    return mine[-4] if len(mine) >= 4 else None


def evacs(n):
    return sum(1 for s in FILLS[:n + 1] if s[2] == FILLS[n][2])


NEV = {e: sum(1 for s in FILLS if s[2] == e) for e in "AV"}

NEEDS = {
    "Q2": lambda h: [("CC", h)], "Q2T": lambda h: [("CC", h)], "WV": lambda h: [("B1", h), ("TV", 1)],
    "Q4": lambda h: [("Q2T", h)], "Q4T": lambda h: [("Q2T", h)], "Z2": lambda h: [("Q2", h)],
    "Q8": lambda h: [("Q4T", h)], "Z3": lambda h: [("Z2", h), ("Q4", h)], "Z4": lambda h: [("Q8", h), ("Z3", h)],
    "X": lambda h: [("Z4", h)], "XT": lambda h: [("Z4", h)], "R1": lambda h: [("Z4", h), ("WV", h)],
    "X2T": lambda h: [("X", h), ("XT", h)], "R2": lambda h: [("X2T", h), ("R1", h)],
    "R3": lambda h: [("R2", h)], "G": lambda h: [("R3", 1), ("TB", 0)], "H": lambda h: [("R3", 1), ("TK", 1)],
    "RP": lambda h: [("R3", 1)],
    "S1": lambda h: [("G", 1), ("H", 1)], "Y": lambda h: [("R3", 0), ("R3", 1)],
}
for _c in range(2, NCH - 1):
    NEEDS[f"S{_c}"] = lambda h, c=_c: [(f"S{c - 1}", 0)]


def trunk(nc, A, out, scratch):
    ctx = ExitStack()
    with ctx:
        def sb(name, shape, dt=F32):
            return ctx.enter_context(nc.sbuf_tensor(name, shape, dt))

        sems = {}

        def S(name):
            if name not in sems:
                sems[name] = ctx.enter_context(nc.semaphore(name))
            return sems[name]

        def gate(eng):
            eng.nop().then_inc(S("gates"), 1)

        PS = ctx.enter_context(nc.psum_tensor("PS", [P, 8, 512], F32))

        def bank(b, *shape):
            v = PS[:, b, :]
            if len(shape) == 2:
                v = v.rearrange("p (a b) -> p a b", a=shape[0])
            if len(shape) == 3:
                v = v.rearrange("p (a b c) -> p a b c", a=shape[0], b=shape[1])
            return v

        h = sb("h", [P, NT, C])
        ring = sb("ring", [P, RING, KC, 512])
        ident = sb("ident", [P, P])
        ones = sb("ones", [P, P])
        gainT = sb("gainT", [P, 7, KC])
        sumsq = sb("sumsq", [P, NT])
        rms = sb("rms", [P, NT])
        rstd = sb("rstd", [P, NT])
        ARENA = 34 * 1024
        arena = sb("arena", [P, ARENA])

        def at(k1024, shape):
            n = 1
            for s in shape:
                n *= s
            o = int(k1024 * 1024)
            assert o + n <= ARENA, (o, n)
            return split(arena[:, o:o + n], shape)

        def split(v, shape):
            if len(shape) == 1:
                return v
            names = "abcd"[:len(shape)]
            return v.rearrange(f"p ({' '.join(names)}) -> p {' '.join(names)}",
                               **{names[j]: shape[j] for j in range(len(shape))})

        K_ = at(0, [KC, T])
        R_ = at(4, [KC, T])
        V_ = at(8, [KC, T])
        xT = at(12, [KC, T])
        dx = at(16, [KC, T])
        xm = [at(20, [KC, T]), at(24, [KC, T])]
        tn0 = at(24, [NT, C])
        KK = at(12, [KC, T])
        SG = at(16, [KC, T])
        AS = at(20, [KC, T])
        l1 = at(28, [KC, 256])
        w2s = at(30, [C])
        a2s = at(31, [C])
        g2s = at(32, [C])
        sg1 = at(33, [T])
        twa = at(33.5, [T])
        mixT = sb("mixT", [P, 6, KC])
        prow = sb("prow", [7 * KC, P])
        prm = sb("prm", [P, 7, KC])
        one_ka = sb("one_ka", [P, KC])
        hones = sb("hones", [P, P])
        masks = sb("masks", [P, 5, P])
        U16s, U64s, U64i, L16s, Loff = [masks[:, n, :] for n in range(5)]
        ident2 = sb("ident2", [P, HD])
        PC = sb("PC", [P, NCH])
        gn_eps = sb("gn_eps", [P, 1])

        hW = h[:, :, :].rearrange("p t c -> p (t c)")
        S_ = hW[:, 0:512]
        Pe = hW[:, 512:1024]
        Pp = hW[:, 1024:1536]
        Pi = hW[:, 1536:2048]
        Pf = hW[:, 2048:2560]
        bb = hW[:, 2560:3072]
        notfirst = hW[:, 3072:3584]
        VTp = hW[:, 3584:4096]
        k2 = at(24, [T])
        AR = at(24.5, [2, T])
        B2 = at(26.5, [T])
        K2 = at(27, [T])
        RK = at(27.5, [T])
        Bt = at(28, [NT, P])
        Kt = at(28.5, [NT, P])
        Vp = at(29, [NT, P])
        Rpp = at(29.5, [T])
        GT = at(30, [NCH, P])
        Hs = at(31, [NCH, P])
        dPC = at(33.5, [NCH, HD])
        ringW = ring[:, :, :, :].rearrange("p r k n -> p (r k n)")
        BT = [at(25.5, [T]), ringW[:, 22 * 512:23 * 512]]
        KT = [at(26, [T]), ringW[:, 23 * 512:24 * 512]]

        def mat(slot, hh):
            o = (2 * slot + hh) * 512
            return split(ringW[:, o:o + 512], [NT, P])

        MdT, Md, Nf, RBT, RKT, WT, Q2, Q2T, Z, XT, RHS = [[mat(s, hh) for hh in range(2)] for s in range(11)]
        Q4, Q4T, Xm, X2T, Q8 = MdT, Md, WT, Q2, Q2T

        YT = at(0, [KC, T])
        Ysq = at(16, [KC, T])
        Ysd = at(20, [KC, T])
        mem_rows = at(26, [M // P, C])
        mem_tn = at(14, [M // P, C])
        mem_xT = at(24, [KC, M])
        memK = at(28, [KC, M])
        memV = at(30, [M // P, C])

        def src8(w):
            return w.rearrange("(p k) n -> p k n", k=KC)

        def srcn(w):
            return w.rearrange("(k p) n -> p k n", p=P)

        def unit_source(u):
            name = UNITS[u]
            i = u - UNITS.index(name)
            if name in ("wr", "wk", "wv"):
                w = src8(A["rw_" + name][0])
            elif name == "rwo":
                w = srcn(A["rw_wo"][0])
            elif name == "memkv":
                w = src8(A["xa_wkv"])
            elif name == "sqkv":
                w = src8(A["sb_wqkv"][0])
            elif name == "so":
                w = srcn(A["sb_wo"][0])
            elif name[:2] == "xq":
                w = src8(A["xa_wq"][int(name[2])])
            else:
                w = srcn(A["xa_wo"][int(name[2])])
            return w[:, :, 512 * i:512 * i + 512]

        def unit_last_group(u):
            name = UNITS[u]
            i = u - UNITS.index(name)
            if name == "memkv":
                return FIRST["memk"] + 4 * i + 3 if i < 2 else FIRST["memv"] + 2 * (i - 2) + 1
            if name == "sqkv":
                return FIRST["sq"] + 4 * i + 3
            return FIRST[name] + 4 * i + 3

        def load_units(sp, u0, u1):
            for u in range(u0, u1):
                if u >= RING:
                    sp.wait_ge(S("proj_filled"), unit_last_group(u - RING) + 1)
                sp.dma_start(ring[:, u % RING, :, :], unit_source(u)).then_inc(S(f"unit_in{u % RING}"), 16)

        def unit_arrived(eng, u):
            eng.wait_ge(S(f"unit_in{u % RING}"), 16 * (u // RING + 1))

        def ldnat(a):
            return a.rearrange("(j p) -> j p", p=P)

        def loads_first(sp):
            for t in range(NT):
                sp.dma_start(h[:, t, :], A["x"][0, P * t:P * t + P, :]).then_inc(S(f"x_in{t}"), 16)
            for n, g in enumerate([A["norm_mix"][0], A["norm_cross"][0], A["norm_ffn"][0], A["norm_mix"][1],
                                   A["norm_cross"][1], A["norm_ffn"][1], A["norm_mem"]]):
                sp.dma_start(gainT[:, n, :], g.rearrange("(p k) -> p k", k=KC)).then_inc(S("small_in"), 16)
            sp.dma_start(mixT[:, :, :], A["rw_mix"][0].rearrange("i (p k) -> p i k", k=KC)).then_inc(S("small_in"), 16)
            for n, g in enumerate([A["rw_w0"][0], A["rw_a0"][0], A["rw_kk"][0], A["rw_ka"][0]]):
                sp.dma_start(prow[8 * n:8 * n + 8, :], ldnat(g)).then_inc(S("small_in"), 16)
            sp.dma_start(prow[32:40, :], A["rw_rk"][0].rearrange("(j a) n -> j (a n)", a=2)).then_inc(S("small_in"), 16)
            for n, g in enumerate([A["rw_lnx_w"][0], A["rw_lnx_b"][0]]):
                sp.dma_start(prow[40 + 8 * n:48 + 8 * n, :], ldnat(g)).then_inc(S("small_in"), 16)
            sp.dma_start(l1[:, :, 0:64], src8(A["rw_w1"][0])).then_inc(S("small_in"), 16)
            sp.dma_start(l1[:, :, 64:128], src8(A["rw_a1"][0])).then_inc(S("small_in"), 16)
            sp.dma_start(l1[:, :, 128:256], src8(A["rw_g1"][0])).then_inc(S("small_in"), 16)
            sp.dma_start(w2s[0:HD, :], A["rw_w2"][0]).then_inc(S("small_in"), 16)
            sp.dma_start(a2s[HD:P, :], A["rw_a2"][0]).then_inc(S("small_in"), 16)
            sp.dma_start(g2s[:, :], A["rw_g2"][0]).then_inc(S("small_in"), 16)
        SMALL = 16 * (7 + 1 + 7 + 6)

        def loads_after_pairs(sp):
            sp.wait_ge(S("filled"), NPAIR * NFILL)
            for t in range(NT):
                sp.dma_start(h[:, t, :], A["x"][0, P * t:P * t + P, :]).then_inc(S("x_again"), 16)
            for m in range(M // P):
                sp.dma_start(mem_rows[:, m, :], A["mem"][0, P * m:P * m + P, :]).then_inc(S("mem_in"), 16)

        def bcast(v):
            return bass.AP(tensor=v.tensor, offset=v.offset, ap=[[0, P]] + [list(x) for x in v.ap])

        def constants(pool):
            n = [0]

            def sel(m, op, fill, base, pattern, cm, view=None):
                pool.wait_ge(S("const_step"), n[0])
                v = m if view is None else view
                pool.affine_select(out=v, in_=v, compare_op=op, fill=fill, base=base, pattern=pattern,
                                   channel_multiplier=cm).then_inc(S("const_step"), 1)
                n[0] += 1

            pool.memset(gn_eps[:, :], GN_EPS).then_inc(S("const_step"), 1)
            n[0] += 1
            for m, v in ((ident, 0.0), (ident2, 0.0), (ones, 1.0), (hones, 1.0), (U16s, 1.0), (U64s, 1.0),
                         (U64i, 1.0), (L16s, 1.0), (Loff, 1.0)):
                pool.memset(m[:, :], v).then_inc(S("const_step"), 1)
                n[0] += 1
            sel(ident[:, :], ALU.not_equal, 1.0, 0, [[-1, P]], 1)
            sel(ident2[:, :], ALU.not_equal, 1.0, 0, [[-1, HD]], 1)
            sel(ident2[:, :], ALU.not_equal, 1.0, -HD, [[-1, HD]], 1)

            def blocks(m, b):
                v = m[:, :].rearrange("p (a b) -> p a b", b=b)
                sel(v, ALU.is_ge, 0.0, 0, [[-b, P // b], [0, b]], 1)
                sel(v, ALU.is_ge, 0.0, b - 1, [[b, P // b], [0, b]], -1)

            blocks(hones, HD)
            blocks(U16s, 16)
            sel(U16s[:, :], ALU.is_gt, 0.0, 0, [[1, P]], -1)
            blocks(U64s, CH)
            sel(U64s[:, :], ALU.is_gt, 0.0, 0, [[1, P]], -1)
            blocks(U64i, CH)
            sel(U64i[:, :], ALU.is_ge, 0.0, 0, [[1, P]], -1)
            blocks(L16s, 16)
            sel(L16s[:, :], ALU.is_gt, 0.0, 0, [[-1, P]], 1)
            blocks(Loff, CH)
            sel(Loff[:, :], ALU.is_gt, 0.0, 0, [[-1, P]], 1)
            pool.wait_ge(S("const_step"), n[0])
            pool.tensor_tensor(Loff[:, :], Loff[:, :], L16s[:, :], ALU.subtract).then_inc(S("const_ready"), 1)
            pool.wait_ge(S("const_ready"), 1)
            pool.memset(w2s[HD:P, :], 0.0).then_inc(S("rates_padded"), 1)
            pool.memset(a2s[0:HD, :], 0.0).then_inc(S("rates_padded"), 1)

        NORMS = [("mix0", NT), ("mem", M // P), ("cross0", NT), ("ffn0", NT), ("mix1", NT), ("cross1", NT),
                 ("ffn1", NT), ("final", NT)]
        NIDX = {n: j for j, (n, _) in enumerate(NORMS)}
        TILE0 = {n: sum(c for _, c in NORMS[:j]) for j, (n, _) in enumerate(NORMS)}
        TPOSE0 = {n: KC * j for j, (n, _) in enumerate(NORMS)}
        GAIN = {"mix0": 0, "cross0": 1, "ffn0": 2, "mix1": 3, "cross1": 4, "ffn1": 5, "mem": 6}

        def norm_act(act, name, src, tn, tile_ready):
            nt = dict(NORMS)[name]
            for t in range(nt):
                tile_ready(act, t)
                act.activation(tn[:, t, :], src[:, t, :], ACT.Square, accum_out=sumsq[:, t:t + 1])\
                    .then_inc(S("norm_squares"), 1)
            act.wait_ge(S("norm_mean"), NIDX[name] + 1)
            act.activation(rms[:, 0:nt], rms[:, 0:nt], ACT.Sqrt).then_inc(S("norm_root"), 1)

        def norm_vec(vec, name, src, tn):
            nt = dict(NORMS)[name]
            vec.wait_ge(S("norm_squares"), TILE0[name] + nt)
            vec.tensor_scalar(rms[:, 0:nt], sumsq[:, 0:nt], 1.0 / C, EPS, ALU.mult, ALU.add)\
                .then_inc(S("norm_mean"), 1)
            vec.wait_ge(S("norm_root"), NIDX[name] + 1)
            vec.reciprocal(rstd[:, 0:nt], rms[:, 0:nt]).then_inc(S("norm_recip"), 1)
            vec.wait_ge(S("norm_recip"), NIDX[name] + 1)
            for t in range(nt):
                vec.tensor_scalar(tn[:, t, :], src[:, t, :], rstd[:, t:t + 1], None, ALU.mult)\
                    .then_inc(S("norm_rows"), 1)

        def norm_pe(pe, name, tn):
            nt = dict(NORMS)[name]
            for k in range(KC):
                n = TPOSE0[name] + k
                if n >= 2:
                    pe.wait_ge(S("xT_act" if n % 2 == 0 else "xT_vec"), n // 2)
                for t in range(nt):
                    if k == 0:
                        pe.wait_ge(S("norm_rows"), TILE0[name] + t + 1)
                    ins = pe.transpose(PS[:, 6 + n % 2, P * t:P * t + P], tn[:, t, k::KC], ident[:, :])
                ins.then_inc(S("norm_turned"), 1)

        def xT_evac(eng, name, dst, which):
            nt = dict(NORMS)[name]
            for k in range(which, KC, 2):
                n = TPOSE0[name] + k
                eng.wait_ge(S("norm_turned"), n + 1)
                g = gainT[:, GAIN[name], k:k + 1]
                if which == 0:
                    eng.activation(dst[:, k, 0:nt * P], PS[:, 6 + n % 2, 0:nt * P], ACT.Copy, scale=g)\
                        .then_inc(S("xT_act"), 1)
                else:
                    eng.tensor_scalar(dst[:, k, 0:nt * P], PS[:, 6 + n % 2, 0:nt * P], g, None, ALU.mult)\
                        .then_inc(S("xT_vec"), 1)

        def xT_there(eng, name, k):
            n = TPOSE0[name] + k
            eng.wait_ge(S("xT_act" if n % 2 == 0 else "xT_vec"), n // 2 + 1)

        def bank_free(pe, g):
            if g >= NBANK:
                pe.wait_ge(S("proj_out_" + OWNER[g - NBANK]), groups_done(g - NBANK))

        def group_out(eng, g):
            eng.wait_ge(S("proj_filled"), g + 1)
            return PS[:, g % NBANK, :]

        def group_evacuated(eng, g):
            eng.wait_ge(S("proj_out_" + OWNER[g]), groups_done(g))

        def project_T(pe, g0, u0, xt, n, ready, chunks=range(8)):
            for j in chunks:
                g = g0 + j
                u = u0 + j // 4
                if j % 4 == 0:
                    unit_arrived(pe, u)
                bank_free(pe, g)
                for k in range(KC):
                    if j == 0:
                        ready(pe, k)
                    ins = pe.matmul(PS[:, g % NBANK, 0:n], ring[:, u % RING, k, P * (j % 4):P * (j % 4) + P],
                                    xt[:, k, 0:n], start=(k == 0), stop=(k == KC - 1))
                ins.then_inc(S("proj_filled"), 1)

        def project_tok(pe, g0, u0, xt, ready, tiles=NT):
            for half in range(2):
                unit_arrived(pe, u0 + half)
                for t in range(tiles):
                    g = g0 + tiles * half + t
                    bank_free(pe, g)
                    for k in range(KC):
                        if half == 0 and t == 0:
                            ready(pe, k)
                        ins = pe.matmul(PS[:, g % NBANK, :], xt[:, k, P * t:P * t + P],
                                        ring[:, (u0 + half) % RING, k, :], start=(k == 0), stop=(k == KC - 1))
                    ins.then_inc(S("proj_filled"), 1)

        def evac_T(act, g0, dst, n=T, chunks=range(8)):
            for j in chunks:
                act.activation(dst[:, j, 0:n], group_out(act, g0 + j)[:, 0:n], ACT.Copy).then_inc(S("proj_out_A"), 1)

        def evac_tok(act, g0, dst, tiles=NT):
            for half in range(2):
                for t in range(tiles):
                    act.activation(dst[:, t, 512 * half:512 * half + 512], group_out(act, g0 + tiles * half + t),
                                   ACT.Copy).then_inc(S("proj_out_A"), 1)

        def add_to_h(vec, g0, ready=None):
            for half in range(2):
                for t in range(NT):
                    if ready and half == 0:
                        ready(vec, t)
                    v = h[:, t, 512 * half:512 * half + 512]
                    vec.tensor_tensor(v, v, group_out(vec, g0 + NT * half + t), ALU.add)\
                        .then_inc(S("proj_out_V"), 1)

        MIXES = [("w1", 1), ("a1", 4), ("g1", 5), ("wr", 0), ("wk", 2), ("wv", 3)]
        LORA_AT = {"w1": (0, 64), "a1": (64, 64), "g1": (128, 128)}

        def rwkv_mix_vec(vec):
            vec.wait_ge(S("small_in"), SMALL)
            for k in range(KC):
                xT_there(vec, "mix0", k)
            vec.tensor_tensor(dx[:, :, 1:T], xT[:, :, 0:T - 1], xT[:, :, 1:T], ALU.subtract).then_inc(S("dx_ready"), 1)
            vec.tensor_scalar(dx[:, :, 0:1], xT[:, :, 0:1], -1.0, None, ALU.mult).then_inc(S("dx_ready"), 1)
            vec.wait_ge(S("dx_ready"), 2)
            for n, (name, i) in enumerate(MIXES):
                if n >= 2:
                    before = MIXES[n - 2][0]
                    vec.wait_ge(S("proj_filled"), FIRST[before] + dict((a, b) for a, b, _ in PLAN)[before])
                for k in range(KC):
                    vec.scalar_tensor_tensor(out=xm[n % 2][:, k, :], in0=dx[:, k, :], scalar=mixT[:, i, k:k + 1],
                                             in1=xT[:, k, :], op0=ALU.mult, op1=ALU.add).then_inc(S("mixed"), 1)

        def rwkv_proj_pe(pe):
            pe.wait_ge(S("small_in"), SMALL)
            pe.transpose(PS[:, 5, 0:7 * KC], prow[:, :], ident[0:7 * KC, 0:7 * KC]).then_inc(S("prm_turned"), 1)
            for n, (name, _) in enumerate(MIXES):
                def ready(e, k, n=n):
                    e.wait_ge(S("mixed"), KC * n + k + 1)
                x_ = xm[n % 2]
                g = FIRST[name]
                if name in LORA_AT:
                    o, m = LORA_AT[name]
                    bank_free(pe, g)
                    for k in range(KC):
                        ready(pe, k)
                        ins = pe.matmul(PS[HD:P, g % NBANK, :] if name == "a1" else PS[0:m, g % NBANK, :],
                                        l1[:, k, o:o + m], x_[:, k, :],
                                        start=(k == 0), stop=(k == KC - 1))
                    ins.then_inc(S("proj_filled"), 1)
                elif name == "wv":
                    rates_pe(pe)
                    project_T(pe, g, UNITS.index(name), x_, T, ready, range(2))
                    norms_pe(pe)
                    project_T(pe, g, UNITS.index(name), x_, T, ready, range(2, 8))
                else:
                    project_T(pe, g, UNITS.index(name), x_, T, ready)

        def rwkv_proj_act(act):
            act.activation(twa[0:HD, :], group_out(act, FIRST["w1"])[0:HD, :], ACT.Tanh).then_inc(S("proj_out_A"), 1)
            act.activation(twa[HD:P, :], group_out(act, FIRST["a1"])[HD:P, :], ACT.Copy).then_inc(S("proj_out_A"), 1)
            act.activation(sg1[:, :], group_out(act, FIRST["g1"]), ACT.Sigmoid).then_inc(S("proj_out_A"), 1)
            evac_T(act, FIRST["wr"], R_)
            evac_T(act, FIRST["wk"], K_)
            rates_act(act)
            evac_T(act, FIRST["wv"], V_, chunks=range(2))
            act.wait_ge(S("pre_norm"), KC)
            act.activation(KK[:, :, :], KK[:, :, :], ACT.Sqrt).then_inc(S("kk_root"), 1)
            exponentials(act, 0, True)
            evac_T(act, FIRST["wv"], V_, chunks=range(2, 8))

        def prm_vec(vec):
            vec.wait_ge(S("prm_turned"), 1)
            vec.tensor_copy(prm[:, :, :], PS[:, 5, 0:7 * KC].rearrange("p (n j) -> p n j", n=7)).then_inc(S("prm_ready"), 1)
            vec.wait_ge(S("prm_ready"), 1)
            vec.tensor_scalar(one_ka[:, :], prm[:, 3, :], -1.0, 1.0, ALU.mult, ALU.add).then_inc(S("prm_ready"), 1)

        def rates_pe(pe):
            group_evacuated(pe, FIRST["a1"])
            pe.wait_ge(S("rates_padded"), 2)
            for j in range(KC):
                if j >= 2:
                    pe.wait_ge(S("pre_sig"), 2 * j - 2)
                else:
                    xT_there(pe, "mix0", 6 + j)
                    pe.wait_ge(S("prm_ready"), 1)
                pe.matmul(PS[:, 4 + 2 * (j % 2), :], w2s[:, P * j:P * j + P], twa, start=True, stop=True)
                pe.matmul(PS[:, 5 + 2 * (j % 2), :], a2s[:, P * j:P * j + P], twa, start=True, stop=True)\
                    .then_inc(S("pre_filled"), 1)

        def norms_pe(pe):
            pe.wait_ge(S("pre_sig"), 2 * KC)
            for j in range(KC):
                pe.wait_ge(S("pre_sq"), j + 1)
                if j >= 4:
                    pe.wait_ge(S("pre_norm"), j - 3)
                pe.matmul(PS[:, 4 + j % 4, :], hones[:, :], KK[:, j, :], start=True, stop=True)\
                    .then_inc(S("pre_summed"), 1)

        def rates_act(act):
            act.wait_ge(S("prm_ready"), 2)
            act.wait_ge(S("mixed"), KC * len(MIXES))
            for j in range(KC):
                act.wait_ge(S("pre_filled"), j + 1)
                act.activation(SG[:, j, :], PS[:, 4 + 2 * (j % 2), :], ACT.Sigmoid, bias=prm[:, 0, j:j + 1])\
                    .then_inc(S("pre_sig"), 1)
                act.activation(AS[:, j, :], PS[:, 5 + 2 * (j % 2), :], ACT.Sigmoid, bias=prm[:, 1, j:j + 1])\
                    .then_inc(S("pre_sig"), 1)
            for j in range(KC):
                group_evacuated(act, FIRST["wk"] + j)
                act.activation(KK[:, j, :], K_[:, j, :], ACT.Square, scale=prm[:, 2, j:j + 1]).then_inc(S("pre_sq"), 1)

        def rwkv_pre_vec(vec):
            vec.memset(notfirst, 1.0).then_inc(S("notfirst_ready"), 1)
            vec.wait_ge(S("notfirst_ready"), 1)
            vec.memset(split(notfirst, [NCH, CH])[:, :, 0:1], 0.0).then_inc(S("notfirst_ready"), 1)
            vec.wait_ge(S("notfirst_ready"), 2)
            vec.wait_ge(S("pre_sig"), 2 * KC)
            sums(vec, 0, True)
            for j in range(KC):
                vec.wait_ge(S("pre_summed"), j + 1)
                vec.tensor_scalar(KK[:, j, :], PS[:, 4 + j % 4, :], 1e-24, None, ALU.max).then_inc(S("pre_norm"), 1)
            vec.wait_ge(S("kk_root"), 1)
            for j in range(KC):
                vec.reciprocal(KK[:, j, :], KK[:, j, :]).then_inc(S("kk_recip"), 1)
                vec.wait_ge(S("kk_recip"), j + 1)
                vec.scalar_tensor_tensor(out=KK[:, j, :], in0=K_[:, j, :], scalar=prm[:, 2, j:j + 1],
                                         in1=KK[:, j, :], op0=ALU.mult, op1=ALU.mult).then_inc(S("kk_ready"), 1)

        NP2 = 6
        TK_FILLED = FILL_NO["TK", 1] + 1

        def half(hh):
            return slice(HD * hh, HD * hh + HD)

        def pair_pool(pool):
            pool.wait_ge(S("pre_filled"), KC)
            pool.memset(GT, 0.0).then_inc(S("zeros_ready"), 1)
            pool.memset(Hs, 0.0).then_inc(S("zeros_ready"), 1)
            pool.wait_ge(S("proj_filled"), FIRST["wv"] + 8)
            for hh in range(2):
                pool.wait_ge(S("zeros_ready"), 2 + 2 * hh)
                pool.memset(BT[hh][half(1 - hh), :], 0.0).then_inc(S("zeros_ready"), 1)
                pool.memset(KT[hh][half(1 - hh), :], 0.0).then_inc(S("zeros_ready"), 1)

            def prepare(j, first=False):
                if not first:
                    pool.wait_ge(S("p2_ready"), NP2 * j)
                    pool.wait_ge(S("b2_ready"), 2 * j)
                pool.wait_ge(S("kk_ready"), j + 1)
                pool.tensor_tensor(bb, KK[:, j, :], AS[:, j, :], ALU.mult).then_inc(S("b_ready"), 1)
                pool.wait_ge(S("k2_step"), j + 1)
                pool.tensor_tensor(k2, k2, K_[:, j, :], ALU.mult).then_inc(S("k2_ready"), 1)
                if not first:
                    pool.wait_ge(S("filled"), (j - 1) * NFILL + TK_FILLED)
                pool.tensor_copy(VTp, V_[:, j, :]).then_inc(S("vt_ready"), 1)
                pool.wait_ge(S("pe_ready"), 2 * j + 2)
                pool.wait_ge(S("b_ready"), j + 1)
                pool.tensor_tensor(B2, bb, Pe, ALU.mult).then_inc(S("b2_ready"), 1)
                pool.wait_ge(S("k2_ready"), j + 1)
                pool.tensor_tensor(K2, k2, Pe, ALU.mult).then_inc(S("b2_ready"), 1)

            pool.wait_ge(S("zeros_ready"), NZERO)
            prepare(0, True)
            with pool.Fori(1, NPAIR) as j:
                prepare(j)

        def parity(m, q, hh):
            return m.rearrange("p (t q) d -> p t q d", q=2)[half(hh), :, q, half(hh)]

        RHS4 = ringW[:, 20 * 512:22 * 512].rearrange("p (a t n) -> p a t n", a=2, t=NT)

        def next_prepared(eng, body):
            with eng.Fori(0, NPAIR - 1) as i:
                body(i, i + 1)
            body(NPAIR - 1, None)

        def exponentials(act, j, first=False):
            if not first:
                act.wait_ge(S("p2_ready"), NP2 * j)
                act.wait_ge(S("b2_ready"), 2 * j)
                act.wait_ge(S("r_ready"), j)
            act.wait_ge(S("sum_ready"), 3 * j + 1)
            act.activation(Pf, S_, ACT.Exp, scale=-DECAY_C).then_inc(S("pf_ready"), 1)
            act.activation(Pi, S_, ACT.Exp, scale=DECAY_C).then_inc(S("pi_ready"), 1)
            if not first:
                act.wait_ge(S("dpc_ready"), j)
            act.activation(PC[:, :], split(S_, [NCH, CH])[:, :, CH - 1], ACT.Exp, scale=-DECAY_C)\
                .then_inc(S("pc_ready"), 1)
            act.wait_ge(S("sum_ready"), 3 * j + 2)
            act.activation(Pp, Pp, ACT.Exp, scale=-DECAY_C).then_inc(S("pe_ready"), 1)
            act.wait_ge(S("sum_ready"), 3 * j + 3)
            act.activation(Pe, Pe, ACT.Exp, scale=DECAY_C).then_inc(S("pe_ready"), 1)

        def pair_act(act):
            def prepare(j):
                act.wait_ge(S("p2_ready"), NP2 * j)
                act.wait_ge(S("b2_ready"), 2 * j)
                k2_step(j)
                exponentials(act, j)

            def k2_step(j):
                act.activation(k2, AS[:, j, :], ACT.Identity, bias=one_ka[:, bass.ds(j, 1)],
                               scale=prm[:, 3, bass.ds(j, 1)]).then_inc(S("k2_step"), 1)

            def body(i, following):
                def evac(step, hh, dst, src, last=True):
                    n = FILL_NO[step, hh]
                    act.wait_ge(S("filled"), i * NFILL + n + 1)
                    ins = act.activation(dst, src, ACT.Copy)
                    if last:
                        ins.then_inc(S("evac_A"), 1)

                for n, (step, hh, e) in enumerate(FILLS):
                    if e != "A":
                        continue
                    b = bank_of(n)
                    if step == "TA":
                        evac(step, hh, RHS4[:, :, :, 0:HD], bank(b, NT, 2, HD).rearrange("p t a d -> p a t d"))
                    elif step == "WV":
                        evac(step, hh, RHS[hh][:, :, HD:P],
                             bank(b, NT, 2, HD)[:, :, hh, :])
                    elif step == "Y":
                        evac(step, hh, K_[:, i, :], PS[:, b, :])
                        act.wait_ge(S("evac_A"), i * NEV["A"] + NEV["A"])
                        act.nop().then_inc(S("y_out"), 1)
                    elif step == "H":
                        for a in range(2):
                            evac(step, hh, parity(Hs, hh, a), bank(b, NT, P)[half(a), :, 0:HD], last=(a == 1))
                    else:
                        dst = {"TB": Bt, "TK": Kt, "TV": Vp}.get(step)
                        if dst is None:
                            dst = {"Q2": Q2, "Q2T": Q2T, "Q4": Q4, "Q4T": Q4T, "Q8": Q8, "X": Xm, "X2T": X2T}[step][hh]
                        evac(step, hh, dst, bank(b, NT, P))
                    if step == "TK" and following is not None:
                        prepare(following)

            act.wait_ge(S("proj_filled"), FIRST["wv"] + 8)
            k2_step(0)
            act.wait_ge(S("zeros_ready"), NZERO)
            next_prepared(act, body)
        NZERO = 6

        def sums(vec, j, first=False):
            if not first:
                vec.wait_ge(S("pc_ready"), j)
                vec.wait_ge(S("pe_ready"), 2 * j)
                vec.wait_ge(S("b2_ready"), 2 * j)
                vec.wait_ge(S("p2_ready"), NP2 * j)
            vec.tensor_tensor_scan(S_, notfirst, SG[:, j, :], 0.0, ALU.mult, ALU.add).then_inc(S("sum_ready"), 1)
            vec.wait_ge(S("sum_ready"), 3 * j + 1)
            vec.tensor_tensor(Pp, S_, SG[:, j, :], ALU.subtract).then_inc(S("sum_ready"), 1)
            s3 = split(S_, [NCH, CH])
            vec.tensor_tensor(split(Pe, [NCH, CH]), s3, s3[:, :, CH - 1:CH].to_broadcast([P, NCH, CH]),
                              ALU.subtract).then_inc(S("sum_ready"), 1)

        def pair_vec(vec):
            mask = {"A": (U16s, U64i), "B": (U64s, U64i), "C": (L16s, Loff)}

            def over(m, n):
                return m[:, :].unsqueeze(1).to_broadcast([P, n, P])

            def factors(j):
                vec.wait_ge(S("k2_ready"), j + 1)
                vec.wait_ge(S("pi_ready"), j + 1)
                for hh in range(2):
                    r = half(hh)
                    vec.tensor_tensor(KT[hh][r, :], k2[r, :], Pi[r, :], ALU.mult).then_inc(S("p2_ready"), 1)
                    vec.tensor_tensor(BT[hh][r, :], bb[r, :], Pi[r, :], ALU.mult).then_inc(S("p2_ready"), 1)
                vec.wait_ge(S("pe_ready"), 2 * j + 1)
                vec.wait_ge(S("kk_ready"), j + 1)
                vec.scalar_tensor_tensor(out=AR[:, 0, :], in0=KK[:, j, :], scalar=-1.0, in1=Pp,
                                         op0=ALU.mult, op1=ALU.mult).then_inc(S("p2_ready"), 1)
                vec.scalar_tensor_tensor(out=RK, in0=R_[:, j, :], scalar=prm[:, 4, bass.ds(j, 1)], in1=k2,
                                         op0=ALU.mult, op1=ALU.mult).then_inc(S("p2_ready"), 1)

            def late_factors(j):
                vec.wait_ge(S("pf_ready"), j + 1)
                vec.tensor_tensor(AR[:, 1, :], R_[:, j, :], Pf, ALU.mult).then_inc(S("r_ready"), 1)
                vec.wait_ge(S("pc_ready"), j + 1)
                vec.tensor_tensor(dPC, ident2[:, :].unsqueeze(1).to_broadcast([P, NCH, HD]),
                                  PC[:, :].unsqueeze(2).to_broadcast([P, NCH, HD]), ALU.mult).then_inc(S("dpc_ready"), 1)

            def body(i, following):
                own = i * NEV["V"]
                if following is not None:
                    sums(vec, following)
                for n, (step, hh, e) in enumerate(FILLS):
                    if e != "V":
                        continue
                    b = bank_of(n)
                    vec.wait_ge(S("filled"), i * NFILL + n + 1)

                    def add(dst, src, old):
                        vec.tensor_tensor(dst, src, old, ALU.add).then_inc(S("evac_V"), 1)

                    def masked(dst, src, m, nt):
                        return vec.tensor_tensor(dst, src, over(m, nt), ALU.mult)

                    if step == "BN":
                        vec.tensor_tensor(V_[:, i, :], V_[:, i, :], PS[:, b, :], ALU.mult).then_inc(S("evac_V"), 1)
                    elif step in ("A0", "A1", "B0", "B1"):
                        q = 2 * int(step[1])
                        left, right = (MdT, RBT) if step[0] == "A" else (WT, RKT)
                        ps = bank(b, 2, 2, P)
                        masked(left[hh][:, q:q + 2, :], ps[:, :, 0, :], mask[step[0]][0], 2)
                        masked(right[hh][:, q:q + 2, :], ps[:, :, 1, :], mask[step[0]][1], 2).then_inc(S("evac_V"), 1)
                    elif step == "CC":
                        masked(Md[hh], bank(b, NT, P), L16s, NT)
                        masked(Nf[hh], bank(b, NT, P), Loff, NT).then_inc(S("evac_V"), 1)
                        vec.wait_ge(S("evac_V"), own + evacs(n))
                        vec.tensor_tensor(Z[hh], MdT[hh], over(ident, NT), ALU.add).then_inc(S("z_begun"), 1)
                    elif step in ("Z2", "Z3", "Z4"):
                        if step == "Z2":
                            vec.wait_ge(S("z_begun"), 2 * i + hh + 1)
                        add(Z[hh], bank(b, NT, P), Z[hh])
                    elif step == "XT":
                        vec.tensor_copy(XT[hh], bank(b, NT, P)).then_inc(S("evac_V"), 1)
                    elif step == "R1":
                        vec.tensor_copy(RHS[hh], bank(b, NT, P)).then_inc(S("evac_V"), 1)
                    elif step in ("R2", "R3"):
                        add(RHS[hh], bank(b, NT, P), RHS[hh])
                    elif step == "RP":
                        add(Rpp, PS[:, b, :], AR[:, 1, :])
                    elif step == "G":
                        for a in range(2):
                            ins = vec.tensor_tensor(parity(GT, hh, a), bank(b, NT, P)[half(a), :, 0:HD],
                                                    dPC.rearrange("p (t q) d -> p t q d", q=2)[half(a), :, hh, :],
                                                    ALU.add)
                        ins.then_inc(S("evac_V"), 1)
                    else:
                        c = int(step[1:])
                        vec.wait_ge(S("evac_A"), i * NEV["A"] + evacs(FILL_NO["H", 1]))
                        add(Hs[:, c, :], PS[:, b, 0:P], Hs[:, c, :])
                    if (step, hh) == ("B1", 1) and following is not None:
                        factors(following)
                if following is not None:
                    late_factors(following)

            factors(0)
            late_factors(0)
            vec.wait_ge(S("zeros_ready"), NZERO)
            next_prepared(vec, body)

        def pair_pe(pe):
            group_evacuated(pe, FIRST["wv"] + 7)
            pe.wait_ge(S("pre_norm"), KC)
            pe.wait_ge(S("zeros_ready"), NZERO)
            pe.nop().then_inc(S("y_out"), 1)
            with pe.Fori(0, NPAIR) as i:
                def fill(step, hh):
                    n = FILL_NO[step, hh]
                    m = bank_before(n)
                    need = [FILL_NO[d] for d in NEEDS.get(step, lambda hh: [])(hh)] + ([m] if m is not None else [])
                    for e in "AV":
                        last = [evacs(m) for m in need if FILLS[m][2] == e]
                        if last:
                            pe.wait_ge(S("evac_" + e), i * NEV[e] + max(last))
                    return bank_of(n)

                def mm4(b, lhs, rhs):
                    for t in range(NT):
                        ins = pe.matmul(PS[:, b, P * t:P * t + P], lhs[:, t, :], rhs[:, t, :], start=True, stop=True)
                    ins.then_inc(S("filled"), 1)

                yb = bank_of(FILL_NO["Y", 1])
                first_in_yb = min(n for n in range(NFILL) if bank_of(n) == yb)
                AT = split(AR[:, 0, :], [NT, P])
                products = {"Q2": (MdT, Md), "Q2T": (Md, MdT), "WV": (WT, [Vp, Vp]), "Q4": (Q2T, Q2),
                            "Q4T": (Q2, Q2T), "Z2": (Q2, Z), "Q8": (Q4T, Q4), "Z3": (Q4, Z), "Z4": (Q8, Z),
                            "X": (Z, Nf), "XT": (Nf, Z), "R1": (Z, RHS), "X2T": (Xm, XT), "R2": (X2T, RHS),
                            "R3": (XT, RHS), "CC": ([AT, AT], [split(m, [NT, P]) for m in BT])}

                def y_local(t):
                    o = slice(P * t, P * t + P)
                    for a in range(2):
                        pe.matmul(PS[half(a), yb, o], RHS[a][:, t, HD:P], RBT[a][:, t, :], start=(t == 0), stop=False,
                                  skip_group_check=True)
                    for a in range(2):
                        pe.matmul(PS[half(a), yb, o], Vp[:, t, half(a)], RKT[a][:, t, :], start=False, stop=False,
                                  skip_group_check=True)

                for n, (step, hh, e) in enumerate(FILLS):
                    if step == "S1":
                        fill("Y", 1)
                    b = fill(step, hh)
                    if n == first_in_yb:
                        pe.wait_ge(S("y_out"), i + 1)
                    if step in ("TA", "TB", "TK", "TV"):
                        src = {"TA": AR[:, 0, :], "TB": B2, "TK": K2, "TV": VTp}[step]
                        if step == "TA":
                            pe.wait_ge(S("p2_ready"), NP2 * i + NP2)
                        if step == "TV":
                            pe.wait_ge(S("vt_ready"), i + 1)
                        if step == "TB":
                            pe.wait_ge(S("b2_ready"), 2 * i + 2)
                        for t in range(NT):
                            ins = pe.transpose(PS[:, b, P * t:P * t + P], src[:, P * t:P * t + P], ident[:, :])
                        ins.then_inc(S("filled"), 1)
                    elif step == "BN":
                        pe.matmul(PS[:, b, :], hones[:, :], RK, start=True, stop=True).then_inc(S("filled"), 1)
                    elif step in ("A0", "A1", "B0", "B1"):
                        if step == "A0":
                            pe.wait_ge(S("r_ready"), i + 1)
                        lhs = (BT if step[0] == "A" else KT)[hh]
                        for q in range(2):
                            t = 2 * int(step[1]) + q
                            ins = pe.matmul(bank(b, 2, 2, P)[:, q, :, :], lhs[:, P * t:P * t + P],
                                            AR[:, :, P * t:P * t + P], start=True, stop=True)
                        ins.then_inc(S("filled"), 1)
                    elif step in products:
                        if step == "Q4":
                            pe.wait_ge(S("z_begun"), 2 * i + hh + 1)
                        mm4(b, products[step][0][hh], products[step][1][hh])
                    elif step == "RP":
                        for t in range(NT):
                            for a in range(2):
                                ins = pe.matmul(PS[half(a), b, P * t:P * t + P], RHS[a][:, t, 0:HD],
                                                RBT[a][:, t, :], start=True, stop=True)
                        ins.then_inc(S("filled"), 1)
                    elif step in ("G", "H"):
                        if step == "G":
                            pe.wait_ge(S("dpc_ready"), i + 1)
                        gate(pe)
                        r = slice(CH * hh, CH * hh + CH)
                        for t in range(NT):
                            o = [PS[half(a), b, P * t:P * t + HD] for a in range(2)]
                            for a in range(2):
                                if step == "G":
                                    ins = pe.matmul(o[a], RHS[a][r, t, 0:HD], Bt[r, t, half(a)], start=True, stop=True)
                                else:
                                    pe.matmul(o[a], Bt[r, t, half(a)], RHS[a][r, t, HD:P], start=True, stop=False)
                            if step == "H":
                                for a in range(2):
                                    ins = pe.matmul(o[a], Kt[r, t, half(a)], Vp[r, t, half(a)], start=False, stop=True)
                        ins.then_inc(S("filled"), 1)
                    elif step[0] == "S":
                        c = int(step[1:])
                        pe.matmul(PS[:, b, 0:P], GT[:, c, :], Hs[:, c - 1, :], start=True, stop=True)\
                            .then_inc(S("filled"), 1)
                        if c <= NT:
                            y_local(c - 1)
                    elif step == "Y":
                        for c in range(1, NCH):
                            if c == 1:
                                pe.wait_ge(S("evac_V"), i * NEV["V"] + evacs(FILL_NO["RP", 0]))
                            if c == NCH - 1:
                                pe.wait_ge(S("evac_V"), i * NEV["V"] + evacs(FILL_NO[f"S{NCH - 2}", 0]))
                            ins = pe.matmul(PS[:, yb, CH * c:CH * c + CH], Hs[:, c - 1, :], Rpp[:, CH * c:CH * c + CH],
                                            start=False, stop=(c == NCH - 1), skip_group_check=True)
                        ins.then_inc(S("filled"), 1)

        GPRE = FIRST["gate"]

        def gn_pe(pe):
            pe.wait_ge(S("evac_A"), NPAIR * NEV["A"])
            pe.wait_ge(S("evac_V"), NPAIR * NEV["V"])
            for j in range(KC):
                if j >= 2:
                    pe.wait_ge(S("gn_centred"), j - 1)
                pe.matmul(PS[:, 4 + j % 2, :], hones[:, :], YT[:, j, :], start=True, stop=True).then_inc(S("gn_summed"), 1)
            for j in range(KC):
                pe.wait_ge(S("gn_squared"), j + 1)
                if j >= 2:
                    pe.wait_ge(S("gn_root"), j - 1)
                else:
                    pe.wait_ge(S("gn_centred"), KC - 1 + j)
                pe.matmul(PS[:, 4 + j % 2, :], hones[:, :], Ysq[:, j, :], start=True, stop=True).then_inc(S("gn_summed"), 1)

        def gn_act(act):
            for j in range(KC):
                act.wait_ge(S("gn_centred"), j + 1)
                act.activation(Ysq[:, j, :], YT[:, j, :], ACT.Square).then_inc(S("gn_squared"), 1)

            for j in range(KC):
                act.wait_ge(S("gn_summed"), KC + j + 1)
                act.activation(Ysd[:, j, :], PS[:, 4 + j % 2, :], ACT.Sqrt, scale=1.0 / HD, bias=gn_eps[:, :])\
                    .then_inc(S("gn_root"), 1)

        def gn_vec(vec):
            for j in range(KC):
                vec.wait_ge(S("gn_summed"), j + 1)
                vec.scalar_tensor_tensor(out=YT[:, j, :], in0=PS[:, 4 + j % 2, :], scalar=-1.0 / HD, in1=YT[:, j, :],
                                         op0=ALU.mult, op1=ALU.add).then_inc(S("gn_centred"), 1)

        def post_vec(vec):
            st = S("post_step")
            for j in range(KC):
                vec.wait_ge(S("gn_root"), j + 1)
                vec.reciprocal(Ysd[:, j, :], Ysd[:, j, :]).then_inc(S("gn_recip"), 1)
            for j in range(KC):
                vec.wait_ge(S("gn_recip"), j + 1)
                vec.tensor_tensor(YT[:, j, :], YT[:, j, :], Ysd[:, j, :], ALU.mult).then_inc(st, 1)
            for j in range(KC):
                vec.wait_ge(st, j + 1)
                vec.tensor_scalar(YT[:, j, :], YT[:, j, :], prm[:, 5, j:j + 1], prm[:, 6, j:j + 1],
                                  ALU.mult, ALU.add).then_inc(st, 1)
            for j in range(KC):
                vec.wait_ge(st, KC + j + 1)
                vec.tensor_tensor(YT[:, j, :], YT[:, j, :], V_[:, j, :], ALU.add).then_inc(st, 1)
            for j in range(KC):
                vec.wait_ge(st, 2 * KC + j + 1)
                vec.tensor_tensor(YT[:, j, :], YT[:, j, :], group_out(vec, GPRE + j), ALU.mult)\
                    .then_inc(S("proj_out_V"), 1)

        def post_pe(pe):
            for j in range(KC):
                bank_free(pe, GPRE + j)
                pe.matmul(PS[:, (GPRE + j) % NBANK, :], g2s[:, P * j:P * j + P], sg1[:, :], start=True, stop=True)\
                    .then_inc(S("proj_filled"), 1)

            project_tok(pe, FIRST["rwo"], UNITS.index("rwo"), YT, lambda e, k: group_evacuated(e, GPRE + k))

        def x_back(vec, t):
            vec.wait_ge(S("x_again"), 16 * NT)


        def mem_pe(pe):
            norm_pe(pe, "mem", mem_tn)

            def ready(e, k):
                xT_there(e, "mem", k)
            u = UNITS.index("memkv")
            project_T(pe, FIRST["memk"], u, mem_xT, M, ready)
            project_tok(pe, FIRST["memv"], u + 2, mem_xT, lambda e, k: None, tiles=M // P)

        def mem_act(act):
            act.wait_ge(S("filled"), NPAIR * NFILL)
            norm_act(act, "mem", mem_rows, mem_tn, lambda e, t: e.wait_ge(S("mem_in"), 16 * (M // P)))
            xT_evac(act, "mem", mem_xT, 0)
            evac_T(act, FIRST["memk"], memK, n=M)
            evac_tok(act, FIRST["memv"], memV, tiles=M // P)

        def mem_vec(vec):
            norm_vec(vec, "mem", mem_rows, mem_tn)
            xT_evac(vec, "mem", mem_xT, 1)

        tnX = at(12, [NT, C])
        xTX = at(16, [KC, T])
        qT = at(20, [KC, T])
        oT = at(24, [KC, T])
        prob = [at(12 + x, [NT, M]) for x in range(2)]
        probT = [at(14 + x, [M // P, T]) for x in range(2)]
        xmax, xsum = sb("xmax", [P, 2, NT]), sb("xsum", [P, 2, NT])

        def h_tile_ready(name):
            return lambda e, t: group_evacuated(e, FIRST[name] + NT + t)

        def cross_pe(pe, l):
            xq, xv, xo = f"xq{l}", f"xv{l}", f"xo{l}"
            norm_pe(pe, f"cross{l}", tnX)
            project_T(pe, FIRST[xq], UNITS.index(xq), xTX, T, lambda e, k: xT_there(e, f"cross{l}", k))

            def scores(x):
                n = XH * l + x
                group_evacuated(pe, FIRST[xq] + 2 * x + 1)
                for b in range(2):
                    if n >= 1:
                        pe.wait_ge(S("x_exp"), NT * (n - 1) + 2 * b + 2)
                    for t in (2 * b, 2 * b + 1):
                        for k in range(2):
                            ins = pe.matmul(PS[:, 4 + b, M * (t % 2):M * (t % 2) + M],
                                            qT[:, 2 * x + k, P * t:P * t + P], memK[:, 2 * x + k, :],
                                            start=(k == 0), stop=(k == 1))
                    ins.then_inc(S("x_scored"), 1)

            scores(0)
            for x in range(XH):
                n = XH * l + x
                if x + 1 < XH:
                    scores(x + 1)
                for m in range(2):
                    if n >= 1:
                        pe.wait_ge(S("x_probT"), 2 * (n - 1) + m + 1)
                    if x == 0:
                        xT_there(pe, f"cross{l}", 6 + m)
                    for t in range(NT):
                        pe.wait_ge(S("x_prob"), NT * n + t + 1)
                        ins = pe.transpose(PS[:, 6 + m, P * t:P * t + P], prob[x % 2][:, t, P * m:P * m + P],
                                           ident[:, :])
                    ins.then_inc(S("x_turned"), 1)
                for m in range(2):
                    pe.wait_ge(S("x_probT"), 2 * n + m + 1)
                    for v in range(2):
                        g = FIRST[xv] + 2 * x + v
                        if m == 0:
                            bank_free(pe, g)
                        ins = pe.matmul(PS[:, g % NBANK, :], memV[:, m, XD * x + P * v:XD * x + P * v + P],
                                        probT[x % 2][:, m, :], start=(m == 0), stop=(m == 1))
                        if m == 1:
                            ins.then_inc(S("proj_filled"), 1)
            project_tok(pe, FIRST[xo], UNITS.index(xo), oT, lambda e, k: group_evacuated(e, FIRST[xv] + k))

        def cross_act(act, l, before):
            norm_act(act, f"cross{l}", h, tnX, h_tile_ready(before))
            xT_evac(act, f"cross{l}", xTX, 0)
            evac_T(act, FIRST[f"xq{l}"], qT)

            def out(x):
                for v in range(2):
                    act.activation(oT[:, 2 * x + v, :], group_out(act, FIRST[f"xv{l}"] + 2 * x + v), ACT.Copy)\
                        .then_inc(S("proj_out_A"), 1)

            for x in range(XH):
                n = XH * l + x
                if x == 0:
                    act.wait_ge(S("norm_turned"), TPOSE0[f"cross{l}"] + KC)
                if x >= 2:
                    act.wait_ge(S("x_turned"), 2 * (n - 1))
                for t in range(NT):
                    act.wait_ge(S("x_nmax"), 2 * n + t // 2 + 1)
                    act.activation(prob[x % 2][:, t, :], PS[:, 4 + t // 2, M * (t % 2):M * (t % 2) + M], ACT.Exp,
                                   bias=xmax[:, x % 2, t:t + 1], scale=XSCALE,
                                   accum_out=xsum[:, x % 2, t:t + 1]).then_inc(S("x_exp"), 1)
                if x >= 1:
                    out(x - 1)
            out(XH - 1)

        def cross_vec(vec, l):
            norm_vec(vec, f"cross{l}", h, tnX)
            xT_evac(vec, f"cross{l}", xTX, 1)

            def maxima(x):
                n = XH * l + x
                if x >= 2:
                    vec.wait_ge(S("x_exp"), NT * (n - 1))
                for b in range(2):
                    vec.wait_ge(S("x_scored"), 2 * n + b + 1)
                    m = xmax[:, x % 2, 2 * b:2 * b + 2]
                    vec.tensor_reduce(m, bank(4 + b, 2, M), AX.X, ALU.max).then_inc(S("x_max"), 1)
                    vec.wait_ge(S("x_max"), 2 * n + b + 1)
                    vec.tensor_scalar(m, m, -XSCALE, None, ALU.mult).then_inc(S("x_nmax"), 1)

            maxima(0)
            for x in range(XH):
                n = XH * l + x
                vec.wait_ge(S("x_exp"), NT * n + NT)
                vec.reciprocal(xsum[:, x % 2, :], xsum[:, x % 2, :]).then_inc(S("x_recip"), 1)
                vec.wait_ge(S("x_recip"), n + 1)
                for t in range(NT):
                    vec.tensor_scalar(prob[x % 2][:, t, :], prob[x % 2][:, t, :], xsum[:, x % 2, t:t + 1], None,
                                      ALU.mult).then_inc(S("x_prob"), 1)
                if x + 1 < XH:
                    maxima(x + 1)
                for m in range(2):
                    vec.wait_ge(S("x_turned"), 2 * n + m + 1)
                    if x >= 2:
                        vec.wait_ge(S("proj_filled"), FIRST[f"xv{l}"] + 2 * (x - 1))
                    vec.tensor_copy(probT[x % 2][:, m, :], PS[:, 6 + m, :]).then_inc(S("x_probT"), 1)
            add_to_h(vec, FIRST[f"xo{l}"])

        tnS = at(0, [NT, C])
        oTS = at(0, [KC, T])
        xTS = at(4, [KC, T])
        qTS = at(8, [KC, T])
        kTS = at(12, [KC, T])
        vS = at(16, [NT, C])
        NBUF = 4
        fail = [at(o, [T + 8]) for o in (20, 20.625, 4, 4.625)]
        beta = [at(o, [T]) for o in (21.5, 22, 5.25, 5.75)]
        attT = [at(22.5 + 2 * a, [NT, T]) for a in range(2)]
        qs = [[at(o + 0.5 * a, [T]) for a in range(2)] for o in (32, 6.25)]
        vs = at(33, [NT, P])
        NU = 2 * NT

        def sb_proj_pe(pe):
            norm_pe(pe, "mix1", tnS)
            project_T(pe, FIRST["sq"], UNITS.index("sqkv"), xTS, T, lambda e, k: xT_there(e, "mix1", k))
            project_T(pe, FIRST["sk"], UNITS.index("sqkv") + 2, xTS, T, lambda e, k: None)
            project_tok(pe, FIRST["sv"], UNITS.index("sqkv") + 4, xTS, lambda e, k: None)

        def sb_proj_act(act):
            norm_act(act, "mix1", h, tnS, lambda e, t: e.wait_ge(S("h_moe0"), t + 1))
            xT_evac(act, "mix1", xTS, 0)
            evac_T(act, FIRST["sq"], qTS)
            evac_T(act, FIRST["sk"], kTS)
            evac_tok(act, FIRST["sv"], vS)

        def two_by_two(eng, body):
            body(0, 0)
            with eng.Fori(0, NPAIR // 2 - 1) as j:
                body(2 * j + 1, 1)
                body(2 * j + 2, 0)
            body(NPAIR - 1, 1)

        def is_first(i):
            return isinstance(i, int) and i == 0

        def is_last(i):
            return isinstance(i, int) and i == NPAIR - 1

        def sb_pool(pool):
            def body(i, parity):
                for n in range(NU):
                    nn = P * (n % NT + 1)
                    pool.wait_ge(S("sb_sig"), 2 * (NU * i + n) + 1)
                    gate(pool)
                    f = fail[n % NBUF][:, T - P:T]
                    pool.affine_select(out=f, in_=f, compare_op=ALU.is_gt, fill=1.0, base=0, pattern=[[-1, P]],
                                       channel_multiplier=1).then_inc(S("sb_cut"), 1)
                    pool.wait_ge(S("sb_sig"), 2 * (NU * i + n) + 2)
                    gate(pool)
                    b = beta[n % NBUF][:, nn - P:nn]
                    pool.affine_select(out=b, in_=b, compare_op=ALU.is_gt, fill=0.0, base=0, pattern=[[-1, P]],
                                       channel_multiplier=1).then_inc(S("sb_cut"), 1)
                    if n == 3:
                        pool.wait_ge(S("sb_summed"), i + 1)
                        pool.tensor_copy(vs, vS.rearrange("p t (i n) -> p t i n", i=NPAIR)[:, :, i, :])\
                            .then_inc(S("sb_v_copied"), 1)

            group_evacuated(pool, FIRST["sv"] + 7)
            two_by_two(pool, body)

        def sb_act(act):
            def copy_q(j, parity):
                for a in range(2):
                    act.activation(qs[parity][a][half(a), :], qTS[half(a), j, :], ACT.Copy)\
                        .then_inc(S("sb_q_copied"), 1)

            def out(j):
                act.wait_ge(S("sb_summed"), j + 2)
                act.activation(oTS[:, j, :], PS[:, 6, :], ACT.Copy).then_inc(S("sb_oT"), 1)

            def body(i, parity):
                for n in range(NU):
                    nn = P * (n % NT + 1)
                    act.wait_ge(S("sb_scored"), NU * i + n + 1)
                    act.wait_ge(S("sb_turned"), NU * i + n + 1)
                    act.activation(fail[n % NBUF][:, T - nn:T], PS[:, n % NT, 0:nn], ACT.Sigmoid, scale=-HD ** -0.5)\
                        .then_inc(S("sb_sig"), 1)
                    act.activation(beta[n % NBUF][:, 0:nn], PS[:, n % NT, 0:nn], ACT.Sigmoid, scale=HD ** -0.5)\
                        .then_inc(S("sb_sig"), 1)
                    if n == 2 and not is_first(i):
                        out(i - 1)
                    if n == 3 and not is_last(i):
                        copy_q(i + 1, 1 - parity)
            act.nop().then_inc(S("sb_oT"), 1)
            act.wait_ge(S("sb_ones"), NBUF + 4)
            copy_q(0, 0)
            two_by_two(act, body)
            out(NPAIR - 1)

        def sb_vec(vec):
            group_evacuated(vec, FIRST["sv"] + 7)
            for b in range(NBUF):
                vec.memset(fail[b][:, T:T + 1], 1.0).then_inc(S("sb_ones"), 1)
            for parity in range(2):
                for a in range(2):
                    vec.memset(qs[parity][a][half(1 - a), :], 0.0).then_inc(S("sb_ones"), 1)
            vec.wait_ge(S("sb_ones"), NBUF + 4)
            with vec.Fori(0, NPAIR) as i:
                for n in range(NU):
                    nn = P * (n % NT + 1)
                    f, b = fail[n % NBUF], beta[n % NBUF]
                    vec.wait_ge(S("sb_cut"), 2 * (NU * i + n) + 2)
                    rev = f[:, T - nn:T][:, ::-1]
                    vec.tensor_tensor_scan(rev, rev, rev, 1.0, ALU.mult, ALU.min).then_inc(S("sb_scan"), 1)
                    vec.wait_ge(S("sb_scan"), NU * i + n + 1)
                    vec.tensor_tensor(b[:, 0:nn], b[:, 0:nn], f[:, T - nn + 1:T + 1], ALU.mult).then_inc(S("sb_att"), 1)
                    if n >= 1:
                        sb_turn_out(vec, i, n - 1)
                sb_turn_out(vec, i, NU - 1)

        def sb_turn_out(vec, i, n):
            t, hh = n % NT, n // NT
            vec.wait_ge(S("sb_turned"), NU * i + n + 1 + NBUF)
            vec.wait_ge(S("sb_summed"), i + 1)
            vec.tensor_copy(attT[hh][:, 0:t + 1, P * t:P * t + P], bank(4 + n % 2, NT, P)[:, 0:t + 1, :])\
                .then_inc(S("sb_attT"), 1)

        def sb_pe(pe):
            def score(j, parity, n):
                t = n % NT
                pe.matmul(PS[:, t, 0:P * (t + 1)], qs[parity][n // NT][:, P * t:P * t + P], kTS[:, j, 0:P * (t + 1)],
                          start=True, stop=True).then_inc(S("sb_scored"), 1)

            def body(i, parity):
                for n in range(NU):
                    t, hh = n % NT, n // NT
                    pe.wait_ge(S("sb_att"), NU * i + n + 1)
                    if n >= 2:
                        pe.wait_ge(S("sb_attT"), NU * i + n - 1)
                    for s in range(t + 1):
                        ins = pe.transpose(PS[:, 4 + n % 2, P * s:P * s + P], beta[n % NBUF][:, P * s:P * s + P],
                                           ident[:, :])
                    ins.then_inc(S("sb_turned"), 1)
                    pe.wait_ge(S("sb_sig"), 2 * (NU * i + n) + 2)
                    if n + NT < NU:
                        score(i, parity, n + NT)
                    elif not is_last(i):
                        pe.wait_ge(S("sb_q_copied"), 2 * i + 4)
                        score(i + 1, 1 - parity, n + NT - NU)
                pe.wait_ge(S("sb_attT"), NU * i + NU)
                pe.wait_ge(S("sb_v_copied"), i + 1)
                pe.wait_ge(S("sb_oT"), i + 1)
                gate(pe)
                for s in range(NT):
                    for a in range(2):
                        ins = pe.matmul(PS[half(a), 6, P * s:T], vs[:, s, half(a)], attT[a][:, s, P * s:T],
                                        start=(s == 0), stop=(s == NT - 1))
                ins.then_inc(S("sb_summed"), 1)

            group_evacuated(pe, FIRST["sv"] + 7)
            pe.nop().then_inc(S("sb_turned"), NBUF)
            pe.nop().then_inc(S("sb_summed"), 1)
            pe.wait_ge(S("sb_q_copied"), 2)
            for n in range(NT):
                score(0, 0, n)
            two_by_two(pe, body)
            pe.wait_ge(S("sb_oT"), NPAIR + 1)
            project_tok(pe, FIRST["so"], UNITS.index("so"), oTS, lambda e, k: None)

        tnE = at(12, [NT, C])
        xTE = at(16, [KC, T])
        ringS = ring[:, :, :, :].rearrange("p r k n -> p (r k n)")

        def slot(p, a):
            return arena[:, 6144 * a:6144 * a + 6144] if p == 0 else ringS[:, 6144 * a:6144 * a + 6144]

        w13 = [[split(slot(p, a)[:, 0:4096], [2, KC, F]) for a in range(2)] for p in range(2)]
        w2e = [[split(slot(p, a)[:, 4096:6144], [2, C]) for a in range(2)] for p in range(2)]
        w13x = [at(12 + 4 * a, [2, KC, F]) for a in range(2)]
        xg = [at(20 + p, [C]) for p in range(2)]
        xgT = [at(22 + p, [KC, P]) for p in range(2)]
        ye = [at(24 + p, [C]) for p in range(2)]
        sig = at(27, [F])
        hid = at(27.25, [F])
        hidT = at(27.5, [2, P])
        yg = [at(12 + n, [C]) for n in range(8)]
        wge = at(26.25, [KC, G + NE])
        bge = at(26.75, [G + NE])
        su = masks[:, 0, :]
        lg = at(27, [NT, G + NE])
        mel = at(27.25, [NT, NE])
        mel2 = at(27.375, [NT, NE])
        O1 = at(27.5, [NT, NE])
        O2 = at(27.625, [NT, NE])
        OO = at(27.75, [NT + 1, NE])
        sc = at(27.875, [NT, NE])
        rk = at(32, [NT + 1, NE])
        cmp_ = at(32.25, [NT * NE * 7])
        O12 = at(27.5, [2 * NT, NE])
        tmp = at(33.25, [NT, NE])
        tmp2 = at(33.375, [2 * NT, NE])
        lT = at(32.25, [T])
        cum = cmp_[:, 0:(NT + 1) * NE].rearrange("p (t e) -> p t e", t=NT + 1)
        OS = [at(33.75 + 0.125 * n, [P]) for n in range(2)]
        OB = [at(26.875 + 0.03125 * n, [32]) for n in range(2)]
        iob = hones[:, :]
        w32 = masks[:, 1, 64:96]
        e2 = masks[:, 1, 96:128]
        ov = masks[:, 2, 0:96].rearrange("p (a e) -> p a e", a=3)
        thr = masks[:, 2, 96:103]
        ep = masks[:, 4, 32:64]
        tokid = masks[:, 2, 104:108]
        c4 = masks[:, 3, 0:48].rearrange("p (n t) -> p n t", n=12)
        gmax, gsum, v1, v2, s1, ed, den, wA, wB = [c4[:, n, :] for n in range(9)]
        bs = masks[:, 4, 64:88].rearrange("p (n t) -> p n t", n=6)
        b8, s8, c8 = [masks[:, 4, 64 + 8 * n:72 + 8 * n] for n in range(3)]
        r8, o8, e8, p8 = [masks[:, 4, 8 * n:8 * n + 8] for n in range(4)]
        q8, g8, h8, n8 = [masks[:, 4, 88 + 8 * n:96 + 8 * n] for n in range(4)]
        overf = masks[:, 3, 64:96]
        pos = sb("pos", [P, NT, 2], I32)
        NPE = NE // 2
        NCOL = NPE + NOVER
        table = sb("table", [P, NCOL], I32)
        over = sb("over", [P, 32], I32)
        xi = [sb(f"xi{a}", [P, 1], I32) for a in range(2)]
        NSTEP = 76

        def moe_constants(pool):
            pool.wait_ge(S("gn_root"), KC)
            pool.iota(iob, [[1, P]], base=0, channel_multiplier=0,
                      allow_small_or_imprecise_dtypes=True).then_inc(S("iota_ready"), 1)
            pool.iota(w32[:, :], [[-1, NE]], base=NE, channel_multiplier=0,
                      allow_small_or_imprecise_dtypes=True).then_inc(S("iota_ready"), 1)
            pool.iota(thr[:, :], [[BLK, 7]], base=BLK, channel_multiplier=0,
                      allow_small_or_imprecise_dtypes=True).then_inc(S("iota_ready"), 1)
            for m, pattern in ((e2, [[2, NPE], [0, 2]]), (ep, [[0, NPE], [BLK, 2]])):
                pool.iota(m.rearrange("p (a b) -> p a b", b=2), pattern, base=0, channel_multiplier=0,
                          allow_small_or_imprecise_dtypes=True).then_inc(S("iota_ready"), 1)
            pool.iota(tokid[:, :], [[P, NT]], base=0, channel_multiplier=1,
                      allow_small_or_imprecise_dtypes=True).then_inc(S("iota_ready"), 1)

            pool.memset(su[:, :], 1.0).then_inc(S("iota_ready"), 1)
            pool.wait_ge(S("iota_ready"), 7)
            pool.affine_select(out=su[:, :], in_=su[:, :], compare_op=ALU.is_gt, fill=0.0, base=0, pattern=[[1, P]],
                               channel_multiplier=-1).then_inc(S("iota_ready"), 1)

        def experts(w, l, k):
            return w[l].rearrange("g e (p k) f -> (g e) p k f", k=k)

        def moe_route_loads(sp, l):
            sp.wait_ge(S("proj_filled"), FIRST[f"xo{l}"] + 8)
            sp.dma_start(wge[:, :, 0:G], A["moe_wg"][l].rearrange("(p k) n -> p k n", k=KC)).then_inc(S("route_in"), 16)
            sp.dma_start(wge[:, :, G:], A["moe_we"][l].rearrange("(p k) n -> p k n", k=KC)).then_inc(S("route_in"), 16)
            sp.dma_start(bge[:, 0:G], bcast(A["moe_bg"][l])).then_inc(S("route_in"), 16)
            sp.dma_start(bge[:, G:], bcast(A["moe_be"][l])).then_inc(S("route_in"), 16)

        def moe_route_pe(pe, l):
            norm_pe(pe, f"ffn{l}", tnE)
            for k in range(KC):
                xT_there(pe, f"ffn{l}", k)
            pe.wait_ge(S("route_in"), 64 * (l + 1))
            for k in range(KC):
                a = k % 2
                ins = pe.matmul(PS[HD * a:HD * a + G + NE, 5, :], wge[:, k, :], xTE[:, k, :],
                                start=(k < 2), stop=(k >= KC - 2))
            ins.then_inc(S("logits"), 1)
            pe.wait_ge(S("logits_out_a"), l + 1)
            pe.wait_ge(S("logits_out_v"), 2 * l + 2)
            for t in range(NT):
                ins = pe.matmul(PS[:, 4, 64 * t:64 * t + G + NE], lT[:, P * t:P * t + P], ident2[:, 0:G + NE],
                                start=True, stop=True)
            ins.then_inc(S("logits"), 1)
            pe.wait_ge(S("chosen"), l + 1)
            pe.wait_ge(S("iota_ready"), 8)
            pe.matmul(PS[:, 4, 0:(NT + 1) * NE], su[:, :], OO.rearrange("p t e -> p (t e)"), start=True, stop=False)
            pe.matmul(PS[:, 4, 0:(NT + 1) * NE], ones[:, :], cum.rearrange("p t e -> p (t e)"), start=False, stop=True)\
                .then_inc(S("ranked"), 1)
            for n in range(8):
                pe.wait_ge(S("onehots"), 2 * (8 * l + n) + 2)
                pe.matmul(PS[:, 5, 0:NCOL], OS[n % 2], OB[n % 2][:, 0:NCOL], start=(n == 0), stop=(n == 7))\
                    .then_inc(S("tabled"), 1)

        def moe_route_act(act, l):
            norm_act(act, f"ffn{l}", h, tnE, h_tile_ready(f"xo{l}"))
            xT_evac(act, f"ffn{l}", xTE, 0)
            act.wait_ge(S("logits"), 2 * l + 1)
            act.wait_ge(S("logits_out_v"), 2 * l + 1)
            act.activation(lT[HD:HD + G + NE, :], PS[HD:HD + G + NE, 5, :], ACT.Copy).then_inc(S("logits_out_a"), 1)
            act.wait_ge(S("route_a"), 2 * l + 1)
            act.activation(sc[:, :, 0:G], mel2[:, :, 0:G], ACT.Exp).then_inc(S("route_exp"), 1)
            act.wait_ge(S("route_a"), 2 * l + 2)
            act.activation(ed, ed, ACT.Exp).then_inc(S("route_exp"), 1)

        def moe_route_vec(vec, l):
            norm_vec(vec, f"ffn{l}", h, tnE)
            xT_evac(vec, f"ffn{l}", xTE, 1)
            step = S("route_step")
            done = [ROUTE_STEPS * l]

            def do(ins):
                ins.then_inc(step, 1)
                done[0] += 1
                vec.wait_ge(step, done[0])

            def wide(m, k):
                return m.unsqueeze(2).to_broadcast([P, NT, k])

            vec.wait_ge(S("iota_ready"), 8)
            vec.memset(lT, 0.0).then_inc(S("logits_out_v"), 1)
            vec.wait_ge(S("logits_out_v"), 2 * l + 1)
            vec.wait_ge(S("logits"), 2 * l + 1)
            vec.tensor_copy(lT[0:G + NE, :], PS[0:G + NE, 5, :]).then_inc(S("logits_out_v"), 1)
            vec.wait_ge(S("logits"), 2 * l + 2)
            do(vec.tensor_tensor(lg, PS[:, 4, 0:256].rearrange("p (t n) -> p t n", t=NT)[:, :, 0:G + NE],
                                 bge.unsqueeze(1).to_broadcast([P, NT, G + NE]), ALU.add))
            gl, el = lg[:, :, 0:G], lg[:, :, G:]
            do(vec.tensor_reduce(gmax, gl, AX.X, ALU.max))
            vec.tensor_tensor(mel2[:, :, 0:G], gl, wide(gmax, G), ALU.subtract).then_inc(S("route_a"), 1)
            do(vec.tensor_tensor(mel[:, :, 0:G], gl, wide(gmax, G), ALU.is_equal))
            do(vec.tensor_tensor(mel[:, :, 0:G], mel[:, :, 0:G], w32[:, 0:G].unsqueeze(1).to_broadcast([P, NT, G]),
                                 ALU.mult))
            do(vec.tensor_reduce(s1, mel[:, :, 0:G], AX.X, ALU.max))
            do(vec.tensor_tensor(mel[:, :, 0:G], mel[:, :, 0:G], wide(s1, G), ALU.is_equal))
            vec.wait_ge(S("route_exp"), 2 * l + 1)
            do(vec.tensor_reduce(gsum, sc[:, :, 0:G], AX.X, ALU.add))
            do(vec.tensor_scalar(tmp[:, :, 0:G], mel[:, :, 0:G], -1.0, BIG, ALU.add, ALU.mult))
            for t in range(NT):
                ins = vec.tensor_tensor(mel[:, t, :].rearrange("p (g e) -> p g e", g=G),
                                        el[:, t, :].rearrange("p (g e) -> p g e", g=G),
                                        tmp[:, t, 0:G].unsqueeze(2).to_broadcast([P, G, E]), ALU.add)
                if t == NT - 1:
                    do(ins)
            for O, v, m in ((O1, v1, mel), (O2, v2, mel2)):
                do(vec.tensor_reduce(v, m, AX.X, ALU.max))
                do(vec.tensor_tensor(O, m, wide(v, NE), ALU.is_equal))
                do(vec.tensor_tensor(O, O, w32[:, :].unsqueeze(1).to_broadcast([P, NT, NE]), ALU.mult))
                do(vec.tensor_reduce(s1, O, AX.X, ALU.max))
                do(vec.tensor_tensor(O, O, wide(s1, NE), ALU.is_equal))
                if O is O1:
                    do(vec.scalar_tensor_tensor(out=mel2, in0=O1, scalar=-2 * BIG, in1=mel, op0=ALU.mult, op1=ALU.add))
            do(vec.memset(OO[:, NT, :], 0.0))
            do(vec.memset(cum[:, 0, :], 0.0))
            do(vec.tensor_tensor(OO[:, 0:NT, :], O1, O2, ALU.add))
            for t in range(NT):
                ins = vec.tensor_tensor(cum[:, t + 1, :], cum[:, t, :], OO[:, t, :], ALU.add)
                if t < NT - 1:
                    do(ins)
            ins.then_inc(S("chosen"), 1)
            vec.tensor_tensor(ed, v2, v1, ALU.subtract).then_inc(S("route_a"), 1)

            def of_choice(dst, m, by_tile=False):
                if by_tile:
                    v = [x.rearrange("p (k t) e -> p k t e", k=2) for x in (tmp2, O12)]
                    do(vec.tensor_tensor(v[0], v[1], m.unsqueeze(1).to_broadcast([P, 2, NT, NE]), ALU.mult))
                else:
                    do(vec.tensor_tensor(tmp2, O12, m.unsqueeze(1).to_broadcast([P, 2 * NT, NE]), ALU.mult))
                do(vec.tensor_reduce(dst, tmp2, AX.X, ALU.add))

            of_choice(e8, e2)
            of_choice(p8, ep)
            do(vec.tensor_scalar(h8, e8, 0.5, None, ALU.mult))
            vec.wait_ge(S("ranked"), l + 1)
            do(vec.tensor_copy(rk, PS[:, 4, 0:(NT + 1) * NE].rearrange("p (t e) -> p t e", t=NT + 1)))
            count = rk[:, NT, :]
            c3 = cmp_.rearrange("p (a b) -> p a b", b=7)
            th = thr[:, :].unsqueeze(1)
            do(vec.tensor_tensor(c3[:, 0:NE, :], count.unsqueeze(2).to_broadcast([P, NE, 7]),
                                 th.to_broadcast([P, NE, 7]), ALU.is_gt))
            do(vec.tensor_reduce(ov[:, 0, :], c3[:, 0:NE, :], AX.X, ALU.add))
            do(vec.tensor_tensor_scan(ov[:, 1, :], ones[:, 0:NE], ov[:, 0, :], 0.0, ALU.mult, ALU.add))
            do(vec.tensor_tensor(ov[:, 2, :], ov[:, 1, :], ov[:, 0, :], ALU.subtract))
            do(vec.tensor_scalar(ov[:, 2, :], ov[:, 2, :], float(NE - 1), None, ALU.add))
            of_choice(r8, rk[:, 0:NT, :], True)
            of_choice(o8, ov[:, 2, :])
            do(vec.tensor_tensor(c3[:, 0:8, :], r8.unsqueeze(2).to_broadcast([P, 8, 7]),
                                 th.to_broadcast([P, 8, 7]), ALU.is_ge))
            do(vec.tensor_reduce(q8, c3[:, 0:8, :], AX.X, ALU.add))
            do(vec.scalar_tensor_tensor(out=s8, in0=q8, scalar=-float(BLK), in1=r8, op0=ALU.mult, op1=ALU.add))
            do(vec.tensor_tensor(b8, q8, o8, ALU.add))
            do(vec.tensor_scalar(g8, q8, 0.0, None, ALU.is_gt))
            do(vec.tensor_scalar(c8, b8, -float(NPE), None, ALU.add))
            for m, first in ((b8, e8), (c8, h8)):
                do(vec.tensor_tensor(m, m, first, ALU.subtract))
                do(vec.tensor_tensor(m, m, g8, ALU.mult))
                do(vec.tensor_tensor(m, m, first, ALU.add))
            do(vec.tensor_scalar(n8, g8, -1.0, 1.0, ALU.mult, ALU.add))
            do(vec.tensor_tensor(n8, n8, p8, ALU.mult))
            do(vec.tensor_tensor(s8, s8, n8, ALU.add))
            if l:
                vec.wait_ge(S("yg_in3"), 32)
            do(vec.scalar_tensor_tensor(out=c4[:, 9:11, :], in0=bs[:, 0:2, :], scalar=float(BLK), in1=bs[:, 2:4, :],
                                        op0=ALU.mult, op1=ALU.add))
            vec.tensor_copy(pos[:, :, :].rearrange("p t k -> p k t"), c4[:, 9:11, :]).then_inc(S("pos_known"), 1)
            for m in range(8):
                k, t = m // NT, m % NT
                if m >= 2:
                    vec.wait_ge(S("tabled"), 8 * l + m - 1)
                vec.tensor_scalar(OS[m % 2], iob, bs[:, 2 + k, t:t + 1], None, ALU.is_equal)\
                    .then_inc(S("onehots"), 1)
                vec.tensor_scalar(OB[m % 2], iob[:, 0:32], bs[:, 4 + k, t:t + 1], tokid[:, t:t + 1], ALU.is_equal, ALU.mult)\
                    .then_inc(S("onehots"), 1)
            vec.wait_ge(S("tabled"), 8 * l + 8)
            vec.tensor_copy(table[:, :], PS[:, 5, 0:NCOL]).then_inc(S("table_ready"), 1)
            c4_ = cmp_[:, 0:16 * NE].rearrange("p (a b) -> p a b", b=NE)
            do(vec.tensor_tensor(c4_, ov[:, 1, :].unsqueeze(1).to_broadcast([P, 16, NE]),
                                 iob[:, 0:16].unsqueeze(2).to_broadcast([P, 16, NE]), ALU.is_le))
            do(vec.tensor_reduce(overf[:, 0:16], c4_, AX.X, ALU.add))
            do(vec.tensor_scalar(overf[:, 0:16], overf[:, 0:16], float(NE - 1), None, ALU.min))
            do(vec.tensor_copy(overf[:, 16:17], ov[:, 1, NE - 1:NE]))
            vec.tensor_copy(over[:, 0:17], overf[:, 0:17]).then_inc(S("over_known"), 1)
            vec.wait_ge(S("route_exp"), 2 * l + 2)
            do(vec.tensor_scalar(den, ed, 1.0, None, ALU.add))
            do(vec.tensor_tensor(den, den, gsum, ALU.mult))
            do(vec.reciprocal(wA, den))
            do(vec.tensor_tensor(wB, wA, ed, ALU.mult))
            assert done[0] == ROUTE_STEPS * (l + 1), done[0] - ROUTE_STEPS * l
        ROUTE_STEPS = 65

        def moe_rows_out(sp, l):
            for t in range(NT):
                sp.wait_ge(S("norm_rows"), TILE0[f"ffn{l}"] + t + 1)
                sp.dma_start(scratch["rows"][P * t:P * t + P, :], tnE[:, t, :]).then_inc(S("rows_out"), 16)

        def load_up(sp, l, e, w, sem):
            sp.dma_start(w[:, 0, :, :], experts(A["moe_w1"], l, KC)[e]).then_inc(sem, 16)
            sp.dma_start(w[:, 1, :, :], experts(A["moe_w3"], l, KC)[e]).then_inc(sem, 16)

        def load_down(sp, l, e, w, sem):
            sp.dma_start(w, experts(A["moe_w2"], l, 2)[e]).then_inc(sem, 16)

        def load_pair(sp, l, n, p):
            for a in range(2):
                load_up(sp, l, 2 * n + a, w13[p][a], S(f"w13_in{p}"))
            for a in range(2):
                load_down(sp, l, 2 * n + a, w2e[p][a], S(f"w2_in{p}"))

        def moe_first_loads(sp, l):
            sp.wait_ge(S("proj_filled"), FIRST["so" if l else "rwo"] + 8)
            load_pair(sp, l, 0, 0)

        def moe_loads(sp, l):
            sp.wait_ge(S("proj_filled"), FIRST[f"xo{l}"] + 8)
            load_pair(sp, l, 1, 1)
            sp.wait_ge(S("rows_out"), 16 * NT * (l + 1))
            sp.wait_ge(S("norm_turned"), TPOSE0[f"ffn{l}"] + KC)
            sp.wait_ge(S("logits"), 2 * l + 1)
            for a in range(2):
                load_up(sp, l, 4 + a, w13x[a], S("w13x_in"))

            def up_weights(n, p):
                for a in range(2):
                    load_up(sp, l, 2 * n + a, w13[p][a], S(f"w13_in{p}"))

            def down_weights(n, p):
                sp.wait_ge(S("down_done"), NPE * l + n - 1)
                for a in range(2):
                    load_down(sp, l, 2 * n + a, w2e[p][a], S(f"w2_in{p}"))

            def two_pairs(j, last=False):
                down_weights(2 * j, 0)
                sp.wait_ge(S("up_done"), NPE * l + 2 * j)
                up_weights(2 * j + 1, 1)
                down_weights(2 * j + 1, 1)
                if not last:
                    sp.wait_ge(S("up_done"), NPE * l + 2 * j + 1)
                    up_weights(2 * j + 2, 0)

            sp.wait_ge(S("up_done"), NPE * l + 1)
            up_weights(4, 0)
            down_weights(2, 0)
            sp.wait_ge(S("up_done"), NPE * l + 2)
            up_weights(3, 1)
            down_weights(3, 1)
            with sp.Fori(2, NPE // 2 - 1) as j:
                two_pairs(j)
            two_pairs(NPE // 2 - 1, True)

        def gather(pool, p, rows):
            return pool.indirect_dma_start(out=xg[p][0:rows, :], out_offset=None, in_=scratch["rows"],
                                           in_offset=bass.IndirectOffsetOnAxis(ap=xi[p][0:rows, 0:1], axis=0))

        def moe_pool(pool, l):
            pool.wait_ge(S("table_ready"), l + 1)
            pool.wait_ge(S("rows_out"), 16 * NT * (l + 1))
            with pool.Fori(0, NPE // 2) as j:
                for p in range(2):
                    pool.wait_ge(S(f"xg_free{p}"), (NPE // 2 + 1) * l + j + 1)
                    pool.tensor_copy(xi[p][:, :], table[:, bass.ds(2 * j + p, 1)]).then_inc(S(f"xi_ready{p}"), 1)
                    pool.wait_ge(S(f"xi_ready{p}"), NPE // 2 * l + j + 1)
                    gate(pool)
                    gather(pool, p, P).then_inc(S(f"xg_in{p}"), 16)

        def moe_combine_pool(pool, l):
            pool.wait_ge(S("pos_known"), l + 1)
            for p in range(2):
                pool.wait_ge(S(f"ye_out{p}"), 16 * (NPE // 2 + 1) * (l + 1))
            pool.wait_ge(S("over_done"), l + 1)
            pool.wait_ge(S("spare_filled"), 32)
            for t in range(NT):
                for k in range(2):
                    pool.indirect_dma_start(out=yg[2 * t + k], out_offset=None, in_=scratch["blocks"],
                                            in_offset=bass.IndirectOffsetOnAxis(ap=pos[:, t, k:k + 1], axis=0))\
                        .then_inc(S(f"yg_in{t}"), 16)

        def moe_combine_vec(vec, l):
            for t in range(NT):
                vec.wait_ge(S(f"yg_in{t}"), 32 * (l + 1))
                for k, w in enumerate((wA, wB)):
                    if k:
                        vec.wait_ge(S("h_half"), NT * l + t + 1)
                    vec.scalar_tensor_tensor(out=h[:, t, :], in0=yg[2 * t + k], scalar=w[:, t:t + 1], in1=h[:, t, :],
                                             op0=ALU.mult, op1=ALU.add)\
                        .then_inc(S("h_half") if k == 0 else S(f"h_moe{l}"), 1)

        def turn_rows(pe, p, rows):
            for k in range(KC):
                ins = pe.transpose(bank(k // 4, 4, P)[:, k % 4, 0:rows], xg[p][0:rows, k::KC], ident[0:rows, 0:rows])
            return ins

        def xgT_out(vec, l, p, rows):
            for b in range(2):
                ins = vec.tensor_tensor(xgT[p][:, 4 * b:4 * b + 4, 0:rows], bank(b, 4, P)[:, :, 0:rows],
                                        gainT[:, GAIN[f"ffn{l}"], 4 * b:4 * b + 4].unsqueeze(2)
                                        .to_broadcast([P, 4, rows]), ALU.mult)
            return ins

        def up(pe, p, n, w):
            for k in range(KC):
                for a in range(n):
                    r = slice(BLK * a, BLK * a + BLK)
                    ins = pe.matmul(bank(2, 2, F)[r, :, :], xgT[p][:, k, r], w[a][:, :, k, :],
                                    start=(k == 0), stop=(k == KC - 1))
            return ins

        def sig_out(act, rows):
            return act.activation(sig[0:rows, :], PS[0:rows, 2, 0:F], ACT.Sigmoid)

        def silu_half(vec, rows):
            return vec.tensor_tensor(hid[0:rows, :], PS[0:rows, 2, 0:F], sig[0:rows, :], ALU.mult)

        def hid_out(vec, rows):
            return vec.tensor_tensor(hid[0:rows, :], PS[0:rows, 2, F:2 * F], hid[0:rows, :], ALU.mult)

        def turn_hid(pe, rows):
            for k in range(2):
                ins = pe.transpose(PS[:, 4, P * k:P * k + rows], hid[0:rows, k::2], ident[0:rows, 0:rows])
            return ins

        def hidT_out(act, rows):
            return act.activation(hidT[:, :, 0:rows], bank(4, 4, P)[:, 0:2, 0:rows], ACT.Copy)

        def down(pe, p, n, half):
            for k in range(2):
                for a in range(n):
                    r = slice(BLK * a, BLK * a + BLK)
                    ins = pe.matmul(PS[r, 6 + half, :], hidT[:, k, r],
                                    w2e[p][a][:, k, 512 * half:512 * half + 512], start=(k == 0), stop=(k == 1))
            return ins

        def ye_half(p, rows, half):
            return ye[p][0:rows, 512 * half:512 * half + 512], PS[0:rows, 6 + half, :]

        def last_peeled(eng, body):
            for j in range(2):
                for p in range(2):
                    body(j, p, False)
            with eng.Fori(2, NPE // 2 - 1) as j:
                for p in range(2):
                    body(j, p, False)
            body(NPE // 2 - 1, 0, False)
            body(NPE // 2 - 1, 1, True)

        def moe_pe(pe, l):
            def turn(j, p):
                pe.wait_ge(S(f"xg_in{p}"), 16 * (NPE // 2 * l + j + 1))
                gate(pe)
                turn_rows(pe, p, P).then_inc(S(f"xg_free{p}"), 1)

            def body(j, p, last):
                n = NPE * l + 2 * j + p
                pe.wait_ge(S("xgT_ready"), n + 1)
                w = w13[p]
                if p == 1:
                    pe.wait_ge(S("w13_in1"), 64 * (NPE // 2 * l + j + 1))
                elif isinstance(j, int) and j == 1:
                    w = w13x
                    pe.wait_ge(S("w13x_in"), 64 * (l + 1))
                elif isinstance(j, int) and j == 0:
                    pe.wait_ge(S("w13_in0"), 64 * ((NPE // 2 - 1) * l + 1))
                else:
                    pe.wait_ge(S("w13_in0"), 64 * ((NPE // 2 - 1) * l + j))
                gate(pe)
                up(pe, p, 2, w).then_inc(S("up_done"), 1)
                if not last:
                    turn(j + p, 1 - p)
                pe.wait_ge(S("hid_ready"), n + 1)
                gate(pe)
                turn_hid(pe, P).then_inc(S("hid_turned"), 1)
                pe.wait_ge(S(f"w2_in{p}"), 32 * (NPE // 2 * l + j + 1))
                pe.wait_ge(S("hidT_ready"), n + 1)
                pe.wait_ge(S("ye_a"), n + l + 1)
                gate(pe)
                down(pe, p, 2, 0).then_inc(S("down_half"), 1)
                pe.wait_ge(S("ye_v"), n + l + 1)
                gate(pe)
                down(pe, p, 2, 1).then_inc(S("down_done"), 1)

            pe.wait_ge(S("table_ready"), l + 1)
            for p in range(2):
                pe.nop().then_inc(S(f"xg_free{p}"), 1)
            turn(0, 0)
            last_peeled(pe, body)

        def moe_act(act, l):
            def body(j, p, last):
                n = NPE * l + 2 * j + p
                act.wait_ge(S("up_done"), n + 1)
                sig_out(act, P).then_inc(S("sig_ready"), 1)
                act.wait_ge(S("hid_turned"), n + 1)
                hidT_out(act, P).then_inc(S("hidT_ready"), 1)
                act.wait_ge(S("down_half"), n + 1)
                act.wait_ge(S(f"ye_out{p}"), 16 * (NPE // 2 * l + l + j + 1))
                d, s = ye_half(p, P, 0)
                act.activation(d, s, ACT.Copy).then_inc(S("ye_a"), 1)
                act.wait_ge(S("ye_v"), n + l + 2)
                act.wait_ge(S("ye_a"), n + l + 2)
                act.dma_start(scratch["blocks"][0:NE * BLK, :].rearrange("(b r) c -> b r c", r=P)[2 * j + p], ye[p])\
                    .then_inc(S(f"ye_out{p}"), 16)

            act.wait_ge(S("table_ready"), l + 1)
            act.nop().then_inc(S("ye_a"), 1)
            for p in range(2):
                act.nop().then_inc(S(f"ye_out{p}"), 16)
            last_peeled(act, body)

        def moe_vec(vec, l):
            def turned(j, p):
                vec.wait_ge(S(f"xg_free{p}"), (NPE // 2 + 1) * l + j + 2)
                xgT_out(vec, l, p, P).then_inc(S("xgT_ready"), 1)

            def body(j, p, last):
                n = NPE * l + 2 * j + p
                vec.wait_ge(S("sig_ready"), n + 1)
                silu_half(vec, P).then_inc(S("silu_ready"), 1)
                vec.wait_ge(S("silu_ready"), n + 1)
                hid_out(vec, P).then_inc(S("hid_ready"), 1)
                if not last:
                    turned(j + p, 1 - p)
                vec.wait_ge(S("down_done"), n + 1)
                vec.wait_ge(S(f"ye_out{p}"), 16 * (NPE // 2 * l + l + j + 1))
                d, s = ye_half(p, P, 1)
                vec.tensor_copy(d, s).then_inc(S("ye_v"), 1)

            vec.nop().then_inc(S("ye_v"), 1)
            turned(0, 0)
            last_peeled(vec, body)

        def further(eng, l, body):
            eng.wait_ge(S("over_known"), l + 1)
            n = eng.value_load(over[0:1, 16:17], min_val=0, max_val=NOVER)
            with eng.If(n > 0):
                with eng.Fori(0, NOVER) as j:
                    with eng.If(j < n):
                        body(j, lambda k: eng.wait_ge(S(f"over_step{l}"), j * NSTEP + k))

        def further_pool(pool, l):
            st = S(f"over_step{l}")

            def body(j, at_step):
                at_step(1)
                pool.tensor_copy(xi[0][:, :], table[:, bass.ds(NPE + j, 1)]).then_inc(st, 1)
                at_step(2)
                gate(pool)
                gather(pool, 0, BLK).then_inc(S(f"over_gathered{l}"), 16)
            further(pool, l, body)

        def further_sp(sp, l):
            st = S(f"over_step{l}")
            for p in range(2):
                sp.wait_ge(S(f"ye_out{p}"), 16 * (NPE // 2 + 1) * (l + 1))
            sp.nop().then_inc(st, 1)

            def body(j, at_step):
                e = sp.value_load(over[0:1, bass.ds(j, 1)], min_val=0, max_val=NE - 1)
                at_step(2)
                load_up(sp, l, e, w13[0][0], st)
                load_down(sp, l, e, w2e[0][0], st)
                at_step(61)
                sp.dma_start(scratch["blocks"].rearrange("(b r) c -> b r c", r=BLK)[NE + j], ye[0][0:BLK, :])\
                    .then_inc(st, 16)
                at_step(77)
                gate(sp)
            further(sp, l, body)
            sp.nop().then_inc(S("over_done"), 1)

        def further_pe(pe, l):
            st = S(f"over_step{l}")

            def step(at_step, k):
                at_step(k)
                gate(pe)

            def body(j, at_step):
                pe.wait_ge(S(f"over_gathered{l}"), 16 * (j + 1))
                step(at_step, 50)
                turn_rows(pe, 0, BLK).then_inc(st, 1)
                step(at_step, 52)
                up(pe, 0, 1, w13[0]).then_inc(st, 1)
                step(at_step, 56)
                turn_hid(pe, BLK).then_inc(st, 1)
                step(at_step, 58)
                down(pe, 0, 1, 0)
                down(pe, 0, 1, 1).then_inc(st, 1)
            further(pe, l, body)

        def further_act(act, l):
            st = S(f"over_step{l}")

            def body(j, at_step):
                at_step(53)
                sig_out(act, BLK).then_inc(st, 1)
                at_step(57)
                hidT_out(act, BLK).then_inc(st, 1)
                at_step(59)
                d, s = ye_half(0, BLK, 0)
                act.activation(d, s, ACT.Copy).then_inc(st, 1)
            further(act, l, body)

        def further_vec(vec, l):
            st = S(f"over_step{l}")

            def body(j, at_step):
                at_step(51)
                xgT_out(vec, l, 0, BLK).then_inc(st, 1)
                at_step(54)
                silu_half(vec, BLK).then_inc(st, 1)
                at_step(55)
                hid_out(vec, BLK).then_inc(st, 1)
                at_step(60)
                d, s = ye_half(0, BLK, 1)
                vec.tensor_copy(d, s).then_inc(st, 1)
            further(vec, l, body)

        tnF = at(0, [NT, C])
        gF = at(4, [C])

        def final_act(act):
            norm_act(act, "final", h, tnF, lambda e, t: e.wait_ge(S("h_moe1"), t + 1))

        def final_vec(vec):
            norm_vec(vec, "final", h, tnF)
            vec.wait_ge(S("final_gain_in"), 16)
            for t in range(NT):
                vec.wait_ge(S("norm_rows"), TILE0["final"] + t + 1)
                vec.tensor_tensor(tnF[:, t, :], tnF[:, t, :], gF, ALU.mult).then_inc(S("result"), 1)

        def final_sp(sp):
            sp.wait_ge(S("over_done"), 2)
            sp.dma_start(gF, bcast(A["norm_final"])).then_inc(S("final_gain_in"), 16)
            for t in range(NT):
                sp.wait_ge(S("result"), t + 1)
                sp.dma_start(out[0, P * t:P * t + P, :], tnF[:, t, :]).then_inc(S("result_out"), 16)
            sp.wait_ge(S("result_out"), 16 * NT)

        block = ctx.enter_context(nc.Block())

        def at_unit(name):
            return UNITS.index(name)

        @block.sync
        def _(sp):
            loads_first(sp)
            load_units(sp, 0, 6)
            spare = scratch["blocks"][NE * BLK:NBLK * BLK, :]
            sp.dma_start(spare[0:T, :], A["x"][0]).then_inc(S("spare_filled"), 16)
            sp.dma_start(spare[T:NOVER * BLK, :], A["x"][0, 0:NOVER * BLK - T, :]).then_inc(S("spare_filled"), 16)
            loads_after_pairs(sp)
            load_units(sp, 6, at_unit("xo0"))
            moe_first_loads(sp, 0)
            load_units(sp, at_unit("xo0"), at_unit("sqkv"))
            moe_route_loads(sp, 0)
            moe_rows_out(sp, 0)
            moe_loads(sp, 0)
            further_sp(sp, 0)
            for t in range(NT):
                sp.wait_ge(S(f"yg_in{t}"), 32)
            load_units(sp, at_unit("sqkv"), at_unit("xo1"))
            moe_first_loads(sp, 1)
            load_units(sp, at_unit("xo1"), len(UNITS))
            moe_route_loads(sp, 1)
            moe_rows_out(sp, 1)
            moe_loads(sp, 1)
            further_sp(sp, 1)
            final_sp(sp)

        @block.gpsimd
        def _(pool):
            constants(pool)
            pair_pool(pool)
            moe_constants(pool)
            for l in range(2):
                if l == 1:
                    sb_pool(pool)
                moe_pool(pool, l)
                further_pool(pool, l)
                moe_combine_pool(pool, l)

        @block.scalar
        def _(act):
            norm_act(act, "mix0", h, tn0, lambda e, t: e.wait_ge(S(f"x_in{t}"), 16))
            act.wait_ge(S("small_in"), SMALL)
            xT_evac(act, "mix0", xT, 0)
            rwkv_proj_act(act)
            pair_act(act)
            gn_act(act)
            mem_act(act)
            for l in range(2):
                if l == 1:
                    sb_proj_act(act)
                    sb_act(act)
                cross_act(act, l, "so" if l else "rwo")
                moe_route_act(act, l)
                moe_act(act, l)
                further_act(act, l)
            final_act(act)

        @block.tensor
        def _(pe):
            pe.wait_ge(S("const_ready"), 1)
            norm_pe(pe, "mix0", tn0)
            rwkv_proj_pe(pe)
            pair_pe(pe)
            gn_pe(pe)
            mem_pe(pe)
            post_pe(pe)
            for l in range(2):
                if l == 1:
                    sb_proj_pe(pe)
                    sb_pe(pe)
                cross_pe(pe, l)
                moe_route_pe(pe, l)
                moe_pe(pe, l)
                further_pe(pe, l)

        @block.vector
        def _(vec):
            for t in range(NT):
                vec.wait_ge(S(f"x_in{t}"), 16)
            norm_vec(vec, "mix0", h, tn0)
            vec.wait_ge(S("small_in"), SMALL)
            xT_evac(vec, "mix0", xT, 1)
            prm_vec(vec)
            rwkv_mix_vec(vec)
            rwkv_pre_vec(vec)
            pair_vec(vec)
            gn_vec(vec)
            mem_vec(vec)
            post_vec(vec)
            add_to_h(vec, FIRST["rwo"], x_back)
            for l in range(2):
                if l == 1:
                    norm_vec(vec, "mix1", h, tnS)
                    xT_evac(vec, "mix1", xTS, 1)
                    sb_vec(vec)
                    add_to_h(vec, FIRST["so"])
                cross_vec(vec, l)
                moe_route_vec(vec, l)
                moe_vec(vec, l)
                further_vec(vec, l)
                moe_combine_vec(vec, l)
            final_vec(vec)

_INS = ["x", "mem", "norm_mix", "norm_cross", "norm_ffn", "norm_mem", "norm_final",
        "rw_mix", "rw_wr", "rw_wk", "rw_wv", "rw_w0", "rw_w1", "rw_w2", "rw_a0", "rw_a1", "rw_a2",
        "rw_g1", "rw_g2", "rw_kk", "rw_ka", "rw_rk", "rw_lnx_w", "rw_lnx_b", "rw_wo",
        "sb_wqkv", "sb_wo", "xa_wq", "xa_wkv", "xa_wo",
        "moe_wg", "moe_bg", "moe_we", "moe_be", "moe_w1", "moe_w3", "moe_w2"]


def kernel(**inputs):
    import numpy as _np
    import concourse.bacc as _bacc
    from concourse.bass_utils import run_bass_kernel_spmd as _run

    nc = _bacc.Bacc("TRN2", target_bir_lowering=False, num_devices=1)
    arrays, aps = {}, {}
    for name in _INS:
        a = _np.ascontiguousarray(inputs[name])
        arrays[f"in_{name}"] = a
        aps[name] = nc.dram_tensor(f"in_{name}", a.shape, mybir.dt.from_np(a.dtype), kind="ExternalInput").ap()
    out = nc.dram_tensor("out_0", (1, T, C), F32, kind="ExternalOutput").ap()
    scratch = {
        "rows": nc.dram_tensor("normed_rows", (T, C), F32, kind="Internal").ap(),
        "blocks": nc.dram_tensor("expert_rows", (NBLK * BLK, C), F32, kind="Internal").ap(),
    }
    trunk(nc, aps, out, scratch)
    r = _run(nc, [arrays], core_ids=[0])
    return r.results[0]["out_0"]
```
